# Optimizing a Trainium2 kernel written in Bass

```python
import math
import jax, jax.numpy as jnp
from jax import lax
import numpy as np

D_MODEL = 1024
BATCH = 1
SEQ = 128
DEPTH = 2
DEC_BATCH = 1
DEC_SEQ = 256
PAST_LEN = 128

GRID_W = 64
EPS = 1e-6
NEG_BIG = -1e30
ATTN_QBLK = 128
A_HEADS = 4
A_DIM = 32
ROPE_BASE = 10000.0
B_HEADS = 4
B_DK = 64
B_DV = 64
B_CHUNK = 32
C_HEADS = 4
C_DIM = 64
NA_WIN_H = 8
NA_WIN_W = 16
NA_QW = 16
NA_KW = NA_QW + NA_WIN_W
D_GROUPS = 4
D_GROUP_DIM = 64
A_W = A_HEADS * 2 * A_DIM
B_KW = B_HEADS * B_DK
B_VW = B_HEADS * B_DV
C_W = C_HEADS * C_DIM
D_W = D_GROUPS * D_GROUP_DIM
MIX_W = A_W + B_VW + C_W + D_W
PROJ_SPLITS = (A_W, A_W, A_W, B_KW, B_KW, B_KW, B_VW, B_VW, C_W, C_W, C_W, D_W)
PROJ_W = 3 * A_W + 3 * B_KW + 2 * B_VW + 3 * C_W + D_W
N_EXPERTS = 16
N_GROUPS = 4
TOP_K = 2
D_EXPERT = 512

kernel_name = "hybrid_dit_prefix_step"

def rmsnorm(x, g):
    xf = x.astype(jnp.float32)
    y = xf * lax.rsqrt(jnp.mean(xf * xf, axis=-1, keepdims=True) + EPS)
    return (y * g.astype(jnp.float32)).astype(x.dtype)

def split_heads(t, n, d):
    b, l, _ = t.shape
    return t.reshape(b, l, n, d).transpose(0, 2, 1, 3)

def merge_heads(t):
    b, h, l, d = t.shape
    return t.transpose(0, 2, 1, 3).reshape(b, l, h * d)

def axial_rope(t):
    l = t.shape[2]
    nf = A_DIM // 4
    freqs = ROPE_BASE ** (-jnp.arange(nf, dtype=jnp.float32) / nf)
    pos = jnp.arange(l)
    row = (pos // GRID_W).astype(jnp.float32)
    col = (pos % GRID_W).astype(jnp.float32)
    ang = jnp.concatenate([row[:, None] * freqs, col[:, None] * freqs], axis=-1)
    cos = jnp.cos(ang).astype(t.dtype)
    sin = jnp.sin(ang).astype(t.dtype)
    tp = t.reshape(t.shape[:-1] + (A_DIM // 2, 2))
    t0, t1 = tp[..., 0], tp[..., 1]
    out = jnp.stack([t0 * cos - t1 * sin, t0 * sin + t1 * cos], axis=-1)
    return out.reshape(t.shape)

def to_query_blocks(q):
    b, h, l, d = q.shape
    qb = min(ATTN_QBLK, l)
    return q.reshape(b, h, l // qb, qb, d).transpose(2, 0, 1, 3, 4)

def from_query_blocks(o):
    nb, b, h, qb, d = o.shape
    return o.transpose(1, 2, 0, 3, 4).reshape(b, h, nb * qb, d)

def diff_attention(q1, q2, k1, k2, v, lam):
    scale = A_DIM ** -0.5

    def one(qs):
        qa, qb = qs
        p1 = jax.nn.softmax(jnp.einsum("bhqd,bhkd->bhqk", qa, k1).astype(jnp.float32) * scale, axis=-1)
        p2 = jax.nn.softmax(jnp.einsum("bhqd,bhkd->bhqk", qb, k2).astype(jnp.float32) * scale, axis=-1)
        w = (p1 - lam * p2).astype(v.dtype)
        return jnp.einsum("bhqk,bhkv->bhqv", w, v)

    return from_query_blocks(lax.map(one, (to_query_blocks(q1), to_query_blocks(q2))))

def softmax_attention(q, k, v):
    scale = q.shape[-1] ** -0.5

    def one(qb):
        p = jax.nn.softmax(jnp.einsum("bhqd,bhkd->bhqk", qb, k).astype(jnp.float32) * scale, axis=-1)
        return jnp.einsum("bhqk,bhkv->bhqv", p.astype(v.dtype), v)

    return from_query_blocks(lax.map(one, to_query_blocks(q)))

def hgrn2_chunked(q, k, v, logf, s0):
    bsz, h, l, dk = q.shape
    dv = v.shape[-1]
    n = l // B_CHUNK
    r = lambda t: t.astype(jnp.float32).reshape(bsz, h, n, B_CHUNK, t.shape[-1])
    q, k, v, lf = r(q), r(k), r(v), r(logf)
    b = jnp.cumsum(lf, axis=3)
    b_last = b[:, :, :, -1:, :]
    causal = jnp.tril(jnp.ones((B_CHUNK, B_CHUNK), dtype=bool))[:, :, None]
    diff = b[:, :, :, :, None, :] - b[:, :, :, None, :, :]
    decay = jnp.where(causal, jnp.exp(jnp.where(causal, diff, 0.0)), 0.0)
    attn = jnp.einsum("bhntk,bhntsk,bhnsk->bhnts", q, decay, k)
    o_intra = jnp.einsum("bhnts,bhnsv->bhntv", attn, v)
    q_dec = q * jnp.exp(b)
    k_dec = k * jnp.exp(b_last - b)
    kv = jnp.einsum("bhnsk,bhnsv->nbhkv", k_dec, v)
    g = jnp.exp(b_last[:, :, :, 0, :]).transpose(2, 0, 1, 3)

    def step(s, xs):
        kv_n, g_n = xs
        return g_n[..., None] * s + kv_n, s

    s_final, s_prev = lax.scan(step, s0.astype(jnp.float32), (kv, g))
    o_inter = jnp.einsum("bhntk,nbhkv->bhntv", q_dec, s_prev)
    return (o_intra + o_inter).reshape(bsz, h, l, dv), s_final

def hgrn2_mixer(bq, bff, bfb, bv, bg, lb_f, lb_b, norm_g, s0_f, s0_b):
    bsz, l, _ = bq.shape
    q = split_heads(jax.nn.silu(bq.astype(jnp.float32)), B_HEADS, B_DK)
    v = split_heads(bv.astype(jnp.float32), B_HEADS, B_DV)

    def forget(z, lb):
        z = split_heads(z.astype(jnp.float32), B_HEADS, B_DK)
        lb = lb.astype(jnp.float32).reshape(B_HEADS, 1, B_DK)
        f = lb + (1.0 - lb) * jax.nn.sigmoid(z)
        i = (1.0 - lb) * jax.nn.sigmoid(-z)
        return jnp.log(f), i

    logf_f, k_f = forget(bff, lb_f)
    logf_b, k_b = forget(bfb, lb_b)
    o_f, s_f = hgrn2_chunked(q, k_f, v, logf_f, s0_f)
    flip = lambda t: jnp.flip(t, axis=2)
    o_b, s_b = hgrn2_chunked(flip(q), flip(k_b), flip(v), flip(logf_b), s0_b)
    o = rmsnorm(o_f + flip(o_b), norm_g)
    o = merge_heads(o) * jax.nn.silu(bg.astype(jnp.float32))
    return o.astype(bq.dtype), s_f, s_b

def na_latent(q, k, v, rpb, ctx_k, ctx_v):
    bsz, h, s, dh = q.shape
    rows = s // GRID_W
    wr = min(NA_WIN_H, rows)
    ncb = GRID_W // NA_QW
    r = np.arange(rows)
    row_idx = np.clip(r - wr // 2, 0, rows - wr)[:, None] + np.arange(wr)[None, :]
    nb = np.arange(ncb)
    col_idx = np.clip(nb * NA_QW - NA_WIN_W // 2, 0, GRID_W - NA_KW)[:, None] + np.arange(NA_KW)[None, :]
    qcol = nb[:, None] * NA_QW + np.arange(NA_QW)[None, :]
    cs = np.clip(qcol - NA_WIN_W // 2, 0, GRID_W - NA_WIN_W)
    valid = (col_idx[:, None, :] >= cs[:, :, None]) & (col_idx[:, None, :] < cs[:, :, None] + NA_WIN_W)
    dc_idx = np.clip(col_idx[:, None, :] - qcol[:, :, None] + NA_WIN_W - 1, 0, 2 * NA_WIN_W - 2)
    dr_idx = row_idx - r[:, None] + NA_WIN_H - 1
    bias = rpb.astype(jnp.float32)[:, dr_idx[:, None, None, :, None], dc_idx[None, :, :, None, :]]
    bias = jnp.where(valid[None, None, :, :, None, :], bias, NEG_BIG).reshape(h, rows, ncb, NA_QW, wr * NA_KW)
    kg = k.reshape(bsz, h, rows, GRID_W, dh)
    vg = v.reshape(bsz, h, rows, GRID_W, dh)
    ri = row_idx[:, None, :, None]
    ci = col_idx[None, :, None, :]
    kb = kg[:, :, ri, ci].reshape(bsz, h, rows, ncb, wr * NA_KW, dh)
    vb = vg[:, :, ri, ci].reshape(bsz, h, rows, ncb, wr * NA_KW, dh)
    qb = q.reshape(bsz, h, rows, ncb, NA_QW, dh)
    scale = dh ** -0.5
    s_loc = jnp.einsum("bhrnqd,bhrnkd->bhrnqk", qb, kb).astype(jnp.float32) * scale + bias
    s_ctx = jnp.einsum("bhrnqd,bhcd->bhrnqc", qb, ctx_k).astype(jnp.float32) * scale
    p = jax.nn.softmax(jnp.concatenate([s_loc, s_ctx], axis=-1), axis=-1).astype(v.dtype)
    nloc = wr * NA_KW
    o = jnp.einsum("bhrnqk,bhrnkd->bhrnqd", p[..., :nloc], vb) + jnp.einsum("bhrnqc,bhcd->bhrnqd", p[..., nloc:], ctx_v)
    return o.reshape(bsz, h, s, dh)

def fourier_mix(u):
    b, l, _ = u.shape
    uf = u.astype(jnp.float32).reshape(b, l, D_GROUPS, D_GROUP_DIM)
    y = jnp.fft.fftn(uf, axes=(1, 3), norm="ortho").real
    return y.reshape(b, l, D_W).astype(u.dtype)

def moe(h, router_w, router_b, w_gate, w_up, w_down):
    t = h.shape[0]
    per = N_EXPERTS // N_GROUPS
    scores = jax.nn.sigmoid((h @ router_w).astype(jnp.float32))
    sel = scores + router_b.astype(jnp.float32)
    group_score = jnp.sum(lax.top_k(sel.reshape(t, N_GROUPS, per), 2)[0], axis=-1)
    best = jnp.argmax(group_score, axis=-1)
    in_group = (jnp.arange(N_EXPERTS) // per)[None, :] == best[:, None]
    _, idx = lax.top_k(jnp.where(in_group, sel, NEG_BIG), TOP_K)
    w = jnp.take_along_axis(scores, idx, axis=-1)
    w = w / jnp.sum(w, axis=-1, keepdims=True)
    gates = jnp.sum(jax.nn.one_hot(idx, N_EXPERTS, dtype=jnp.float32) * w[..., None], axis=1)
    a = jnp.einsum("td,edf->tef", h, w_gate)
    u = jnp.einsum("td,edf->tef", h, w_up)
    z = jax.nn.silu(a) * u * gates[:, :, None].astype(h.dtype)
    return jnp.einsum("tef,efd->td", z, w_down)

def trunk_layer(x, mod, layer_idx, norm1_g, norm2_g, w_in, w_out, lam_qk, subln_g, lb_f, lb_b, hgrn_norm_g, rpb,
                router_w, router_b, w_gate, w_up, w_down, ctx):
    bsz, l, _ = x.shape
    latent = ctx is not None
    shift1, scale1, gate1, shift2, scale2, gate2 = jnp.split(mod, 6, axis=-1)
    h = rmsnorm(x, norm1_g) * (1 + scale1) + shift1
    offsets = [int(o) for o in np.cumsum(PROJ_SPLITS)[:-1]]
    aq, ak, av, bq, bff, bfb, bv, bg, cq, ck, cv, du = jnp.split(h @ w_in, offsets, axis=-1)

    aq = aq.reshape(bsz, l, A_HEADS, 2, A_DIM).transpose(0, 2, 3, 1, 4)
    ak = ak.reshape(bsz, l, A_HEADS, 2, A_DIM).transpose(0, 2, 3, 1, 4)
    q1, q2, k1, k2 = aq[:, :, 0], aq[:, :, 1], ak[:, :, 0], ak[:, :, 1]
    va = split_heads(av, A_HEADS, 2 * A_DIM)
    if latent:
        q1, q2, k1, k2 = axial_rope(q1), axial_rope(q2), axial_rope(k1), axial_rope(k2)
    ka = jnp.concatenate([k1, k2], axis=-1)
    if latent:
        ka_all = jnp.concatenate([ctx[0], ka], axis=2)
        va_all = jnp.concatenate([ctx[1], va], axis=2)
    else:
        ka_all, va_all = ka, va
    lam_init = 0.8 - 0.6 * math.exp(-0.3 * layer_idx)
    lq = lam_qk.astype(jnp.float32)
    lam = jnp.exp(jnp.sum(lq[0] * lq[1])) - jnp.exp(jnp.sum(lq[2] * lq[3])) + lam_init
    o_a = diff_attention(q1, q2, ka_all[..., :A_DIM], ka_all[..., A_DIM:], va_all, lam)
    o_a = merge_heads(rmsnorm(o_a, subln_g) * (1.0 - lam_init))

    if latent:
        s0_f, s0_b = ctx[4][:, 0], ctx[4][:, 1]
    else:
        s0_f = jnp.zeros((bsz, B_HEADS, B_DK, B_DV), jnp.float32)
        s0_b = s0_f
    o_b, s_f, s_b = hgrn2_mixer(bq, bff, bfb, bv, bg, lb_f, lb_b, hgrn_norm_g, s0_f, s0_b)

    qc, kc, vc = split_heads(cq, C_HEADS, C_DIM), split_heads(ck, C_HEADS, C_DIM), split_heads(cv, C_HEADS, C_DIM)
    if latent:
        o_c = na_latent(qc, kc, vc, rpb, ctx[2], ctx[3])
    else:
        o_c = softmax_attention(qc, kc, vc)

    o_d = fourier_mix(du)

    mixed = jnp.concatenate([o_a, o_b, merge_heads(o_c), o_d], axis=-1) @ w_out
    x = x + gate1 * mixed
    h2 = rmsnorm(x, norm2_g) * (1 + scale2) + shift2
    x = x + gate2 * moe(h2.reshape(bsz * l, -1), router_w, router_b, w_gate, w_up, w_down).reshape(bsz, l, -1)
    if latent:
        return x
    return x, (ka, va, kc, vc, jnp.stack([s_f, s_b], axis=1).astype(x.dtype))

def setup_inputs(seed: int = 0) -> dict:
    key = jax.random.key(seed)
    ks = jax.random.split(key, 26)
    f32 = jnp.float32
    nrm = lambda k, shape, s: jax.random.normal(k, shape, f32) * s
    return {
        "x_prompt": nrm(ks[0], (BATCH, SEQ, D_MODEL), 1.0),
        "x_sample": nrm(ks[1], (DEC_BATCH, DEC_SEQ, D_MODEL), 1.0),
        "cache_diff_k": nrm(ks[2], (DEC_BATCH, DEPTH, A_HEADS, PAST_LEN, 2 * A_DIM), 1.0),
        "cache_diff_v": nrm(ks[3], (DEC_BATCH, DEPTH, A_HEADS, PAST_LEN, 2 * A_DIM), 1.0),
        "cache_na_k": nrm(ks[4], (DEC_BATCH, DEPTH, C_HEADS, PAST_LEN, C_DIM), 1.0),
        "cache_na_v": nrm(ks[5], (DEC_BATCH, DEPTH, C_HEADS, PAST_LEN, C_DIM), 1.0),
        "state_hgrn": nrm(ks[6], (DEC_BATCH, DEPTH, 2, B_HEADS, B_DK, B_DV), 0.5),
        "c": nrm(ks[7], (DEC_BATCH, D_MODEL), 1.0),
        "c_ctx": nrm(ks[8], (D_MODEL,), 1.0),
        "norm1_g": 1.0 + nrm(ks[9], (DEPTH, D_MODEL), 0.05),
        "norm2_g": 1.0 + nrm(ks[10], (DEPTH, D_MODEL), 0.05),
        "ada_w": nrm(ks[11], (DEPTH, D_MODEL, 6 * D_MODEL), 0.5 * D_MODEL ** -0.5),
        "ada_b": nrm(ks[12], (DEPTH, 6 * D_MODEL), 0.02),
        "w_in": nrm(ks[13], (DEPTH, D_MODEL, PROJ_W), D_MODEL ** -0.5),
        "w_out": nrm(ks[14], (DEPTH, MIX_W, D_MODEL), MIX_W ** -0.5),
        "diff_lambda": nrm(ks[15], (DEPTH, 4, A_DIM), 0.1),
        "diff_subln_g": 1.0 + nrm(ks[16], (DEPTH, 2 * A_DIM), 0.05),
        "hgrn_lb_logits": nrm(ks[17], (DEPTH, 2, B_KW), 0.5),
        "hgrn_norm_g": 1.0 + nrm(ks[18], (DEPTH, B_DV), 0.05),
        "na_rpb": nrm(ks[19], (DEPTH, C_HEADS, 2 * NA_WIN_H - 1, 2 * NA_WIN_W - 1), 0.5),
        "router_w": nrm(ks[20], (D_MODEL, N_EXPERTS), D_MODEL ** -0.5),
        "router_b": nrm(ks[21], (N_EXPERTS,), 0.01),
        "moe_w_gate": nrm(ks[22], (DEPTH, N_EXPERTS, D_MODEL, D_EXPERT), D_MODEL ** -0.5),
        "moe_w_up": nrm(ks[23], (DEPTH, N_EXPERTS, D_MODEL, D_EXPERT), D_MODEL ** -0.5),
        "moe_w_down": nrm(ks[24], (DEPTH, N_EXPERTS, D_EXPERT, D_MODEL), D_EXPERT ** -0.5),
        "final_norm_g": 1.0 + nrm(ks[25], (D_MODEL,), 0.05),
    }

def reference(x_prompt, x_sample, cache_diff_k, cache_diff_v, cache_na_k, cache_na_v, state_hgrn, c, c_ctx,
              norm1_g, norm2_g, ada_w, ada_b, w_in, w_out, diff_lambda, diff_subln_g, hgrn_lb_logits, hgrn_norm_g,
              na_rpb, router_w, router_b, moe_w_gate, moe_w_up, moe_w_down, final_norm_g):
    lb_sm = jax.nn.softmax(hgrn_lb_logits.astype(jnp.float32), axis=0)
    lb_all = jnp.cumsum(lb_sm, axis=0) - lb_sm[0:1]
    xp, xs = x_prompt, x_sample
    dk_l, dv_l, nk_l, nv_l, hs_l = [], [], [], [], []
    for l in range(DEPTH):
        mod_ctx = (jax.nn.silu(c_ctx) @ ada_w[l] + ada_b[l])[None, None, :]
        mod_lat = (jax.nn.silu(c) @ ada_w[l] + ada_b[l])[:, None, :]
        shared = (norm1_g[l], norm2_g[l], w_in[l], w_out[l], diff_lambda[l], diff_subln_g[l], lb_all[l, 0],
                  lb_all[l, 1], hgrn_norm_g[l], na_rpb[l], router_w, router_b, moe_w_gate[l], moe_w_up[l],
                  moe_w_down[l])
        xp, (dk, dv, nk, nv, hs) = trunk_layer(xp, mod_ctx, l, *shared, None)
        dk_l.append(dk)
        dv_l.append(dv)
        nk_l.append(nk)
        nv_l.append(nv)
        hs_l.append(hs)
        xs = trunk_layer(xs, mod_lat, l, *shared,
                         (cache_diff_k[:, l], cache_diff_v[:, l], cache_na_k[:, l], cache_na_v[:, l], state_hgrn[:, l]))
    y_prompt = rmsnorm(xp, final_norm_g)
    y_sample = rmsnorm(xs, final_norm_g)
    new_diff_k = jnp.stack(dk_l, axis=1)
    new_diff_v = jnp.stack(dv_l, axis=1)
    new_na_k = jnp.stack(nk_l, axis=1)
    new_na_v = jnp.stack(nv_l, axis=1)
    new_state_hgrn = jnp.stack(hs_l, axis=1)
    return (y_prompt, y_sample, new_diff_k, new_diff_v, new_na_k, new_na_v, new_state_hgrn)


_drawn_inputs = setup_inputs


def setup_inputs(seed=0):
    import zlib

    import numpy as np

    out = dict(_drawn_inputs(seed))
    spreads = {}
    factors = {'state_hgrn': 8.0, 'hgrn_norm_g': 4.049}
    for name, (base, spread) in spreads.items():
        noise = np.random.default_rng([zlib.crc32(name.encode()), seed]).standard_normal(out[name].shape)
        drawn = base * np.exp(spread * noise) if base else spread * noise
        out[name] = __import__('jax').numpy.asarray(drawn.astype(out[name].dtype))
    for name, factor in factors.items():
        out[name] = (out[name] * factor).astype(out[name].dtype)
    return out
```

```python
import math
from contextlib import ExitStack

import numpy as np

import concourse.bass as bass
from concourse import mybir

F32 = mybir.dt.float32
ALU = mybir.AluOpType
ACT = mybir.ActivationFunctionType
AX = mybir.AxisListType.X

P = 128
D = 1024
KC = D // P
L = 2
NT = 3
T = NT * P
H = 4
HP = 2
GRID_W = 64
EPS = 1e-6
NE = 16
FE = 512
FC = FE // P
BANKS = 8
SLOTS = 4
BLK = 4096
LEVELS = [64, 32, 16, 8, 4, 2, 1]
NLEV = len(LEVELS)
GRAM = 2 * NLEV + 1
DCOLS = 2 * NLEV * P + 4 * P + 2
TINY = 2.0 ** -60
RPB_H, RPB_W = 15, 31
RPER = 2 * GRID_W - 1
ADA_COL = [0, 1, 2, 3]
ADA_GATE1 = [4, 5]
ADA_COL2 = [6, 7, 8, 9]
ADA_GATE2 = [10, 11]
WIN_ORDER = [1, 2, 3, 0, 4, 5]
EXP_PER_BODY = 4
NBODY = NE // EXP_PER_BODY
PRE = ([("ada", j) for j in ADA_COL + ADA_GATE1 + ADA_COL2] + [("win", j) for j in WIN_ORDER]
       + [("wout", j) for j in range(2)] + [("ada", j) for j in ADA_GATE2])
PER_LAYER = len(PRE) + 3 * NE
assert len(PRE) % SLOTS == 0 and PER_LAYER % SLOTS == 0 and 3 * EXP_PER_BODY % SLOTS == 0
UNITS = [(t, hp) for t in range(NT) for hp in range(HP)]
ATT = ([("A", 0, h) for h in range(H)] + [("C", 0, h) for h in range(H)]
       + [(m, t, h) for t in (1, 2) for m in "AC" for h in range(H)])
AQ, AK, AV, BV, BG, CV, DU = 0, 256, 512, 768, 1024, 1280, 1536
PTOK = 1792


def layer_jobs(l):
    jobs = [("mod", l, j) for j in ADA_COL] + [("grow", l, j) for j in ADA_GATE1] + [("mod", l, j) for j in ADA_COL2]
    jobs += [("gbc", l, j, s) for j in ADA_GATE1 for s in range(2)]
    jobs += [("hT", 2 * l, k) for k in range(KC)]
    jobs += [("bq", l, 0), ("bq", l, 1)] + [("av", l, t) for t in range(NT)]
    jobs += [("z", l, d, hp) for d in range(2) for hp in range(HP)]
    jobs += [("bvg", l, t) for t in range(NT)] + [("aqk", l, t) for t in range(NT)]
    jobs += [("cq", l, hp) for hp in range(HP)] + [("ck", l, hp) for hp in range(HP)]
    jobs += [("cvdu", l, t) for t in range(NT)]
    jobs += [("du", l, c, w) for c in range(2) for w in range(2)] + [("dy", l, c) for c in range(2)]
    jobs += [("cc", l), ("nk", l)]
    for u in range(len(UNITS)):
        jobs += [("kd", l, u)] + [("gram", l, u, 0, g) for g in range(4)] + [("kv", l, u)]
        jobs += [("gram", l, u, 1, g) for g in range(4)]
    jobs += [("bo", l, t, h2) for t in range(NT) for h2 in range(2)]
    jobs += [("aT", l, w, hp) for w in range(2) for hp in range(HP)]
    for i in range(len(ATT) + 2):
        if i < len(ATT):
            jobs += [("sc", l, i, m) for m in range(2 if ATT[i][0] == "A" else 1)]
        if 0 <= i - 1 < len(ATT):
            jobs += [("pT", l, i - 1)]
        if i >= 2:
            jobs += [("ao", l, i - 2)]
    jobs += [("mT", l, c) for c in range(6)]
    jobs += [("wo", l, b, t) for b in range(2) for t in range(NT)]
    jobs += [("grow", l, j) for j in ADA_GATE2] + [("gbc", l, j, s) for j in ADA_GATE2 for s in range(2)]
    jobs += [("hT", 2 * l + 1, k) for k in range(KC)] + [("rt", l)]
    return jobs


def expert_jobs(l):
    return [job for e in range(EXP_PER_BODY)
            for job in [("a", l, e, 0), ("u", l, e, 0)] + [(w, l, e, f) for f in range(1, FC) for w in "au"]
            + [("dn", l, e, b, t) for b in range(2) for t in range(NT)]]


def place_jobs():
    place, n, uses = {}, 0, [0] * BANKS
    per_body = 0
    for l in range(L):
        for job in layer_jobs(l):
            b = n % BANKS
            uses[b] += 1
            place[job] = (b, uses[b])
            n += 1
        body = expert_jobs(l)
        assert len(body) % BANKS == 0
        per_body = len(body) // BANKS
        for i, job in enumerate(body):
            b = (n + i) % BANKS
            place[job] = (b, uses[b] + 1 + i // BANKS)
        uses = [x + per_body * NBODY for x in uses]
        n += len(body) * NBODY
    return place, per_body


def hybrid_step(nc, x_prompt, x_sample, cache_diff_k, cache_diff_v, cache_na_k, cache_na_v, state_hgrn, ada_w, ada_b,
                w_in, w_out, diff_lambda, diff_subln_g, hgrn_norm_g, router_w, router_b, moe_w_gate, moe_w_up,
                moe_w_down, final_norm_g, params, rpb_pad, consts, masks, outs):
    y_prompt, y_sample, new_diff_k, new_diff_v, new_na_k, new_na_v, new_state = outs
    place, PER_BODY = place_jobs()

    with ExitStack() as ctx:
        def sb(name, shape, dt=F32):
            return ctx.enter_context(nc.sbuf_tensor(name, shape, dt))

        def sem(name):
            return ctx.enter_context(nc.semaphore(name))

        ring = sb("ring", [P, SLOTS, BLK])
        x = sb("x", [P, NT, D])
        hT = sb("hT", [P, KC, T])
        gate = sb("gate", [P, 2, D])
        big = sb("big", [P, 7168])
        dbuf = sb("dbuf", [P, 2 * DCOLS])
        bbuf = sb("bbuf", [P, 3852])
        mprod = sb("mprod", [P, 8, P])
        attT = sb("attT", [P, len(UNITS) * 2, P])
        qdec = sb("qdec", [P, 2, HP, 2, P])
        kdT = sb("kdT", [P, 2, 2, P])
        bias = sb("bias", [P, H, 2, 4, GRID_W])
        cachek = sb("cachek", [P, 4, H, 64])
        S0 = sb("S0", [P, HP, 2, 64])
        S1 = sb("S1", [P, HP, 2, 64])
        mk = sb("mk", [P, GRAM, P], mybir.dt.bfloat16)
        const = sb("const", [P, consts.shape[1]])
        par = sb("par", [P, params.shape[1]])
        wrt = sb("wrt", [P, KC, NE])
        rbias = sb("rbias", [P, NE])
        gsub = sb("gsub", [P, 2, L, 64])
        modT = sb("modT", [P, 4, KC, 2])
        rtmp = sb("rtmp", [P, 512])
        small = sb("small", [P, 860])
        ps = ctx.enter_context(nc.psum_tensor("ps", [P, BANKS, 512], F32))

        def carve(buf, at, *shape):
            names = "abcde"[:len(shape)]
            v = buf[:, at:at + int(np.prod(shape))]
            if len(shape) == 1:
                return v
            return v.rearrange(f"p ({' '.join(names)}) -> p {' '.join(names)}", **dict(zip(names, shape)))

        def strided(v, offset, *dims):
            return bass.AP(v.tensor, v.offset + offset, [list(v.ap[0])] + [list(d) for d in dims])

        tok = carve(big, 0, NT, PTOK)
        cqT = carve(big, NT * PTOK, HP, T)
        ckT = carve(big, NT * PTOK + HP * T, HP, 4 * P)
        xn = carve(big, 0, NT, D)
        ysum = carve(big, NT * D, NT, D)
        junk = carve(big, NT * D, D)
        gbias = carve(big, 2 * NT * D, D)
        qT = carve(bbuf, 0, HP, T)
        kT = carve(bbuf, HP * T, 2, HP, T)
        C2 = carve(bbuf, 3 * HP * T, HP, NT, 258)
        aqT = carve(bbuf, 0, HP, T)
        akT = carve(bbuf, HP * T, HP, 4 * P)
        oA = carve(bbuf, HP * T + HP * 4 * P, NT * H, 64)
        oC = carve(bbuf, HP * T + HP * 4 * P + NT * H * 64, NT * H, 64)
        Z = carve(dbuf, 0, 2, HP, T)
        E = carve(dbuf, 2 * HP * T, 2, HP, T)
        F = carve(dbuf, 4 * HP * T, 2, HP, T)
        dec = [dbuf[:, u * DCOLS:(u + 1) * DCOLS] for u in range(2)]
        prob = carve(dbuf, 0, 2, 2, T)
        wmix = carve(dbuf, 4 * T, 2, T)
        scb = carve(dbuf, 6 * T, 2, T)
        wT = carve(dbuf, 8 * T, 2, T)
        oB = carve(dbuf, 10 * T, NT * H, 64)
        post = carve(dbuf, 0, 2, NT * H, 64)
        pz = carve(dbuf, 2 * NT * H * 64, NT, 256)
        zT = carve(dbuf, 0, 2, FC, T)
        sT = carve(dbuf, 2 * FC * T, 2, T)
        mflat = mprod[:, :, :].rearrange("p a b -> p (a b)")
        grow = carve(mflat, 0, 2, 512)
        lamt = carve(mflat, 0, L, 4, 32)
        Ud = carve(attT[:, :, :].rearrange("p a b -> p (a b)"), 0, 2, 768)
        nkout = carve(rtmp, 0, H, 64)
        stout = carve(rtmp, 256, HP, 2, 64)

        o = [0]

        def cst(*shape):
            v = carve(const, o[0], *shape)
            o[0] += int(np.prod(shape))
            return v

        ident = cst(P)
        dftc = cst(2 * P)
        dftl = cst(2, 512)
        chc, chs = cst(P), cst(P)
        ropec, ropes = cst(2, 32), cst(2, 16)
        namask = cst(GRID_W)
        ones = cst(P)
        sel = cst(2, P)
        rank = cst(4)
        assert o[0] == consts.shape[1]
        par_g1, par_g2 = carve(par, 0, L, KC), carve(par, L * KC, L, KC)
        par_ab = carve(par, 2 * L * KC, L, 48)
        par_lb = carve(par, 2 * L * KC + 48 * L, L, 4)
        par_c = carve(par, 2 * L * KC + 52 * L, KC, 2)
        npar = 2 * L * KC + 52 * L + 2 * KC
        assert npar == params.shape[1]

        o[0] = 0

        def tmp(*shape):
            v = carve(small, o[0], *shape)
            o[0] += int(np.prod(shape))
            return v

        ss, ms, lnv, rs, nt1, nt2 = (tmp(24) for _ in range(6))
        sc = tmp(KC, 2)
        lbt, omlb = tmp(L, 4), tmp(L, 4)
        lam = tmp(L)
        A1 = tmp(2, KC, 2)
        sums = tmp(2, 2)
        mx, nmx = tmp(2, 2), tmp(2, 2)
        rsum = tmp(4, 2)
        rneg = tmp(2, 1)
        logit, score, selv = tmp(NT, NE), tmp(NT, NE), tmp(NT, NE)
        eqv, oh1, oh2, rest = (tmp(NT * 4, 4) for _ in range(4))
        m1, m2, gsc, gsel = (tmp(NT * 4) for _ in range(4))
        gm = tmp(NT)
        den = tmp(NT)
        gates = tmp(NT, NE)
        gdec = tmp(6, 2)
        e1 = tmp(KC, 2)
        lbe = tmp(L, 4)
        lbm = tmp(4)
        lm2 = tmp(L, 2)
        lme = tmp(L, 2)

        full = [sem(f"bank{b}_filled") for b in range(BANKS)]
        free = [sem(f"bank{b}_read_out") for b in range(BANKS)]
        landed = [sem(f"slot{s}_landed") for s in range(SLOTS)]
        d_x, d_const, d_par, d_row, d_out = (sem(n) for n in ("x_landed", "consts_landed", "params_landed", "rows_landed", "outputs_stored"))
        d_st, d_y = sem("scan_states_stored"), sem("y_stored")
        d_skew = sem("skew_rows_written")
        skew = nc.dram_tensor("skew_rows", (L * H * RPB_H, GRID_W, RPER), F32, kind="Internal").ap()
        d_gb, d_cache, d_state, d_bias, d_fin = (sem(n) for n in ("gatebias_landed", "cache_landed", "state_landed", "bias_landed", "final_gain_landed"))
        ch_dve, ch_act, ch_pool = (sem(n) for n in ("vector_step", "scalar_step", "pool_step"))
        s_expc, s_sc, s_lbl, s_lbe = (sem(n) for n in ("exp_c_ready", "silu_c_ready", "init_exponents_ready", "init_exps_ready"))
        s_ss, s_ms, s_ln, s_xn = (sem(n) for n in ("sumsq_ready", "meansq_ready", "rstd_guess_ready", "xnorm_ready"))
        s_mod, s_eq, s_e, s_f, s_lf = (sem(n) for n in ("modulation_ready", "exp_q_ready", "exp_z_ready", "forget_ready", "log_forget_ready"))
        s_q, s_diff, s_dec, s_X, s_att = (sem(n) for n in ("q_ready", "exponents_ready", "decays_ready", "operands_ready", "b_scores_ready"))
        s_rope, s_bias, s_mx, s_pr, s_w = (sem(n) for n in ("rope_done", "bias_masked", "neg_max_ready", "c_latent_probs_ready", "weights_ready"))
        s_pss, s_pln, s_ebg, s_post = (sem(n) for n in ("sub_meansq_ready", "sub_rstd_guess_ready", "exp_bg_ready", "subnorm_ready"))
        s_x, s_rl, s_re, s_gates, s_y = (sem(n) for n in ("residual_done", "logits_ready", "router_exp_ready", "gates_ready", "result_ready"))

        def bank(job, i=0):
            b, nth = place[job]
            return b, nth + i * PER_BODY

        def begin(pe, job, i=0):
            b, nth = bank(job, i)
            if place[job][1] > 1:
                pe.wait_ge(free[b], nth - 1)
            return ps[:, b, :]

        def ready(eng, job, i=0):
            b, nth = bank(job, i)
            eng.wait_ge(full[b], nth)
            return ps[:, b, :]

        def moved(eng, job, i=0):
            b, nth = bank(job, i)
            eng.wait_ge(free[b], nth)

        def release(eng, ins, job, i=0):
            b, nth = bank(job, i)
            ins.then_inc(free[b], 1)
            eng.wait_ge(free[b], nth)

        def nth_block(l, kind, j):
            return l * PER_LAYER + PRE.index((kind, j))

        last_job = {}
        for l in range(L):
            for j in ADA_COL + ADA_COL2:
                last_job[("ada", l, j)] = ("mod", l, j)
            for j in ADA_GATE1 + ADA_GATE2:
                last_job[("ada", l, j)] = ("grow", l, j)
            for j, job in zip(WIN_ORDER, [("av", l, 2), ("z", l, 1, 1), ("bvg", l, 2), ("aqk", l, 2), ("ck", l, 1), ("cvdu", l, 2)]):
                last_job[("win", l, j)] = job
            for j in range(2):
                last_job[("wout", l, j)] = ("wo", l, j, NT - 1)
        EXPERT_LAST = [lambda e, l: ("a", l, e, FC - 1), lambda e, l: ("u", l, e, FC - 1), lambda e, l: ("dn", l, e, 1, NT - 1)]

        block = ctx.enter_context(nc.Block())

        @block.sync
        def _(sp):
            sp.dma_start(par[:, :], params).then_inc(d_par, 16)
            xs = x_sample[0].rearrange("(t p) d -> p t d", p=P)
            sp.dma_start(x[:, 0, :], x_prompt[0]).then_inc(d_x, 16)
            sp.dma_start(x[:, 1:3, :], xs).then_inc(d_x, 16)
            order = []
            for l in range(L):
                order += [(kind, l, j) for kind, j in PRE]
                for i_n, blk in enumerate([(k, l, j) for k, j in PRE]):
                    n = l * PER_LAYER + i_n
                    kind, _, j = blk
                    if n >= SLOTS and i_n >= SLOTS:
                        ready(sp, last_job[order[-len(PRE) + i_n - SLOTS]])
                    elif n >= SLOTS:
                        q = 3 * EXP_PER_BODY - SLOTS + i_n
                        ready(sp, EXPERT_LAST[q % 3](q // 3, l - 1), NBODY - 1)
                    if kind == "ada":
                        src = ada_w[l, :, j * 512:(j + 1) * 512]
                    elif kind == "win":
                        src = w_in[l, :, j * 512:(j + 1) * 512]
                    else:
                        src = w_out[l, :, j * 512:(j + 1) * 512]
                    sp.dma_start(ring[:, n % SLOTS, :].rearrange("p (k n) -> p k n", k=KC),
                                 src.rearrange("(k p) n -> p k n", p=P)).then_inc(landed[n % SLOTS], 16)
                gview = moe_w_gate[l].rearrange("e (k p) n -> e p k n", p=P)
                uview = moe_w_up[l].rearrange("e (k p) n -> e p k n", p=P)
                dview = moe_w_down[l].rearrange("e (k p) n -> e p k n", p=P)

                def expert_block(e, i, q, first):
                    slot = (len(PRE) + q) % SLOTS
                    if first and q < SLOTS:
                        kind, j = PRE[len(PRE) - SLOTS + q]
                        ready(sp, last_job[(kind, l, j)])
                    else:
                        back = q - SLOTS
                        if back >= 0:
                            ready(sp, EXPERT_LAST[back % 3](back // 3, l), i)
                        else:
                            back += 3 * EXP_PER_BODY
                            ready(sp, EXPERT_LAST[back % 3](back // 3, l), i - 1)
                        if not first:
                            sp.wait_ge(d_par, 16)
                    src = (gview, uview, dview)[q % 3][e]
                    dst = ring[:, slot, :].rearrange("p (k n) -> p k n", k=(KC, KC, FC)[q % 3])
                    sp.dma_start(dst, src).then_inc(landed[slot], 16)

                for q in range(3 * EXP_PER_BODY):
                    expert_block(q // 3, 0, q, True)
                with sp.Fori(1, NBODY) as i:
                    for q in range(3 * EXP_PER_BODY):
                        expert_block(i * EXP_PER_BODY + q // 3, i, q, False)
            sp.wait_ge(s_y, 1)
            sp.dma_start(y_prompt[0], xn[:, 0, :]).then_inc(d_y, 16)
            sp.dma_start(y_sample[0].rearrange("(t p) d -> p t d", p=P), xn[:, 1:3, :]).then_inc(d_y, 16)
            sp.wait_ge(d_y, 32)
            sp.wait_ge(d_out, 16 * 4 * L)

        @block.gpsimd
        def _(pool):
            n_pool = [0]

            def step(ins):
                n_pool[0] += 1
                ins.then_inc(ch_pool, 1)
                pool.wait_ge(ch_pool, n_pool[0])

            pool.dma_start(skew, rpb_pad.unsqueeze(1).broadcast_to([L * H * RPB_H, GRID_W, RPER])).then_inc(d_skew, 16)
            pool.dma_start(const[:, :], consts).then_inc(d_const, 16)
            pool.dma_start(mk[:, :, :], masks.rearrange("p (g n) -> p g n", g=GRAM)).then_inc(d_const, 16)
            pool.dma_start(mflat[:, 0:L * 128], diff_lambda.rearrange('l a d -> (l a d)').partition_broadcast(P)).then_inc(d_row, 16)
            pool.dma_start(gsub[:, 0, :, :], diff_subln_g.partition_broadcast(P)).then_inc(d_row, 16)
            pool.dma_start(gsub[:, 1, :, :], hgrn_norm_g.partition_broadcast(P)).then_inc(d_row, 16)
            pool.dma_start(wrt[:, :, :], router_w.rearrange("(k p) n -> p k n", p=P)).then_inc(d_row, 16)
            pool.dma_start(rbias[:, :], router_b.partition_broadcast(P)).then_inc(d_row, 16)
            for l in range(L):
                if l:
                    moved(pool, ("grow", l - 1, ADA_GATE2[1]))
                    moved(pool, ("ao", l - 1, len(ATT) - 1))
                pool.dma_start(gbias[0:2, :], ada_b[l, 2 * D:3 * D].partition_broadcast(2)).then_inc(d_gb, 16)
                for n, src in enumerate((cache_diff_k, cache_diff_v, cache_na_k, cache_na_v)):
                    pool.dma_start(cachek[:, n, :, :], src[0, l].rearrange("h p d -> p h d")).then_inc(d_cache, 16)
                for hp in range(HP):
                    for d in range(2):
                        pool.dma_start(S0[:, hp, d, :], state_hgrn[0, l, d, 2 * hp:2 * hp + 2].rearrange("h k v -> (h k) v")).then_inc(d_state, 16)
                if l == 0:
                    pool.wait_ge(d_skew, 16)
                for h in range(H):
                    for qt in range(2):
                        for r2 in range(2):
                            at = ((l * H + h) * RPB_H + 7 - 2 * qt - r2) * GRID_W * RPER + GRID_W - 1
                            src = bass.AP(skew.tensor, skew.offset + at, [[RPER - 1, GRID_W], [GRID_W * RPER, 4], [1, GRID_W]])
                            pool.dma_start(bias[64 * r2:64 * r2 + 64, h, qt, :, :], src).then_inc(d_bias, 16)
                pool.wait_ge(d_const, 32)
                pool.wait_ge(d_bias, 256 * (l + 1))
                bv3 = bias[:, :, :, :, :].rearrange("p h q r c -> p (h q r) c")
                pool.tensor_tensor(bv3, bv3, namask.unsqueeze(1).broadcast_to([P, 32, GRID_W]), ALU.add).then_inc(s_bias, 1)
                for t in range(NT):
                    moved(pool, ("aqk", l, t))
                if l:
                    pool.wait_ge(d_st, 16 * HP * 2 * l)
                    pool.wait_ge(d_out, 16 * 4 * l)
                qk = tok[:, 1:3, 0:512]
                for t in range(2):
                    v = qk[:, t, :].rearrange("p (g r) -> p g r", r=32)
                    pr = qk[:, t, :].rearrange("p (g r two) -> p g r two", r=16, two=2)
                    rr = rtmp[:, :].rearrange("p (g r two) -> p g r two", r=16, two=2)
                    sn = ropes[:, t, :].unsqueeze(1).broadcast_to([P, 16, 16])
                    step(pool.tensor_tensor(rr[:, :, :, 0], pr[:, :, :, 1], sn, ALU.mult))
                    step(pool.tensor_tensor(rr[:, :, :, 1], pr[:, :, :, 0], sn, ALU.mult))
                    step(pool.tensor_tensor(v, v, ropec[:, t, :].unsqueeze(1).broadcast_to([P, 16, 32]), ALU.mult))
                    step(pool.tensor_tensor(pr[:, :, :, 0], pr[:, :, :, 0], rr[:, :, :, 0], ALU.subtract))
                    step(pool.tensor_tensor(pr[:, :, :, 1], pr[:, :, :, 1], rr[:, :, :, 1], ALU.add))
                pool.engine_nop().then_inc(s_rope, 1)
                moved(pool, ("cvdu", l, 0))
                for dst, c0 in ((new_diff_k, AK), (new_diff_v, AV), (new_na_v, CV)):
                    pool.dma_start(dst[0, l].rearrange("h p d -> p h d"),
                                   tok[:, 0, c0:c0 + 256].rearrange("p (h d) -> p h d", h=H)).then_inc(d_out, 16)
                moved(pool, ("nk", l))
                pool.dma_start(new_na_k[0, l].rearrange("h p d -> p h d"), nkout).then_inc(d_out, 16)
                moved(pool, ("kv", l, 0))
                moved(pool, ("kv", l, 1))
                for n in range(HP * 2):
                    hp, d = n // 2, n % 2
                    pool.dma_start(new_state[0, l, d, 2 * hp:2 * hp + 2].rearrange("h k v -> (h k) v"),
                                   stout[:, hp, d, :]).then_inc(d_st, 16)
                moved(pool, ("ao", l, len(ATT) - 1))
                pool.dma_start(gbias[0:2, :], ada_b[l, 5 * D:6 * D].partition_broadcast(2)).then_inc(d_gb, 16)
            pool.wait_ge(s_x, 2 * L)
            pool.dma_start(gate[:, 0, :], final_norm_g.partition_broadcast(P)).then_inc(d_fin, 16)
            pool.wait_ge(d_st, 16 * HP * 2 * L)

        @block.scalar
        def _(act):
            n_act = [0]

            def step(ins):
                n_act[0] += 1
                ins.then_inc(ch_act, 1)
                act.wait_ge(ch_act, n_act[0])

            def rstd_guess(cols, s_in, n_in, s_done):
                act.wait_ge(s_in, n_in)
                step(act.activation(lnv[:, 0:cols], ms[:, 0:cols], ACT.Ln))
                act.activation(rs[:, 0:cols], lnv[:, 0:cols], ACT.Exp, scale=-0.5).then_inc(s_done, 1)

            def sum_squares(n):
                if n:
                    act.wait_ge(s_x, n)
                else:
                    act.wait_ge(d_x, 32)
                for t in range(NT):
                    ins = act.activation(junk, x[:, t, :], ACT.Square, accum_out=ss[:, t:t + 1])
                    if t < NT - 1:
                        step(ins)
                    else:
                        ins.then_inc(s_ss, 1)
                rstd_guess(NT, s_ms, n + 1, s_ln)

            def gate_copy(l, js):
                for j in js:
                    for s in range(2):
                        p = ready(act, ("gbc", l, j, s))
                        release(act, act.activation(gate[:, s, (j % 2) * 512:(j % 2 + 1) * 512], p, ACT.Copy), ("gbc", l, j, s))

            def modulate(l, which):
                act.wait_ge(s_mod, l + 1)
                for k in range(1, KC, 2):
                    job = ("hT", 2 * l + which, k)
                    p = ready(act, job)
                    for s, (a, b) in enumerate(((0, P), (P, T))):
                        ins = act.activation(hT[:, k, a:b], p[:, a:b], ACT.Identity, scale=A1[:, which, k, s:s + 1],
                                             bias=modT[:, 2 * which, k, s:s + 1])
                        if s == 0:
                            step(ins)
                    release(act, ins, job)

            def copy_out(dst, job, cols=None, src=None):
                p = ready(act, job)
                release(act, act.activation(dst, p[:, 0:cols] if src is None else src(p), ACT.Copy), job)

            act.wait_ge(d_par, 16)
            act.activation(e1, par_c, ACT.Exp, scale=-1.0).then_inc(s_expc, 1)
            act.wait_ge(s_lbl, 1)
            act.activation(lbe, lbe, ACT.Exp).then_inc(s_lbe, 1)
            act.activation(lme, lm2, ACT.Exp).then_inc(s_lbe, 1)
            c_lat = 0
            for l in range(L):
                sum_squares(2 * l)
                gate_copy(l, ADA_GATE1)
                modulate(l, 0)
                for hp in range(HP):
                    p = ready(act, ("bq", l, hp))
                    act.activation(E[:, 0, hp, :], p[:, 0:T], ACT.Exp, scale=-1.0).then_inc(s_eq, 1)
                for t in range(NT):
                    copy_out(tok[:, t, AV:AV + 256], ("av", l, t), 256)
                for d in range(2):
                    for hp in range(HP):
                        moved(act, ("z", l, d, hp))
                act.activation(E, Z, ACT.Exp, scale=-1.0).then_inc(s_e, 1)
                for t in range(NT):
                    copy_out(tok[:, t, BV:BV + 512], ("bvg", l, t), 512)
                act.wait_ge(s_f, l + 1)
                act.activation(F, F, ACT.Ln).then_inc(s_lf, 1)

                def decays(u):
                    act.wait_ge(s_diff, l * len(UNITS) + u + 1)
                    act.activation(dec[u % 2], dec[u % 2], ACT.Exp).then_inc(s_dec, 1)

                for t in range(NT):
                    copy_out(tok[:, t, 0:512], ("aqk", l, t), 512)
                decays(0)
                for hp in range(HP):
                    copy_out(cqT[:, hp, :], ("cq", l, hp), T)
                for hp in range(HP):
                    p = ready(act, ("ck", l, hp))
                    step(act.activation(ckT[:, hp, 0:P], p[:, 0:P], ACT.Copy))
                    release(act, act.activation(ckT[:, hp, 2 * P:4 * P], p[:, P:T], ACT.Copy), ("ck", l, hp))
                decays(1)
                for t in range(NT):
                    copy_out(tok[:, t, CV:CV + 512], ("cvdu", l, t), 512)
                for c in range(2):
                    copy_out(Ud[:, c, 0:256], ("du", l, c, 0), 256)
                    copy_out(Ud[:, c, 256:768], ("du", l, c, 1), 512)
                for c in range(2):
                    copy_out(hT[:, 6 + c, :], ("dy", l, c), T)
                copy_out(ckT[:, :, P:2 * P], ("cc", l), src=lambda p: p[:, 0:256].rearrange("p (a b) -> p a b", a=HP))
                act.wait_ge(s_rope, l + 1)
                copy_out(rtmp[:, 0:256], ("nk", l), 256)
                for u, (t, hp) in enumerate(UNITS):
                    nd = 2 if t == 0 else 1
                    copy_out(kdT[:, u % 2, 0:nd, :].rearrange("p a b -> p (a b)"), ("kd", l, u), nd * P)
                    if u + 2 < len(UNITS):
                        decays(u + 2)
                for t in range(NT):
                    for h2 in range(2):
                        copy_out(oB[:, t * H + h2:(t + 1) * H:2, :], ("bo", l, t, h2),
                                 src=lambda p: p[:, 0:P].rearrange("p (a b) -> p a b", a=HP))
                for hp in range(HP):
                    copy_out(aqT[:, hp, :], ("aT", l, 0, hp), T)
                for hp in range(HP):
                    copy_out(akT[:, hp, :], ("aT", l, 1, hp), 4 * P)
                for i in range(len(ATT) + 2):
                    if i < len(ATT):
                        m, t, h = ATT[i]
                        nk = T if t else P
                        act.wait_ge(s_mx, l * len(ATT) + i + 1)
                        if m == "C" and t:
                            act.activation(prob[:, i % 2, 0, 0:nk], scb[:, i % 2, 0:nk], ACT.Exp, bias=nmx[:, i % 2, 0:1],
                                           accum_out=sums[:, i % 2, 0:1]).then_inc(s_pr, 1)
                        else:
                            scale = 32 ** -0.5 if m == "A" else 64 ** -0.5
                            for mp in range(2 if m == "A" else 1):
                                p = ready(act, ("sc", l, i, mp))
                                release(act, act.activation(prob[:, i % 2, mp, 0:nk], p[:, 0:nk], ACT.Exp, scale=scale,
                                                            bias=nmx[:, i % 2, mp:mp + 1],
                                                            accum_out=sums[:, i % 2, mp:mp + 1]), ("sc", l, i, mp))
                    if 0 <= i - 1 < len(ATT):
                        nk = T if ATT[i - 1][1] else P
                        copy_out(wT[:, (i - 1) % 2, 0:nk], ("pT", l, i - 1), nk)
                    if i >= 2:
                        m, t, h = ATT[i - 2]
                        p = ready(act, ("ao", l, i - 2))
                        act.wait_ge(s_w, l * len(ATT) + i - 1)
                        dst = (oA if m == "A" else oC)[:, t * H + h, :]
                        release(act, act.activation(dst, p[:, 0:64], ACT.Copy, scale=rsum[:, (i - 2) % 4, 0:1]), ("ao", l, i - 2))
                act.activation(pz, tok[:, :, BG:BG + 256], ACT.Exp, scale=-1.0).then_inc(s_ebg, 1)
                rstd_guess(24, s_pss, l + 1, s_pln)
                for c in range(1, 6, 2):
                    copy_out(hT[:, c, :], ("mT", l, c), T)
                act.wait_ge(d_out, 16 * 4 * (l + 1))
                sum_squares(2 * l + 1)
                gate_copy(l, ADA_GATE2)
                modulate(l, 1)
                act.wait_ge(s_rl, l + 1)
                act.activation(score, logit, ACT.Exp, scale=-1.0).then_inc(s_re, 1)
                with act.Fori(0, NBODY) as i:
                    for e in range(EXP_PER_BODY):
                        for f in range(FC):
                            p = ready(act, ("a", l, e, f), i)
                            if f >= 2:
                                moved(act, ("u", l, e, f - 2), i)
                            elif e:
                                moved(act, ("u", l, e - 1, f + 2), i)
                            release(act, act.activation(sT[:, f % 2, :], p[:, 0:T], ACT.Silu), ("a", l, e, f), i)
            sum_squares(2 * L)

        @block.vector
        def _(dve):
            n_dve = [0]

            def step(ins):
                n_dve[0] += 1
                ins.then_inc(ch_dve, 1)
                dve.wait_ge(ch_dve, n_dve[0])

            def newton(cols):
                a, r = nt1[:, 0:cols], rs[:, 0:cols]
                step(dve.tensor_tensor(a, r, r, ALU.mult))
                step(dve.tensor_tensor(a, a, ms[:, 0:cols], ALU.mult))
                step(dve.tensor_scalar(a, a, -0.5, 1.5, ALU.mult, ALU.add))
                step(dve.tensor_tensor(r, r, a, ALU.mult))

            def normalize(n):
                dve.wait_ge(s_ss, n + 1)
                dve.tensor_scalar(ms[:, 0:NT], ss[:, 0:NT], 1.0 / D, EPS, ALU.mult, ALU.add).then_inc(s_ms, 1)
                dve.wait_ge(s_ms, n + 1)
                dve.wait_ge(s_ln, n + 1)
                newton(NT)
                for t in range(NT):
                    ins = dve.tensor_scalar(xn[:, t, :], x[:, t, :], rs[:, t:t + 1], None, ALU.mult)
                    if t < NT - 1:
                        step(ins)
                ins.then_inc(s_xn, 1)
                dve.wait_ge(s_xn, n + 1)

            def modulation(l, j):
                vec = {0: 0, 1: 1, 3: 2, 4: 3}[j // 2]
                p = ready(dve, ("mod", l, j))
                out = modT[:, vec, 4 * (j % 2):4 * (j % 2) + 4, :]
                b = par_ab[:, l, 4 * j:4 * j + 4].unsqueeze(2).broadcast_to([P, 4, 2])
                release(dve, dve.tensor_tensor(out, p[:, 0:8].rearrange("p (c s) -> p c s", s=2), b, ALU.add), ("mod", l, j))

            def gate_rows(l, which, js):
                dve.wait_ge(d_gb, 16 * (2 * l + which + 1))
                for j in js:
                    p = ready(dve, ("grow", l, j))
                    release(dve, dve.tensor_tensor(grow[0:2, j % 2, :], p[0:2, :], gbias[0:2, (j % 2) * 512:(j % 2 + 1) * 512],
                                                   ALU.add), ("grow", l, j))

            def modulate(l, which):
                for k in range(0, KC, 2):
                    job = ("hT", 2 * l + which, k)
                    p = ready(dve, job)
                    for s, (a, b) in enumerate(((0, P), (P, T))):
                        ins = dve.tensor_scalar(hT[:, k, a:b], p[:, a:b], A1[:, which, k, s:s + 1],
                                                modT[:, 2 * which, k, s:s + 1], ALU.mult, ALU.add)
                        if s == 0:
                            step(ins)
                    release(dve, ins, job)

            def exponents(l, u):
                t, hp = UNITS[u]
                c2, out = C2[:, hp, t, :], dec[u % 2]
                for n, m in enumerate(LEVELS):
                    M, nb = 2 * m, P // (2 * m)
                    ref = strided(c2, m, [129, 2], [M, nb], [0, m])
                    right, left = (strided(c2, 1 + o_, [P, 2], [M, nb], [1, m]) for o_ in (m, 0))
                    step(dve.tensor_tensor(strided(out, n * 2 * P + m, [P, 2], [M, nb], [1, m]), right, ref, ALU.subtract))
                    step(dve.tensor_tensor(strided(out, n * 2 * P, [P, 2], [M, nb], [1, m]), ref, left, ALU.subtract))
                at = NLEV * 2 * P
                step(dve.tensor_copy(out[:, at:at + P], c2[:, 1:129]))
                step(dve.tensor_copy(out[:, at + 3 * P:at + 4 * P], c2[:, 129:257]))
                step(dve.tensor_scalar(out[:, at + P:at + 2 * P], c2[:, 129:257], -1.0, c2[:, 257:258], ALU.mult, ALU.add))
                step(dve.tensor_scalar(out[:, at + 2 * P:at + 3 * P], c2[:, 1:129], -1.0, c2[:, 128:129], ALU.mult, ALU.add))
                dve.tensor_copy(out[:, at + 4 * P:at + 4 * P + 2], strided(c2, 128, [129, 2])).then_inc(s_diff, 1)
                dve.wait_ge(s_diff, l * len(UNITS) + u + 1)

            def operands(l, u):
                t, hp = UNITS[u]
                d_, q0, k0 = dec[u % 2], qT[:, hp, t * P:(t + 1) * P], kT[:, 0, hp, t * P:(t + 1) * P]
                dve.wait_ge(s_dec, l * len(UNITS) + u + 1)
                for n, m in enumerate(LEVELS):
                    M, nb, base = 2 * m, P // (2 * m), n * 2 * P
                    o_ = strided(d_, base + m, [P - m, 2], [M, nb], [1, m])
                    step(dve.tensor_tensor(o_, o_, strided(q0, m, [-m, 2], [M, nb], [1, m]), ALU.mult))
                    o_ = strided(d_, base, [P + m, 2], [M, nb], [1, m])
                    step(dve.tensor_tensor(o_, o_, strided(k0, 0, [HP * T + m, 2], [M, nb], [1, m]), ALU.mult))
                at = NLEV * 2 * P
                if t:
                    step(dve.tensor_tensor(qdec[:, t - 1, hp, :, :], strided(d_, at, [P, 2], [1, P]),
                                           q0.unsqueeze(1).broadcast_to([P, 2, P]), ALU.mult))
                kk = strided(d_, at + 2 * P, [P, 2], [1, P])
                step(dve.tensor_tensor(kk, kk, strided(k0, 0, [HP * T, 2], [1, P]), ALU.mult))
                step(dve.tensor_copy(gdec[:, u, :], d_[:, at + 4 * P:at + 4 * P + 2]))
                dve.tensor_tensor(d_[:, at:at + P], k0, kT[:, 1, hp, t * P:(t + 1) * P], ALU.add).then_inc(s_X, 1)
                dve.wait_ge(s_X, l * len(UNITS) + u + 1)

            def masked_scores(l, u, h2):
                dst = attT[:, 2 * u + h2, :]
                for half in range(2):
                    for g in (2 * half, 2 * half + 1):
                        n = min(4, GRAM - 4 * g)
                        p = ready(dve, ("gram", l, u, h2, g))
                        release(dve, dve.tensor_tensor(mprod[:, 4 * (g % 2):4 * (g % 2) + n, :],
                                                       p[:, 0:n * P].rearrange("p (a b) -> p a b", a=n),
                                                       mk[:, 4 * g:4 * g + n, :], ALU.mult), ("gram", l, u, h2, g))
                    n = 8 - half
                    red = mprod[:, 0:n, :].rearrange("p a b -> p b a")
                    if half == 0:
                        step(dve.tensor_reduce(dst, red, AX, ALU.add))
                    else:
                        step(dve.tensor_reduce(mprod[:, 7, :], red, AX, ALU.add))
                dve.tensor_tensor(dst, dst, mprod[:, 7, :], ALU.add).then_inc(s_att, 1)
                dve.wait_ge(s_att, (l * len(UNITS) + u) * 2 + h2 + 1)

            def states(l, u):
                t, hp = UNITS[u]
                job = ("kv", l, u)
                p = ready(dve, job)
                if t == 0:
                    dve.wait_ge(s_rope, l + 1)
                else:
                    dve.wait_ge(d_state, 16 * 4 * (l + 1))
                for h2 in range(2):
                    r = slice(64 * h2, 64 * h2 + 64)
                    if t == 0:
                        ins = dve.tensor_copy(stout[r, hp, :, :], p[r, 0:2 * P].rearrange("p (d c) -> p d c", d=2)[:, :, 64 * h2:64 * h2 + 64])
                    else:
                        ins = dve.scalar_tensor_tensor(out=S1[r, hp, t - 1, :], in0=S0[r, hp, t - 1, :],
                                                       scalar=gdec[r, u, t - 1:t], in1=p[r, 64 * h2:64 * h2 + 64],
                                                       op0=ALU.mult, op1=ALU.add)
                    if h2 == 0:
                        step(ins)
                release(dve, ins, job)

            dve.wait_ge(d_par, 16)
            dve.wait_ge(d_row, 16 * 5)
            dve.wait_ge(d_const, 32)
            step(dve.tensor_tensor(lbm, par_lb[:, 0, :], par_lb[:, 1, :], ALU.max))
            step(dve.tensor_tensor(lbe, par_lb, lbm.unsqueeze(1).broadcast_to([P, L, 4]), ALU.subtract))
            step(dve.tensor_tensor(lamt[:, :, 0::2, :], lamt[:, :, 0::2, :], lamt[:, :, 1::2, :], ALU.mult))
            dve.tensor_reduce(lm2, lamt[:, :, 0::2, :], AX, ALU.add).then_inc(s_lbl, 1)
            dve.wait_ge(s_lbl, 1)
            dve.wait_ge(s_expc, 1)
            step(dve.tensor_scalar(e1, e1, 1.0, None, ALU.add))
            step(dve.reciprocal(e1, e1))
            dve.tensor_tensor(sc, par_c, e1, ALU.mult).then_inc(s_sc, 1)
            dve.wait_ge(s_lbe, 2)
            step(dve.tensor_tensor(lbm, lbe[:, 0, :], lbe[:, 1, :], ALU.add))
            step(dve.reciprocal(lbm, lbm))
            step(dve.tensor_tensor(lbe, lbe, lbm.unsqueeze(1).broadcast_to([P, L, 4]), ALU.mult))
            step(dve.tensor_tensor(lbt[:, 0, :], lbe[:, 0, :], lbe[:, 0, :], ALU.subtract))
            step(dve.tensor_tensor(lbt[:, 1, :], lbt[:, 0, :], lbe[:, 1, :], ALU.add))
            step(dve.tensor_scalar(omlb, lbt, -1.0, 1.0, ALU.mult, ALU.add))
            for l in range(L):
                lam_init = 0.8 - 0.6 * math.exp(-0.3 * l)
                step(dve.tensor_tensor(lam[:, l:l + 1], lme[:, l, 1:2], lme[:, l, 0:1], ALU.subtract))
                step(dve.tensor_scalar(lam[:, l:l + 1], lam[:, l:l + 1], -lam_init, None, ALU.add))
                step(dve.tensor_scalar(gsub[:, 0, l, :], gsub[:, 0, l, :], 1.0 - lam_init, None, ALU.mult))

            for l in range(L):
                normalize(2 * l)
                for j in ADA_COL:
                    modulation(l, j)
                gate_rows(l, 0, ADA_GATE1)
                for j in ADA_COL2:
                    modulation(l, j)
                for w, g in enumerate((par_g1, par_g2)):
                    step(dve.tensor_scalar(A1[:, w, :, :], modT[:, 2 * w + 1, :, :], 1.0, None, ALU.add))
                    ins = dve.tensor_tensor(A1[:, w, :, :], A1[:, w, :, :], g[:, l, :].unsqueeze(2).broadcast_to([P, KC, 2]), ALU.mult)
                    if w == 0:
                        step(ins)
                ins.then_inc(s_mod, 1)
                dve.wait_ge(s_mod, l + 1)
                modulate(l, 0)
                for hp in range(HP):
                    dve.wait_ge(s_eq, HP * l + hp + 1)
                    step(dve.tensor_scalar(E[:, 0, hp, :], E[:, 0, hp, :], 1.0, None, ALU.add))
                    step(dve.reciprocal(E[:, 0, hp, :], E[:, 0, hp, :]))
                    p = ready(dve, ("bq", l, hp))
                    release(dve, dve.tensor_tensor(qT[:, hp, :], E[:, 0, hp, :], p[:, 0:T], ALU.mult), ("bq", l, hp))
                for d in range(2):
                    for hp in range(HP):
                        p = ready(dve, ("z", l, d, hp))
                        release(dve, dve.tensor_scalar(Z[:, d, hp, :], p[:, 0:T], -80.0, None, ALU.max), ("z", l, d, hp))
                dve.wait_ge(s_e, l + 1)
                step(dve.tensor_scalar(Z, E, 1.0, None, ALU.add))
                step(dve.reciprocal(Z, Z))
                for d in range(2):
                    for hp in range(HP):
                        w = 2 * d + hp
                        step(dve.tensor_scalar(F[:, d, hp, :], Z[:, d, hp, :], omlb[:, l, w:w + 1], lbt[:, l, w:w + 1], ALU.mult, ALU.add))
                        step(dve.scalar_tensor_tensor(out=kT[:, d, hp, :], in0=E[:, d, hp, :], scalar=omlb[:, l, w:w + 1],
                                                      in1=Z[:, d, hp, :], op0=ALU.mult, op1=ALU.mult))
                dve.tensor_scalar(F, F, TINY, None, ALU.max).then_inc(s_f, 1)
                step(dve.memset(strided(C2[:, 0, 0, :], 0, [129, 2 * HP * NT]), 0.0))
                dve.wait_ge(s_lf, l + 1)
                for hp in range(HP):
                    for t in range(NT):
                        for d in range(2):
                            step(dve.tensor_tensor_scan(C2[:, hp, t, d * 129 + 1:d * 129 + 129], ones, F[:, d, hp, t * P:(t + 1) * P],
                                                        0.0, ALU.mult, ALU.add))
                exponents(l, 0)
                exponents(l, 1)
                operands(l, 0)
                for u in range(1, len(UNITS) + 1):
                    for h2 in range(2):
                        masked_scores(l, u - 1, h2)
                        if h2 == 0:
                            states(l, u - 1)
                    if u + 1 < len(UNITS):
                        exponents(l, u + 1)
                    if u < len(UNITS):
                        operands(l, u)
                n_clat = 0
                seen = {}
                for i in range(len(ATT) + 1):
                    if i < len(ATT):
                        m, t, h = ATT[i]
                        nk = T if t else P
                        if m == "C" and t:
                            n_clat += 1
                            seen[i] = n_clat
                            job = ("sc", l, i, 0)
                            p = ready(dve, job)
                            step(dve.tensor_scalar(scb[:, i % 2, 0:P], p[:, 0:P], 64 ** -0.5, None, ALU.mult))
                            dve.wait_ge(s_bias, l + 1)
                            release(dve, dve.scalar_tensor_tensor(
                                out=scb[:, i % 2, P:T], in0=p[:, P:T], scalar=64 ** -0.5,
                                in1=bias[:, h, t - 1, :, :].rearrange("p a b -> p (a b)"), op0=ALU.mult, op1=ALU.add), job)
                            step(dve.tensor_reduce(mx[:, i % 2, 0:1], scb[:, i % 2, :], AX, ALU.max))
                            dve.tensor_scalar(nmx[:, i % 2, 0:1], mx[:, i % 2, 0:1], -1.0, None, ALU.mult).then_inc(s_mx, 1)
                        else:
                            nm = 2 if m == "A" else 1
                            scale = 32 ** -0.5 if m == "A" else 64 ** -0.5
                            for mp in range(nm):
                                p = ready(dve, ("sc", l, i, mp))
                                step(dve.tensor_reduce(mx[:, i % 2, mp:mp + 1], p[:, 0:nk], AX, ALU.max))
                            dve.tensor_scalar(nmx[:, i % 2, 0:nm], mx[:, i % 2, 0:nm], -scale, None, ALU.mult).then_inc(s_mx, 1)
                    if i >= 1:
                        m, t, h = ATT[i - 1]
                        j = i - 1
                        nk = T if t else P
                        if m == "C" and t:
                            dve.wait_ge(s_pr, l * 8 + seen[j])
                        else:
                            for mp in range(2 if m == "A" else 1):
                                moved(dve, ("sc", l, j, mp))
                        if m == "A":
                            step(dve.reciprocal(rsum[:, j % 4, :], sums[:, j % 2, :]))
                            step(dve.tensor_scalar(rneg[:, j % 2, :], sums[:, j % 2, 0:1], rsum[:, j % 4, 1:2], lam[:, l:l + 1], ALU.mult, ALU.mult))
                            if j >= 2:
                                ready(dve, ("pT", l, j - 2))
                            dve.scalar_tensor_tensor(out=wmix[:, j % 2, 0:nk], in0=prob[:, j % 2, 1, 0:nk], scalar=rneg[:, j % 2, :],
                                                     in1=prob[:, j % 2, 0, 0:nk], op0=ALU.mult, op1=ALU.add).then_inc(s_w, 1)
                        else:
                            dve.reciprocal(rsum[:, j % 4, 0:1], sums[:, j % 2, 0:1]).then_inc(s_w, 1)
                        dve.wait_ge(s_w, l * len(ATT) + j + 1)
                for t in range(NT):
                    for h2 in range(2):
                        moved(dve, ("bo", l, t, h2))
                for i in (len(ATT) - 1, len(ATT) - 2, len(ATT) - 1 - H, len(ATT) - 2 - H):
                    moved(dve, ("ao", l, i))
                for n, o_ in enumerate((oA, oB)):
                    step(dve.tensor_tensor(post[:, n, :, :], o_, o_, ALU.mult))
                step(dve.tensor_reduce(ss, post.rearrange("p a b c -> p (a b) c"), AX, ALU.add))
                dve.tensor_scalar(ms, ss, 1.0 / 64, EPS, ALU.mult, ALU.add).then_inc(s_pss, 1)
                dve.wait_ge(s_pss, l + 1)
                dve.wait_ge(s_ebg, l + 1)
                step(dve.tensor_scalar(pz, pz, 1.0, None, ALU.add))
                step(dve.reciprocal(pz, pz))
                step(dve.tensor_tensor(pz, pz, tok[:, :, BG:BG + 256], ALU.mult))
                dve.wait_ge(s_pln, l + 1)
                newton(24)
                for n, o_ in enumerate((oB, oA)):
                    r0 = 12 * (1 - n)
                    step(dve.tensor_tensor(o_, o_, rs[:, r0:r0 + 12].unsqueeze(2).broadcast_to([P, 12, 64]), ALU.mult))
                    ins = dve.tensor_tensor(o_, o_, gsub[:, 1 - n, l, :].unsqueeze(1).broadcast_to([P, 12, 64]), ALU.mult)
                    if n == 0:
                        step(ins)
                        step(dve.tensor_tensor(o_, o_, pz.rearrange("p t (h c) -> p (t h) c", c=64), ALU.mult))
                ins.then_inc(s_post, 1)
                for c in range(0, 6, 2):
                    p = ready(dve, ("mT", l, c))
                    release(dve, dve.tensor_copy(hT[:, c, :], p[:, 0:T]), ("mT", l, c))
                for j in ADA_GATE1:
                    for s in range(2):
                        moved(dve, ("gbc", l, j, s))
                for b in range(2):
                    for t in range(NT):
                        job = ("wo", l, b, t)
                        p = ready(dve, job)
                        release(dve, dve.tensor_tensor(mflat[:, 0:512], p, gate[:, min(t, 1), b * 512:(b + 1) * 512], ALU.mult), job)
                        xs = x[:, t, b * 512:(b + 1) * 512]
                        ins = dve.tensor_tensor(xs, xs, mflat[:, 0:512], ALU.add)
                        if (b, t) != (1, NT - 1):
                            step(ins)
                ins.then_inc(s_x, 1)
                dve.wait_ge(s_x, 2 * l + 1)
                gate_rows(l, 1, ADA_GATE2)
                dve.wait_ge(d_out, 16 * 4 * (l + 1))
                normalize(2 * l + 1)
                modulate(l, 1)
                p = ready(dve, ("rt", l))
                release(dve, dve.tensor_copy(logit, p[:, 0:NT * NE].rearrange("p (t e) -> p t e", t=NT)), ("rt", l))
                dve.engine_nop().then_inc(s_rl, 1)
                dve.wait_ge(s_re, l + 1)
                step(dve.tensor_scalar(score, score, 1.0, None, ALU.add))
                step(dve.reciprocal(score, score))
                step(dve.tensor_tensor(selv, score, rbias[:, :].unsqueeze(1).broadcast_to([P, NT, NE]), ALU.add))
                sg = selv.rearrange("p t (g e) -> p (t g) e", e=4)
                rankb = rank.unsqueeze(1).broadcast_to([P, NT * 4, 4])

                def first_max(one_hot, values, best, n):
                    rb = rank.unsqueeze(1).broadcast_to([P, n, 4])
                    step(dve.tensor_reduce(best, values, AX, ALU.max))
                    step(dve.tensor_tensor(eqv[:, 0:n, :], values, best.unsqueeze(2).broadcast_to([P, n, 4]), ALU.is_equal))
                    step(dve.tensor_tensor(eqv[:, 0:n, :], eqv[:, 0:n, :], rb, ALU.mult))
                    step(dve.tensor_reduce(gsel[:, 0:n], eqv[:, 0:n, :], AX, ALU.max))
                    step(dve.tensor_tensor(one_hot, eqv[:, 0:n, :], gsel[:, 0:n].unsqueeze(2).broadcast_to([P, n, 4]), ALU.is_equal))

                first_max(oh1, sg, m1, NT * 4)
                step(dve.scalar_tensor_tensor(out=rest, in0=oh1, scalar=-1e30, in1=sg, op0=ALU.mult, op1=ALU.add))
                first_max(oh2, rest, m2, NT * 4)
                step(dve.tensor_tensor(gsc, m1, m2, ALU.add))
                step(dve.tensor_tensor(oh1, oh1, oh2, ALU.add))
                g4 = rest[:, 0:NT, :]
                first_max(g4, gsc.rearrange("p (t g) -> p t g", g=4), gm, NT)
                step(dve.tensor_tensor(oh1.rearrange("p (t g) e -> p t g e", g=4), oh1.rearrange("p (t g) e -> p t g e", g=4),
                                       g4.unsqueeze(3).broadcast_to([P, NT, 4, 4]), ALU.mult))
                step(dve.tensor_tensor(gates, score, oh1.rearrange("p (t g) e -> p t (g e)", g=4), ALU.mult))
                step(dve.tensor_reduce(den, gates, AX, ALU.add))
                step(dve.reciprocal(den, den))
                step(dve.tensor_tensor(gates, gates, den.unsqueeze(2).broadcast_to([P, NT, NE]), ALU.mult))
                step(dve.memset(ysum, 0.0))
                with dve.Fori(0, NBODY) as i:
                    for e in range(EXP_PER_BODY):
                        for f in range(FC):
                            moved(dve, ("a", l, e, f), i)
                            p = ready(dve, ("u", l, e, f), i)
                            release(dve, dve.tensor_tensor(zT[:, e % 2, f, :], sT[:, f % 2, :], p[:, 0:T], ALU.mult), ("u", l, e, f), i)
                        for b in range(2):
                            for t in range(NT):
                                p = ready(dve, ("dn", l, e, b, t), i)
                                yv = ysum[:, t, b * 512:(b + 1) * 512]
                                release(dve, dve.scalar_tensor_tensor(out=yv, in0=p, scalar=gates[:, t, bass.ds(i * EXP_PER_BODY + e, 1)], in1=yv,
                                                                      op0=ALU.mult, op1=ALU.add), ("dn", l, e, b, t), i)
                for j in ADA_GATE2:
                    for s in range(2):
                        moved(dve, ("gbc", l, j, s))
                step(dve.tensor_tensor(ysum[:, 0, :], ysum[:, 0, :], gate[:, 0, :], ALU.mult))
                step(dve.tensor_tensor(ysum[:, 1:3, :], ysum[:, 1:3, :], gate[:, 1, :].unsqueeze(1).broadcast_to([P, 2, D]), ALU.mult))
                dve.tensor_tensor(x[:, :, :], x[:, :, :], ysum, ALU.add).then_inc(s_x, 1)
                dve.wait_ge(s_x, 2 * l + 2)
            normalize(2 * L)
            dve.wait_ge(d_fin, 16)
            dve.tensor_tensor(xn, xn, gate[:, 0, :].unsqueeze(1).broadcast_to([P, NT, D]), ALU.mult).then_inc(s_y, 1)

        @block.tensor
        def _(pe):
            def slot(l, kind, j):
                n = nth_block(l, kind, j)
                pe.wait_ge(landed[n % SLOTS], 16 * (n // SLOTS + 1))
                return ring[:, n % SLOTS, :].rearrange("p (k n) -> p k n", k=KC)

            def fill(ins, job, i=0):
                ins.then_inc(full[bank(job, i)[0]], 1)

            def matmuls(out, pairs):
                for n, (a, b) in enumerate(pairs):
                    ins = pe.matmul(out, a, b, start=(n == 0), stop=(n == len(pairs) - 1))
                return ins

            def modulation(l, j):
                w, job = slot(l, "ada", j), ("mod", l, j)
                p = begin(pe, job)
                for c in range(4):
                    ins = matmuls(p[:, 2 * c:2 * c + 2], [(w[:, k, c * P:(c + 1) * P], sc[:, k, :]) for k in range(KC)])
                fill(ins, job)

            def gate_row(l, j):
                w, job = slot(l, "ada", j), ("grow", l, j)
                p = begin(pe, job)
                fill(matmuls(p[0:2, :], [(sc[:, k, :], w[:, k, :]) for k in range(KC)]), job)

            def gate_spread(l, js):
                for j in js:
                    for s in range(2):
                        job = ("gbc", l, j, s)
                        p = begin(pe, job)
                        moved(pe, ("grow", l, j))
                        fill(pe.matmul(p, sel[0:2, s, :], grow[0:2, j % 2, :], start=True, stop=True), job)

            def transposes(job, srcs):
                p = begin(pe, job)
                for n, s in enumerate(srcs):
                    ins = pe.transpose(p[:, n * P:(n + 1) * P], s, ident)
                fill(ins, job)

            def hidden(n):
                pe.wait_ge(s_xn, n + 1)
                for k in range(KC):
                    transposes(("hT", n, k), [xn[:, t, k * P:(k + 1) * P] for t in range(NT)])
                for k in range(KC):
                    moved(pe, ("hT", n, k))

            def by_token(l, w, job, t, c0, c1):
                p = begin(pe, job)
                fill(matmuls(p[:, 0:c1 - c0], [(hT[:, k, t * P:(t + 1) * P], w[:, k, c0:c1]) for k in range(KC)]), job)

            def by_feature(l, w, job, c):
                p = begin(pe, job)
                fill(matmuls(p[:, 0:T], [(w[:, k, c * P:(c + 1) * P], hT[:, k, :]) for k in range(KC)]), job)

            pe.wait_ge(s_sc, 1)
            pe.wait_ge(d_const, 32)
            pe.wait_ge(d_row, 16 * 5)
            for l in range(L):
                for j in ADA_COL:
                    modulation(l, j)
                for j in ADA_GATE1:
                    gate_row(l, j)
                for j in ADA_COL2:
                    modulation(l, j)
                gate_spread(l, ADA_GATE1)
                hidden(2 * l)
                w = slot(l, "win", 1)
                for hp in range(HP):
                    by_feature(l, w, ("bq", l, hp), 2 + hp)
                for t in range(NT):
                    by_token(l, w, ("av", l, t), t, 0, 256)
                w = slot(l, "win", 2)
                for d in range(2):
                    for hp in range(HP):
                        by_feature(l, w, ("z", l, d, hp), 2 * d + hp)
                w = slot(l, "win", 3)
                for t in range(NT):
                    by_token(l, w, ("bvg", l, t), t, 0, 512)
                w = slot(l, "win", 0)
                for t in range(NT):
                    by_token(l, w, ("aqk", l, t), t, 0, 512)
                w = slot(l, "win", 4)
                for hp in range(HP):
                    by_feature(l, w, ("cq", l, hp), hp)
                for hp in range(HP):
                    by_feature(l, w, ("ck", l, hp), 2 + hp)
                w = slot(l, "win", 5)
                for t in range(NT):
                    by_token(l, w, ("cvdu", l, t), t, 0, 512)
                for t in range(NT):
                    moved(pe, ("cvdu", l, t))
                for c in range(2):
                    ch = slice(DU + c * P, DU + (c + 1) * P)
                    p = begin(pe, ("du", l, c, 0))
                    fill(pe.matmul(p[:, 0:256], tok[:, 0, ch], dftc, start=True, stop=True), ("du", l, c, 0))
                    p = begin(pe, ("du", l, c, 1))
                    fill(matmuls(p, [(tok[:, 1 + t, ch], dftl[:, t, :]) for t in range(2)]), ("du", l, c, 1))
                for c in range(2):
                    job = ("dy", l, c)
                    p = begin(pe, job)
                    moved(pe, ("du", l, c, 0))
                    moved(pe, ("du", l, c, 1))
                    matmuls(p[:, 0:P], [(chc, Ud[:, c, 0:P]), (chs, Ud[:, c, P:2 * P])])
                    fill(matmuls(p[:, P:T], [(chc, Ud[:, c, 256:512]), (chs, Ud[:, c, 512:768])]), job)
                pe.wait_ge(d_cache, 64 * (l + 1))
                transposes(("cc", l), [cachek[:, 2, 2 * hp:2 * hp + 2, :].rearrange("p a b -> p (a b)") for hp in range(HP)])
                for hp in range(HP):
                    moved(pe, ("ck", l, hp))
                transposes(("nk", l), [ckT[:, hp, 0:P] for hp in range(HP)])
                at = NLEV * 2 * P
                for t in range(NT):
                    moved(pe, ("bvg", l, t))
                for u, (t, hp) in enumerate(UNITS):
                    d_ = dec[u % 2]
                    pe.wait_ge(s_X, l * len(UNITS) + u + 1)
                    dirs = (0, 1) if t == 0 else (t - 1,)
                    transposes(("kd", l, u), [d_[:, at + (2 + d) * P:at + (3 + d) * P] for d in dirs])
                    for h2 in range(2):
                        r = slice(64 * h2, 64 * h2 + 64)
                        for g in range(4):
                            job = ("gram", l, u, h2, g)
                            p = begin(pe, job)
                            for n in range(4 * g, min(4 * g + 4, GRAM)):
                                if n < 2 * NLEV:
                                    a = b = d_[r, n * P:(n + 1) * P]
                                else:
                                    a, b = d_[r, at:at + P], qT[r, hp, t * P:(t + 1) * P]
                                ins = pe.matmul(p[:, (n % 4) * P:(n % 4 + 1) * P], a, b, start=True, stop=True)
                            fill(ins, job)
                        if h2 == 0:
                            job = ("kv", l, u)
                            p = begin(pe, job)
                            moved(pe, ("kd", l, u))
                            for n in range(len(dirs)):
                                ins = pe.matmul(p[:, n * P:(n + 1) * P], kdT[:, u % 2, n, :], tok[:, t, BV + hp * P:BV + (hp + 1) * P],
                                                start=True, stop=True)
                            fill(ins, job)
                for u in range(len(UNITS)):
                    moved(pe, ("kv", l, u))
                pe.wait_ge(s_att, 2 * len(UNITS) * (l + 1))
                for t in range(NT):
                    for h2 in range(2):
                        job = ("bo", l, t, h2)
                        p = begin(pe, job)
                        r = slice(64 * h2, 64 * h2 + 64)
                        for hp in range(HP):
                            h = 2 * hp + h2
                            pairs = [(attT[:, 2 * (t * HP + hp) + h2, :], tok[:, t, BV + 64 * h:BV + 64 * h + 64])]
                            if t:
                                pairs += [(qdec[r, t - 1, hp, d, :], (S0 if (t == 1) == (d == 0) else S1)[r, hp, d, :]) for d in range(2)]
                            ins = matmuls(p[:, 64 * hp:64 * hp + 64], pairs)
                        fill(ins, job)
                pe.wait_ge(s_rope, l + 1)
                for hp in range(HP):
                    transposes(("aT", l, 0, hp), [tok[:, t, AQ + hp * P:AQ + (hp + 1) * P] for t in range(NT)])
                for hp in range(HP):
                    kc = cachek[:, 0, 2 * hp:2 * hp + 2, :].rearrange("p a b -> p (a b)")
                    kt = [tok[:, t, AK + hp * P:AK + (hp + 1) * P] for t in range(NT)]
                    transposes(("aT", l, 1, hp), [kt[0], kc, kt[1], kt[2]])
                for w in range(2):
                    for hp in range(HP):
                        moved(pe, ("aT", l, w, hp))
                moved(pe, ("cc", l))
                for hp in range(HP):
                    moved(pe, ("cq", l, hp))
                n_clat = 0
                for i in range(len(ATT) + 2):
                    if i < len(ATT):
                        m, t, h = ATT[i]
                        hp, h2 = h // 2, h % 2
                        keys = slice(P, 4 * P) if t else slice(0, P)
                        nk = T if t else P
                        for mp in range(2 if m == "A" else 1):
                            job = ("sc", l, i, mp)
                            p = begin(pe, job)
                            if m == "A":
                                r = slice(64 * h2 + 32 * mp, 64 * h2 + 32 * mp + 32)
                                q, k = aqT, akT
                            else:
                                r = slice(64 * h2, 64 * h2 + 64)
                                q, k = cqT, ckT
                            kw = {"tile_position": (r.start, 0)} if m == "A" else {}
                            fill(pe.matmul(p[:, 0:nk], q[r, hp, t * P:(t + 1) * P], k[r, hp, keys], start=True, stop=True, **kw), job)
                    if 0 <= i - 1 < len(ATT):
                        m, t, h = ATT[i - 1]
                        pe.wait_ge(s_w, l * len(ATT) + i)
                        src = wmix[:, (i - 1) % 2, :] if m == "A" else prob[:, (i - 1) % 2, 0, :]
                        transposes(("pT", l, i - 1), [src[:, n * P:(n + 1) * P] for n in range(3 if t else 1)])
                    if i >= 2:
                        m, t, h = ATT[i - 2]
                        c0 = AV if m == "A" else CV
                        job = ("ao", l, i - 2)
                        p = begin(pe, job)
                        moved(pe, ("pT", l, i - 2))
                        w_ = wT[:, (i - 2) % 2, :]
                        vt = [tok[:, tt, c0 + 64 * h:c0 + 64 * h + 64] for tt in range(NT)]
                        v = [cachek[:, 1 if m == "A" else 3, h, :], vt[1], vt[2]] if t else [vt[0]]
                        fill(matmuls(p[:, 0:64], [(w_[:, n * P:(n + 1) * P], v[n]) for n in range(len(v))]), job)
                pe.wait_ge(s_post, l + 1)
                for i in range(len(ATT)):
                    if i >= len(ATT) - BANKS:
                        moved(pe, ("ao", l, i))
                for c in range(6):
                    src = (oA, oB, oC)[c // 2].rearrange("p (t h) c -> p t (h c)", t=NT)
                    transposes(("mT", l, c), [src[:, t, (c % 2) * P:(c % 2 + 1) * P] for t in range(NT)])
                for c in range(6):
                    moved(pe, ("mT", l, c))
                for c in range(2):
                    moved(pe, ("dy", l, c))
                for b in range(2):
                    w = slot(l, "wout", b)
                    for t in range(NT):
                        by_token(l, w, ("wo", l, b, t), t, 0, 512)
                for j in ADA_GATE2:
                    gate_row(l, j)
                gate_spread(l, ADA_GATE2)
                hidden(2 * l + 1)
                job = ("rt", l)
                p = begin(pe, job)
                for t in range(NT):
                    ins = matmuls(p[:, t * NE:(t + 1) * NE], [(hT[:, k, t * P:(t + 1) * P], wrt[:, k, :]) for k in range(KC)])
                fill(ins, job)
                n0 = l * PER_LAYER + len(PRE)
                with pe.Fori(0, NBODY) as i:
                    for e in range(EXP_PER_BODY):
                        def block_of(q):
                            n = n0 + 3 * e + q
                            pe.wait_ge(landed[n % SLOTS], i * (16 * 3 * EXP_PER_BODY // SLOTS) + 16 * (n // SLOTS + 1))
                            return ring[:, n % SLOTS, :].rearrange("p (k n) -> p k n", k=(KC, KC, FC)[q])

                        def project(w, name, f):
                            job = (name, l, e, f)
                            p = begin(pe, job, i)
                            fill(matmuls(p[:, 0:T], [(w[:, k, f * P:(f + 1) * P], hT[:, k, :]) for k in range(KC)]), job, i)

                        wg = block_of(0)
                        project(wg, "a", 0)
                        wu = block_of(1)
                        project(wu, "u", 0)
                        for f in range(1, FC):
                            project(wg, "a", f)
                            project(wu, "u", f)
                        wd = block_of(2)
                        for f in range(FC):
                            moved(pe, ("u", l, e, f), i)
                        for b in range(2):
                            for t in range(NT):
                                job = ("dn", l, e, b, t)
                                p = begin(pe, job, i)
                                fill(matmuls(p, [(zT[:, e % 2, f, t * P:(t + 1) * P], wd[:, f, b * 512:(b + 1) * 512]) for f in range(FC)]), job, i)


def constants():
    def dft(n):
        ang = 2 * np.pi * (np.outer(np.arange(n), np.arange(n)) % n) / n
        return np.cos(ang), np.sin(ang)

    parts = [np.eye(P)]
    c, s = dft(P)
    parts.append(np.concatenate([c, s], 1) / math.sqrt(P))
    c, s = dft(2 * P)
    parts.append((np.concatenate([c, s], 1) / math.sqrt(2 * P)).reshape(2, P, 512).transpose(1, 0, 2))
    c, s = dft(64)
    parts += [np.kron(np.eye(2), c) / 8.0, -np.kron(np.eye(2), s) / 8.0]
    freq = (np.float32(10000.0) ** (-np.arange(8, dtype=np.float32) / np.float32(8))).astype(np.float32)
    pos = np.arange(2 * P)
    ang = np.concatenate([(pos // GRID_W).astype(np.float32)[:, None] * freq, (pos % GRID_W).astype(np.float32)[:, None] * freq], -1)
    cos, sin = np.cos(ang.astype(np.float64)), np.sin(ang.astype(np.float64))
    parts.append(np.repeat(cos, 2, -1).reshape(2, P, 32).transpose(1, 0, 2))
    parts.append(sin.reshape(2, P, 16).transpose(1, 0, 2))
    qc = np.arange(P) % GRID_W
    start = np.clip(qc - 8, 0, GRID_W - 16)
    kc = np.arange(GRID_W)
    parts.append(np.where((kc[None] >= start[:, None]) & (kc[None] < start[:, None] + 16), 0.0, -1e30))
    parts.append(np.ones((P, P)))
    sel = np.zeros((P, 2, P))
    sel[0, 0], sel[1, 1] = 1.0, 1.0
    parts.append(sel)
    parts.append(np.tile(np.array([4.0, 3.0, 2.0, 1.0]), (P, 1)))
    return np.concatenate([p.reshape(P, -1) for p in parts], 1).astype(np.float32)


def level_masks():
    s, t = np.arange(P)[:, None], np.arange(P)[None]
    out = []
    for m in LEVELS:
        same = s // (2 * m) == t // (2 * m)
        out.append(same & (s // m % 2 == 0) & (t // m % 2 == 1))
        out.append(same & (s // m % 2 == 1) & (t // m % 2 == 0))
    out.append(s == t)
    return np.stack(out, 1).reshape(P, -1)


def kernel(**inputs):
    import ml_dtypes
    import concourse.bacc as bacc
    from concourse.bass_utils import run_bass_kernel_spmd

    a = {k: np.ascontiguousarray(v) for k, v in inputs.items()}

    def cols(v):
        v = v.reshape(v.shape[0], -1, P)
        return v.transpose(2, 0, 1).reshape(P, -1)

    cc = np.stack([a["c_ctx"].reshape(KC, P), a["c"][0].reshape(KC, P)], -1)
    params = np.concatenate([cols(a["norm1_g"]), cols(a["norm2_g"]), cols(a["ada_b"]),
                             cols(a["hgrn_lb_logits"].reshape(L, -1)), cc.transpose(1, 0, 2).reshape(P, -1)], 1)
    pad = np.zeros((L * H * RPB_H, RPER), np.float32)
    pad[:, GRID_W - RPB_W // 2 - 1:GRID_W - RPB_W // 2 - 1 + RPB_W] = a["na_rpb"].reshape(-1, RPB_W)
    direct = ["x_prompt", "x_sample", "cache_diff_k", "cache_diff_v", "cache_na_k", "cache_na_v", "state_hgrn", "ada_w",
              "ada_b", "w_in", "w_out", "diff_lambda", "diff_subln_g", "hgrn_norm_g", "router_w", "router_b",
              "moe_w_gate", "moe_w_up", "moe_w_down", "final_norm_g"]
    arrays = {n: a[n] for n in direct}
    arrays["params"] = np.ascontiguousarray(params)
    arrays["rpb_pad"] = pad
    arrays["consts"] = constants()
    arrays["masks"] = level_masks().astype(ml_dtypes.bfloat16)

    nc = bacc.Bacc("TRN2", target_bir_lowering=False, num_devices=1)
    args = {n: nc.dram_tensor(n, v.shape, mybir.dt.from_np(v.dtype), kind="ExternalInput").ap() for n, v in arrays.items()}
    shapes = {"y_prompt": (1, P, D), "y_sample": (1, 2 * P, D), "new_diff_k": (1, L, H, P, 64), "new_diff_v": (1, L, H, P, 64),
              "new_na_k": (1, L, H, P, 64), "new_na_v": (1, L, H, P, 64), "new_state": (1, L, 2, H, 64, 64)}
    outs = [nc.dram_tensor(n, s, F32, kind="ExternalOutput").ap() for n, s in shapes.items()]
    hybrid_step(nc, outs=outs, **args)
    r = run_bass_kernel_spmd(nc, [arrays], core_ids=[0])
    return tuple(r.results[0][n] for n in shapes)
```

```python
import math
from contextlib import ExitStack

import numpy as np

import concourse.bass as bass
from concourse import mybir

F32 = mybir.dt.float32
U32 = mybir.dt.uint32
ALU = mybir.AluOpType
ACT = mybir.ActivationFunctionType
AX = mybir.AxisListType.X

P = 128
D = 1024
KC = D // P
L = 2
NT = 3
T = NT * P
H = 4
HP = 2
GRID_W = 64
EPS = 1e-6
NE = 16
FE = 512
FC = FE // P
BANKS = 8
SLOTS = 4
BLK = 4096
LEVELS = [64, 32, 16, 8, 4, 2, 1]
NLEV = len(LEVELS)
GRAM = 2 * NLEV + 1
DCOLS = 2 * NLEV * P + 4 * P + 2
TINY = 2.0 ** -60
RPB_H, RPB_W = 15, 31
RPER = 2 * GRID_W - 1
ADA_FIRST = [0, 1, 2, 3]
ADA_REST = list(range(4, 12))
WIN_ORDER = [1, 2, 3, 0, 4, 5]
EXP_PER_BODY = 4
CAP = P
MAXOV = 5
NOWHERE = 1 << 20
EJOBS = ["xt0", "xt1", "zt", "a", "dn0", "dn1", "u"]
NBODY = NE // EXP_PER_BODY
BETWEEN = [[(l, j) for j in ADA_REST] + [(l + 1, j) for j in ADA_FIRST if l + 1 < L] for l in range(L)]
PRE = [[("ada", 0, j) for j in ADA_FIRST if l == 0] + [("win", l, j) for j in WIN_ORDER]
       + [("ada", m, j) for m, j in BETWEEN[l]] + [("wout", l, j) for j in range(2)] for l in range(L)]
FIRST_BLOCK = [sum(len(PRE[m]) + 3 * NE for m in range(l)) for l in range(L)]
BLOCK_NO = {blk: FIRST_BLOCK[l] + n for l in range(L) for n, blk in enumerate(PRE[l])}
assert all(len(p) % SLOTS == 0 for p in PRE) and 3 * NE % SLOTS == 0 and 3 * EXP_PER_BODY % SLOTS == 0
UNITS = [(t, hp) for t in range(NT) for hp in range(HP)]
ATT = ([("A", 0, h) for h in range(H)] + [("C", 0, h) for h in range(H)]
       + [(m, t, h) for t in (1, 2) for m in "AC" for h in range(H)])
AQ, AK, AV, BV, BG, CV, DU = 0, 256, 512, 768, 1024, 1280, 1536
PTOK = 1792


def pipelined(blocks):
    jobs = []
    for n, (l, j) in enumerate(blocks):
        jobs += [("row", l, j)] + ([("mod", *blocks[n - 1])] if n else [])
    return jobs + [("mod", *blocks[-1])]


def layer_jobs(l):
    jobs = pipelined([(0, j) for j in ADA_FIRST]) if l == 0 else []
    jobs += [("hT", 2 * l, k) for k in range(KC)]
    jobs += [("bq", l, 0), ("bq", l, 1)] + [("av", l, t) for t in range(NT)]
    jobs += [("z", l, d, hp) for d in range(2) for hp in range(HP)]
    jobs += [("bvg", l, t) for t in range(NT)] + [("aqk", l, t) for t in range(NT)]
    jobs += [("cq", l, hp) for hp in range(HP)] + [("ck", l, hp) for hp in range(HP)]
    jobs += [("cvdu", l, t) for t in range(NT)]
    jobs += [("du", l, c, w) for c in range(2) for w in range(2)] + [("dy", l, c) for c in range(2)]
    jobs += [("cc", l), ("nk", l)]
    for u in range(len(UNITS)):
        for h2 in range(2):
            jobs += [("kd", l, u)] if h2 == 0 else []
            jobs += [("gram", l, u, h2, g) for g in range(4)] + ([("kv", l, u)] if h2 == 0 else [])
            n = 2 * u + h2
            jobs += [("row", *BETWEEN[l][n])] if n < len(BETWEEN[l]) else []
            jobs += [("mod", *BETWEEN[l][n - 1])] if 0 <= n - 1 < len(BETWEEN[l]) else []
    jobs += [("mod", *BETWEEN[l][-1])] if len(BETWEEN[l]) == 2 * len(UNITS) else []
    jobs += [("bo", l, t, h2) for t in range(NT) for h2 in range(2)]
    jobs += [("aT", l, w, hp) for w in range(2) for hp in range(HP)]
    for i in range(len(ATT) + 2):
        if i < len(ATT):
            jobs += [("sc", l, i, m) for m in range(2 if ATT[i][0] == "A" else 1)]
        if 0 <= i - 1 < len(ATT):
            jobs += [("pT", l, i - 1)]
        if i >= 2:
            jobs += [("ao", l, i - 2)]
    jobs += [("mT", l, c) for c in range(6)] + [("gbc", l, 0, s, b) for s in range(2) for b in range(2)]
    jobs += [("wo", l, b, t) for b in range(2) for t in range(NT)]
    jobs += [("gbc", l, 1, s, b) for s in range(2) for b in range(2)]
    jobs += [("hT", 2 * l + 1, k) for k in range(KC)] + [("hb", l, t, b) for t in range(NT) for b in range(2)]
    jobs += [("rt", l), ("pos", l)]
    return jobs


def place_jobs():
    place, n, uses = {}, 0, [0] * BANKS
    for l in range(L):
        for job in layer_jobs(l):
            b = n % BANKS
            uses[b] += 1
            place[job] = (b, uses[b])
            n += 1
        for b, kind in enumerate(EJOBS):
            place[(kind, l)] = (b, uses[b] + 1)
            uses[b] += NE
    return place


def hybrid_step(nc, x_prompt, x_sample, cache_diff_k, cache_diff_v, cache_na_k, cache_na_v, state_hgrn, ada_w, ada_b,
                w_in, w_out, diff_lambda, diff_subln_g, hgrn_norm_g, router_w, router_b, moe_w_gate, moe_w_up,
                moe_w_down, final_norm_g, params, rpb_pad, consts, masks, slots0, outs):
    y_prompt, y_sample, new_diff_k, new_diff_v, new_na_k, new_na_v, new_state = outs
    place = place_jobs()

    with ExitStack() as ctx:
        def sb(name, shape, dt=F32):
            return ctx.enter_context(nc.sbuf_tensor(name, shape, dt))

        def sem(name):
            return ctx.enter_context(nc.semaphore(name))

        ring = sb("ring", [P, SLOTS, BLK])
        x = sb("x", [P, NT, D])
        hT = sb("hT", [P, KC, T])
        gate = sb("gate", [P, 2, D])
        big = sb("big", [P, 7168])
        dbuf = sb("dbuf", [P, 2 * DCOLS])
        bbuf = sb("bbuf", [P, 3852])
        mprod = sb("mprod", [P, 8, P])
        attT = sb("attT", [P, len(UNITS) * 2, P])
        qdec = sb("qdec", [P, 2, HP, 2, P])
        kdT = sb("kdT", [P, 2, 2, P])
        bias = sb("bias", [P, H, 2, 4, GRID_W])
        cachek = sb("cachek", [P, 4, H, 64])
        S0 = sb("S0", [P, HP, 2, 64])
        S1 = sb("S1", [P, HP, 2, 64])
        mk = sb("mk", [P, GRAM, P], mybir.dt.bfloat16)
        const = sb("const", [P, consts.shape[1]])
        par = sb("par", [P, params.shape[1]])
        wrt = sb("wrt", [P, KC, NE])
        rbias = sb("rbias", [P, NE])
        gsub = sb("gsub", [P, 2, L, 64])
        modv = sb("modv", [P, L, 6 * KC, 2])
        scp = sb("scp", [P, KC, 32])
        lst = sb("lst", [P, NE, 4], U32)
        lsto = sb("lsto", [P, 4], U32)
        pay = sb("pay", [P, NT, 2, 4], U32)
        slotu = sb("slotu", [P, NT, 2], U32)
        ovt = sb("ovt", [1, 1 + 2 * MAXOV], mybir.dt.int32)
        rtmp = sb("rtmp", [P, 512])
        small = sb("small", [P, 320])
        ps = ctx.enter_context(nc.psum_tensor("ps", [P, BANKS, 512], F32))

        def carve(buf, at, *shape):
            names = "abcde"[:len(shape)]
            v = buf[:, at:at + int(np.prod(shape))]
            if len(shape) == 1:
                return v
            return v.rearrange(f"p ({' '.join(names)}) -> p {' '.join(names)}", **dict(zip(names, shape)))

        def strided(v, offset, *dims):
            return bass.AP(v.tensor, v.offset + offset, [list(v.ap[0])] + [list(d) for d in dims])

        tok = carve(big, 0, NT, PTOK)
        cqT = carve(big, NT * PTOK, HP, T)
        ckT = carve(big, NT * PTOK + HP * T, HP, 4 * P)
        xn = carve(big, 0, NT, D)
        htok = carve(big, 0, NT, D)
        ybuf = carve(big, NT * D, 2, D)
        sS = carve(big, NT * D + 2 * D, FE)
        zb = carve(big, NT * D + 2 * D + FE, FE)
        yr = carve(big, 0, NT, 2, D)
        junk = carve(big, NT * D, D)
        qT = carve(bbuf, 0, HP, T)
        kT = carve(bbuf, HP * T, 2, HP, T)
        C2 = carve(bbuf, 3 * HP * T, HP, NT, 258)
        aqT = carve(bbuf, 0, HP, T)
        akT = carve(bbuf, HP * T, HP, 4 * P)
        oA = carve(bbuf, HP * T + HP * 4 * P, NT * H, 64)
        oC = carve(bbuf, HP * T + HP * 4 * P + NT * H * 64, NT * H, 64)
        Z = carve(dbuf, 0, 2, HP, T)
        E = carve(dbuf, 2 * HP * T, 2, HP, T)
        F = carve(dbuf, 4 * HP * T, 2, HP, T)
        dec = [dbuf[:, u * DCOLS:(u + 1) * DCOLS] for u in range(2)]
        prob = carve(dbuf, 0, 2, 2, T)
        wmix = carve(dbuf, 4 * T, 2, T)
        scb = carve(dbuf, 6 * T, 2, T)
        wT = carve(dbuf, 8 * T, 2, T)
        oB = carve(dbuf, 10 * T, NT * H, 64)
        post = carve(dbuf, 0, 2, NT * H, 64)
        pz = carve(dbuf, 2 * NT * H * 64, NT, 256)
        xg = carve(dbuf, 0, 2, D)
        hTg = carve(dbuf, 2 * D, KC, P)
        zTg = carve(dbuf, 2 * D + KC * P, FC, P)
        mflat = mprod[:, :, :].rearrange("p a b -> p (a b)")
        diag = carve(mflat, 0, 2, 4, P)
        rows = gate[:, 0, :].rearrange("p (b n) -> p b n", b=2)
        lamt = carve(mflat, 0, L, 4, 32)
        Ud = carve(attT[:, :, :].rearrange("p a b -> p (a b)"), 0, 2, 768)
        nkout = carve(rtmp, 0, H, 64)
        stout = carve(rtmp, 256, HP, 2, 64)

        o = [0]

        def cst(*shape):
            v = carve(const, o[0], *shape)
            o[0] += int(np.prod(shape))
            return v

        ident = cst(P)
        dftc = cst(2 * P)
        dftl = cst(2, 512)
        chc, chs = cst(P), cst(P)
        ropec, ropes = cst(2, 32), cst(2, 16)
        namask = cst(GRID_W)
        ones = cst(P)
        fold = cst(2)
        rank = cst(4)
        tri = cst(P)
        eidx, erow, ridx = cst(NE), cst(NE), cst(MAXOV)
        assert o[0] == consts.shape[1]
        par_g1, par_g2 = carve(par, 0, L, KC), carve(par, L * KC, L, KC)
        par_ab = carve(par, 2 * L * KC, L, 48)
        par_lb = carve(par, 2 * L * KC + 48 * L, L, 4)
        par_c = carve(par, 2 * L * KC + 52 * L, KC, 2)
        npar = 2 * L * KC + 52 * L + 2 * KC
        assert npar == params.shape[1]

        o[0] = 0

        def tmp(*shape):
            v = carve(small, o[0], *shape)
            o[0] += int(np.prod(shape))
            return v

        ss, ms, lnv, rs, nt1, nt2 = (tmp(24) for _ in range(6))
        lbt, omlb = tmp(L, 4), tmp(L, 4)
        lam = tmp(L)
        A1 = tmp(2, KC, 2)
        sums = tmp(2, 2)
        mx, nmx = tmp(2, 2), tmp(2, 2)
        rsum = tmp(4, 2)
        rneg = tmp(2, 1)
        gdec = tmp(6, 2)
        e1 = tmp(KC, 2)
        lbe = tmp(L, 4)
        lbm = tmp(4)
        lm2 = tmp(L, 2)
        lme = tmp(L, 2)
        rtr_at = [0]

        def rtr(*shape):
            v = carve(attT[:, :, :].rearrange("p a b -> p (a b)"), rtr_at[0], *shape)
            rtr_at[0] += int(np.prod(shape))
            return v

        logit, score, selv = rtr(NT, NE), rtr(NT, NE), rtr(NT, NE)
        eqv, oh1, oh2, rest, slotc = (rtr(NT * 4, 4) for _ in range(5))
        slotf = rtr(NT, 2)
        posn, selm = rtr(NT, NE), rtr(NT, NE)
        cnt, novv, pin, pexc, ex2 = (rtr(NE) for _ in range(5))
        mat, mat2 = rtr(MAXOV, NE), rtr(MAXOV, NE)
        oeid, orow = rtr(MAXOV), rtr(MAXOV)
        m1, m2, gsc, gsel = (rtr(NT * 4) for _ in range(4))
        gm = rtr(NT)
        den = rtr(NT)
        gates = rtr(NT, NE)

        full = [sem(f"bank{b}_filled") for b in range(BANKS)]
        free = [sem(f"bank{b}_read_out") for b in range(BANKS)]
        landed = [sem(f"slot{s}_landed") for s in range(SLOTS)]
        d_x, d_const, d_par, d_row, d_out = (sem(n) for n in ("x_landed", "consts_landed", "params_landed", "rows_landed", "outputs_stored"))
        d_st, d_y = sem("scan_states_stored"), sem("y_stored")
        d_skew = sem("skew_rows_written")
        d_tab, d_hrow, d_slot, d_lst, d_yr = (sem(n) for n in ("table_cleared", "hidden_rows_stored", "slots_scattered", "slot_lists_landed", "expert_rows_landed"))
        d_g = [sem(f"gathered{i}") for i in range(2)]
        d_sc = [sem(f"expert_rows_stored{i}") for i in range(2)]
        s_sel, s_pay, s_ovt = (sem(n) for n in ("choices_ready", "slots_ready", "overflow_table_ready"))
        sync_passed, pool_passed = sem("sync_passed"), sem("pool_passed")
        ov = [{k: sem(f"ov{l}_{k}") for k in ("weights_landed", "tensor", "vector", "scalar", "list_landed", "gathered", "stored")} for l in range(L)]
        table = nc.dram_tensor("slot_table", (NE * T, 4), U32, kind="Internal").ap()
        hrow = nc.dram_tensor("hidden_rows", (T, D), F32, kind="Internal").ap()
        yrow = nc.dram_tensor("expert_rows", (2 * T, D), F32, kind="Internal").ap()
        skew = nc.dram_tensor("skew_rows", (L * H * RPB_H, GRID_W, RPER), F32, kind="Internal").ap()
        d_cache, d_state, d_bias, d_fin = (sem(n) for n in ("cache_landed", "state_landed", "bias_landed", "final_gain_landed"))
        ch_dve, ch_act, ch_pool = (sem(n) for n in ("vector_step", "scalar_step", "pool_step"))
        s_expc, s_sc, s_lbl, s_lbe = (sem(n) for n in ("exp_c_ready", "silu_c_ready", "init_exponents_ready", "init_exps_ready"))
        s_ss, s_ms, s_ln, s_xn = (sem(n) for n in ("sumsq_ready", "meansq_ready", "rstd_guess_ready", "xnorm_ready"))
        s_mod, s_eq, s_e, s_f, s_lf = (sem(n) for n in ("modulation_ready", "exp_q_ready", "exp_z_ready", "forget_ready", "log_forget_ready"))
        s_q, s_diff, s_dec, s_X, s_att = (sem(n) for n in ("q_ready", "exponents_ready", "decays_ready", "operands_ready", "b_scores_ready"))
        s_rope, s_bias, s_mx, s_pr, s_w = (sem(n) for n in ("rope_done", "bias_masked", "neg_max_ready", "c_latent_probs_ready", "weights_ready"))
        s_pss, s_pln, s_ebg, s_post = (sem(n) for n in ("sub_meansq_ready", "sub_rstd_guess_ready", "exp_bg_ready", "subnorm_ready"))
        s_diag = sem("gate_diagonals_ready")
        s_x, s_rl, s_re, s_gates, s_y = (sem(n) for n in ("residual_done", "logits_ready", "router_exp_ready", "gates_ready", "result_ready"))

        def bank(job, i=0):
            b, nth = place[job]
            return b, nth + i

        def begin(pe, job, i=0):
            b, nth = bank(job, i)
            if place[job][1] > 1:
                pe.wait_ge(free[b], nth - 1)
            return ps[:, b, :]

        def ready(eng, job, i=0):
            b, nth = bank(job, i)
            eng.wait_ge(full[b], nth)
            return ps[:, b, :]

        def moved(eng, job, i=0):
            b, nth = bank(job, i)
            eng.wait_ge(free[b], nth)

        def release(eng, ins, job, i=0):
            b, nth = bank(job, i)
            ins.then_inc(free[b], 1)
            eng.wait_ge(free[b], nth)

        last_job = {}
        for l in range(L):
            for j in ADA_FIRST + ADA_REST:
                last_job[("ada", l, j)] = ("row", l, j)
            for j, job in zip(WIN_ORDER, [("av", l, 2), ("z", l, 1, 1), ("bvg", l, 2), ("aqk", l, 2), ("ck", l, 1), ("cvdu", l, 2)]):
                last_job[("win", l, j)] = job
            for j in range(2):
                last_job[("wout", l, j)] = ("wo", l, j, NT - 1)
        EXPERT_LAST = ["a", "u", "dn1"]

        def exponents(eng, step, l, u):
            t, hp = UNITS[u]
            c2, out = C2[:, hp, t, :], dec[u % 2]
            for n, m in enumerate(LEVELS):
                M, nb = 2 * m, P // (2 * m)
                ref = strided(c2, m, [129, 2], [M, nb], [0, m])
                right, left = (strided(c2, 1 + o_, [P, 2], [M, nb], [1, m]) for o_ in (m, 0))
                step(eng.tensor_tensor(strided(out, n * 2 * P + m, [P, 2], [M, nb], [1, m]), right, ref, ALU.subtract))
                step(eng.tensor_tensor(strided(out, n * 2 * P, [P, 2], [M, nb], [1, m]), ref, left, ALU.subtract))
            at = NLEV * 2 * P
            step(eng.tensor_copy(out[:, at:at + P], c2[:, 1:129]))
            step(eng.tensor_copy(out[:, at + 3 * P:at + 4 * P], c2[:, 129:257]))
            step(eng.tensor_scalar(out[:, at + P:at + 2 * P], c2[:, 129:257], -1.0, c2[:, 257:258], ALU.mult, ALU.add))
            step(eng.tensor_scalar(out[:, at + 2 * P:at + 3 * P], c2[:, 1:129], -1.0, c2[:, 128:129], ALU.mult, ALU.add))
            eng.tensor_copy(out[:, at + 4 * P:at + 4 * P + 2], strided(c2, 128, [129, 2])).then_inc(s_diff, 1)
            eng.wait_ge(s_diff, l * len(UNITS) + u + 1)

        def gate_of(e):
            at = slice(e, e + 1) if isinstance(e, int) else bass.ds(e, 1)
            return lst[:, at, 2].bitcast(F32)

        def stored(eng, l, i, c):
            n = 16 * (NE // 2 * l + c // 2)
            if isinstance(i, int):
                if n + 16 * (EXP_PER_BODY // 2) * i > 0:
                    eng.wait_ge(d_sc[c % 2], n + 16 * (EXP_PER_BODY // 2) * i)
            else:
                eng.wait_ge(d_sc[c % 2], i * (16 * (EXP_PER_BODY // 2)) + n)

        block = ctx.enter_context(nc.Block())

        @block.sync
        def _(sp):
            sp.dma_start(par[:, :], params).then_inc(d_par, 16)
            for l in range(L):
                for i_n, (kind, m, j) in enumerate(PRE[l]):
                    n = FIRST_BLOCK[l] + i_n
                    if i_n >= SLOTS:
                        ready(sp, last_job[PRE[l][i_n - SLOTS]])
                    elif n >= SLOTS:
                        q = 3 * NE - SLOTS + i_n
                        ready(sp, (EXPERT_LAST[q % 3], l - 1), q // 3)
                    if kind == "ada":
                        src = ada_w[m, :, j * 512:(j + 1) * 512]
                    elif kind == "win":
                        src = w_in[l, :, j * 512:(j + 1) * 512]
                    else:
                        src = w_out[l, :, j * 512:(j + 1) * 512]
                    sp.dma_start(ring[:, n % SLOTS, :].rearrange("p (k n) -> p k n", k=KC),
                                 src.rearrange("(k p) n -> p k n", p=P)).then_inc(landed[n % SLOTS], 16)
                gview = moe_w_gate[l].rearrange("e (k p) n -> e p k n", p=P)
                uview = moe_w_up[l].rearrange("e (k p) n -> e p k n", p=P)
                dview = moe_w_down[l].rearrange("e (k p) n -> e p k n", p=P)

                def expert_block(e, i, q, first):
                    slot = (len(PRE[l]) + q) % SLOTS
                    if first and q < SLOTS:
                        ready(sp, last_job[PRE[l][len(PRE[l]) - SLOTS + q]])
                    else:
                        back = q - SLOTS
                        ready(sp, (EXPERT_LAST[back % 3], l), i * EXP_PER_BODY + back // 3)
                        if not first:
                            sp.wait_ge(d_par, 16)
                    src = (gview, uview, dview)[q % 3][e]
                    dst = ring[:, slot, :].rearrange("p (k n) -> p k n", k=(KC, KC, FC)[q % 3])
                    sp.dma_start(dst, src).then_inc(landed[slot], 16)

                for q in range(3 * EXP_PER_BODY):
                    expert_block(q // 3, 0, q, True)
                with sp.Fori(1, NBODY) as i:
                    for q in range(3 * EXP_PER_BODY):
                        expert_block(i * EXP_PER_BODY + q // 3, i, q, False)
                o_ = ov[l]
                ready(sp, ("dn1", l), NE - 1)
                sp.wait_ge(s_ovt, l + 1)
                n_ov = sp.value_load(ovt[0:1, 0:1], min_val=0, max_val=MAXOV)
                with sp.If(n_ov > 0):
                    with sp.Fori(0, n_ov) as r:
                        e = sp.value_load(ovt[0:1, bass.ds(r + 1, 1)], min_val=0, max_val=NE - 1)
                        for q, view in enumerate((gview, uview, dview)):
                            dst = ring[:, q, :].rearrange("p (k n) -> p k n", k=(KC, KC, FC)[q])
                            sp.dma_start(dst, view[e]).then_inc(o_["weights_landed"], 16)
                        sp.wait_ge(o_["tensor"], 4 * r + 4)
                        sp.sem_inc(sync_passed, 1)
            sp.wait_ge(s_y, 1)
            sp.dma_start(y_prompt[0], xn[:, 0, :]).then_inc(d_y, 16)
            sp.dma_start(y_sample[0].rearrange("(t p) d -> p t d", p=P), xn[:, 1:3, :]).then_inc(d_y, 16)
            sp.wait_ge(d_y, 32)
            sp.wait_ge(d_out, 16 * 4 * L)

        @block.gpsimd
        def _(pool):
            n_pool = [0]

            def step(ins):
                n_pool[0] += 1
                ins.then_inc(ch_pool, 1)
                pool.wait_ge(ch_pool, n_pool[0])

            pool.dma_start(const[:, :], consts).then_inc(d_const, 16)
            pool.dma_start(mflat[:, 0:L * 128], diff_lambda.rearrange('l a d -> (l a d)').partition_broadcast(P)).then_inc(d_row, 16)
            pool.dma_start(gsub[:, 0, :, :], diff_subln_g.partition_broadcast(P)).then_inc(d_row, 16)
            pool.dma_start(gsub[:, 1, :, :], hgrn_norm_g.partition_broadcast(P)).then_inc(d_row, 16)
            pool.dma_start(mk[:, :, :], masks.rearrange("p (g n) -> p g n", g=GRAM)).then_inc(d_const, 16)
            pool.dma_start(pay[:, :, :, :], slots0[:, 4 * NE * NT:].rearrange("p (t k w) -> p t k w", t=NT, k=2)).then_inc(d_const, 16)
            pool.dma_start(wrt[:, :, :], router_w.rearrange("(k p) n -> p k n", p=P)).then_inc(d_row, 16)
            pool.dma_start(rbias[:, :], router_b.partition_broadcast(P)).then_inc(d_row, 16)
            pool.dma_start(skew, rpb_pad.unsqueeze(1).broadcast_to([L * H * RPB_H, GRID_W, RPER])).then_inc(d_skew, 16)
            for l in range(L):
                if l:
                    moved(pool, ("ao", l - 1, len(ATT) - 1))
                for n, src in enumerate((cache_diff_k, cache_diff_v, cache_na_k, cache_na_v)):
                    pool.dma_start(cachek[:, n, :, :], src[0, l].rearrange("h p d -> p h d")).then_inc(d_cache, 16)
                for hp in range(HP):
                    for d in range(2):
                        pool.dma_start(S0[:, hp, d, :], state_hgrn[0, l, d, 2 * hp:2 * hp + 2].rearrange("h k v -> (h k) v")).then_inc(d_state, 16)
                if l == 0:
                    pool.wait_ge(d_skew, 16)
                for h in range(H):
                    for qt in range(2):
                        for r2 in range(2):
                            at = ((l * H + h) * RPB_H + 7 - 2 * qt - r2) * GRID_W * RPER + GRID_W - 1
                            src = bass.AP(skew.tensor, skew.offset + at, [[RPER - 1, GRID_W], [GRID_W * RPER, 4], [1, GRID_W]])
                            pool.dma_start(bias[64 * r2:64 * r2 + 64, h, qt, :, :], src).then_inc(d_bias, 16)
                pool.wait_ge(d_const, 48)
                pool.wait_ge(d_bias, 256 * (l + 1))
                bv3 = bias[:, :, :, :, :].rearrange("p h q r c -> p (h q r) c")
                pool.tensor_tensor(bv3, bv3, namask.unsqueeze(1).broadcast_to([P, 32, GRID_W]), ALU.add).then_inc(s_bias, 1)
                for t in range(NT):
                    moved(pool, ("aqk", l, t))
                if l:
                    pool.wait_ge(d_st, 16 * HP * 2 * l)
                    pool.wait_ge(d_out, 16 * 4 * l)
                qk = tok[:, 1:3, 0:512]
                for t in range(2):
                    v = qk[:, t, :].rearrange("p (g r) -> p g r", r=32)
                    pr = qk[:, t, :].rearrange("p (g r two) -> p g r two", r=16, two=2)
                    rr = rtmp[:, :].rearrange("p (g r two) -> p g r two", r=16, two=2)
                    sn = ropes[:, t, :].unsqueeze(1).broadcast_to([P, 16, 16])
                    step(pool.tensor_tensor(rr[:, :, :, 0], pr[:, :, :, 1], sn, ALU.mult))
                    step(pool.tensor_tensor(rr[:, :, :, 1], pr[:, :, :, 0], sn, ALU.mult))
                    step(pool.tensor_tensor(v, v, ropec[:, t, :].unsqueeze(1).broadcast_to([P, 16, 32]), ALU.mult))
                    step(pool.tensor_tensor(pr[:, :, :, 0], pr[:, :, :, 0], rr[:, :, :, 0], ALU.subtract))
                    step(pool.tensor_tensor(pr[:, :, :, 1], pr[:, :, :, 1], rr[:, :, :, 1], ALU.add))
                pool.engine_nop().then_inc(s_rope, 1)
                moved(pool, ("cvdu", l, 0))
                for dst, c0 in ((new_diff_k, AK), (new_diff_v, AV), (new_na_v, CV)):
                    pool.dma_start(dst[0, l].rearrange("h p d -> p h d"),
                                   tok[:, 0, c0:c0 + 256].rearrange("p (h d) -> p h d", h=H)).then_inc(d_out, 16)
                moved(pool, ("nk", l))
                pool.dma_start(new_na_k[0, l].rearrange("h p d -> p h d"), nkout).then_inc(d_out, 16)
                for u in range(2, len(UNITS)):
                    ready(pool, ("gram", l, u - 2, 1, 3))
                    exponents(pool, step, l, u)
                moved(pool, ("kv", l, 0))
                moved(pool, ("kv", l, 1))
                for n in range(HP * 2):
                    hp, d = n // 2, n % 2
                    pool.dma_start(new_state[0, l, d, 2 * hp:2 * hp + 2].rearrange("h k v -> (h k) v"),
                                   stout[:, hp, d, :]).then_inc(d_st, 16)
                pool.dma_start(table.rearrange("(p r) w -> p (r w)", p=P), slots0[:, 0:4 * NE * NT]).then_inc(d_tab, 16)
                pool.wait_ge(d_tab, 16 * (l + 1))
                pool.wait_ge(s_pay, l + 1)
                for t in range(NT):
                    for k in range(2):
                        pool.indirect_dma_start(table, bass.IndirectOffsetOnAxis(slotu[:, t, k:k + 1], 0), pay[:, t, k, :],
                                                None).then_inc(d_slot, 16)
                pool.wait_ge(d_slot, 16 * 2 * NT * (l + 1))
                pool.dma_start(lst[:, :, :], table.rearrange("(e s) w -> s e w", e=NE)[0:CAP]).then_inc(d_lst, 16)
                pool.wait_ge(d_lst, 16 * (l + 1))
                pool.wait_ge(d_hrow, 16 * (l + 1))

                def gather(e):
                    pool.indirect_dma_start(xg[:, e % 2, :], None, hrow, bass.IndirectOffsetOnAxis(lst[:, e, 0:1], 0)).then_inc(d_g[e % 2], 16)

                gather(0)
                gather(1)
                for e in range(NE + 1):
                    if e + 2 < NE:
                        ready(pool, ("xt1", l), e)
                        gather(e + 2)
                    if e:
                        moved(pool, ("dn0", l), e - 1)
                        moved(pool, ("dn1", l), e - 1)
                        pool.indirect_dma_start(yrow, bass.IndirectOffsetOnAxis(lst[:, e - 1, 1:2], 0), ybuf[:, (e - 1) % 2, :], None,
                                                bounds_check=2 * T - 1, oob_is_err=False).then_inc(d_sc[(e - 1) % 2], 16)
                o_ = ov[l]
                pool.wait_ge(s_ovt, l + 1)
                n_ov = pool.value_load(ovt[0:1, 0:1], min_val=0, max_val=MAXOV)
                with pool.If(n_ov > 0):
                    for b in range(2):
                        pool.wait_ge(d_sc[b], 16 * (NE // 2) * (l + 1))
                    with pool.Fori(0, n_ov) as r:
                        row = pool.value_load(ovt[0:1, bass.ds(r + (1 + MAXOV), 1)], min_val=0, max_val=(NE - 1) * T + 2 * CAP)
                        pool.dma_start(lsto[:, :], table[bass.ds(row, CAP)]).then_inc(o_["list_landed"], 16)
                        pool.wait_ge(o_["list_landed"], 16 * r + 16)
                        pool.sem_inc(pool_passed, 1)
                        pool.indirect_dma_start(xg[:, 0, :], None, hrow, bass.IndirectOffsetOnAxis(lsto[:, 0:1], 0)).then_inc(o_["gathered"], 16)
                        pool.wait_ge(o_["vector"], 4 * r + 4)
                        pool.sem_inc(pool_passed, 1)
                        pool.indirect_dma_start(yrow, bass.IndirectOffsetOnAxis(lsto[:, 1:2], 0), ybuf[:, 0, :], None,
                                                bounds_check=2 * T - 1, oob_is_err=False).then_inc(o_["stored"], 16)
                        pool.wait_ge(o_["stored"], 16 * r + 16)
                        pool.sem_inc(pool_passed, 1)
                for b in range(2):
                    pool.wait_ge(d_sc[b], 16 * (NE // 2) * (l + 1))
                for t in range(NT):
                    pool.dma_start(yr[:, t, :, :], yrow[2 * t * P:2 * (t + 1) * P].rearrange("(p k) d -> p k d", k=2)).then_inc(d_yr, 16)
            pool.wait_ge(s_x, 2 * L)
            pool.dma_start(gate[:, 0, :], final_norm_g.partition_broadcast(P)).then_inc(d_fin, 16)
            pool.wait_ge(d_st, 16 * HP * 2 * L)

        @block.scalar
        def _(act):
            n_act = [0]

            def step(ins):
                n_act[0] += 1
                ins.then_inc(ch_act, 1)
                act.wait_ge(ch_act, n_act[0])

            def rstd_guess(cols, s_in, n_in, s_done):
                act.wait_ge(s_in, n_in)
                step(act.activation(lnv[:, 0:cols], ms[:, 0:cols], ACT.Ln))
                act.activation(rs[:, 0:cols], lnv[:, 0:cols], ACT.Exp, scale=-0.5).then_inc(s_done, 1)

            def sum_squares(n):
                if n:
                    act.wait_ge(s_x, n)
                else:
                    act.wait_ge(d_x, 32)
                for t in range(NT):
                    ins = act.activation(junk, x[:, t, :], ACT.Square, accum_out=ss[:, t:t + 1])
                    if t < NT - 1:
                        step(ins)
                    else:
                        ins.then_inc(s_ss, 1)
                rstd_guess(NT, s_ms, n + 1, s_ln)

            def gate_copy(l, which):
                for s in range(2):
                    for b in range(2):
                        p = ready(act, ("gbc", l, which, s, b))
                        release(act, act.activation(gate[:, s, b * 512:(b + 1) * 512], p, ACT.Copy), ("gbc", l, which, s, b))

            def row_copy(blocks, n):
                if n >= 2:
                    ready(act, ("mod", *blocks[n - 2]))
                copy_out(rows[:, n % 2, :], ("row", *blocks[n]), 512)

            def modulate(l, which):
                act.wait_ge(s_mod, 2 * l + which + 1)
                for k in range(1, KC, 2):
                    job = ("hT", 2 * l + which, k)
                    p = ready(act, job)
                    for s, (a, b) in enumerate(((0, P), (P, T))):
                        ins = act.activation(hT[:, k, a:b], p[:, a:b], ACT.Identity, scale=A1[:, which, k, s:s + 1],
                                             bias=modv[:, l, 3 * KC * which + k, s:s + 1])
                        if s == 0:
                            step(ins)
                    release(act, ins, job)

            def copy_out(dst, job, cols=None, src=None):
                p = ready(act, job)
                release(act, act.activation(dst, p[:, 0:cols] if src is None else src(p), ACT.Copy), job)

            act.dma_start(x[:, 0, :], x_prompt[0]).then_inc(d_x, 16)
            act.dma_start(x[:, 1:3, :], x_sample[0].rearrange("(t p) d -> p t d", p=P)).then_inc(d_x, 16)
            act.wait_ge(d_par, 16)
            act.activation(e1, par_c, ACT.Exp, scale=-1.0).then_inc(s_expc, 1)
            act.wait_ge(s_lbl, 1)
            act.activation(lbe, lbe, ACT.Exp).then_inc(s_lbe, 1)
            act.activation(lme, lm2, ACT.Exp).then_inc(s_lbe, 1)
            c_lat = 0
            for l in range(L):
                sum_squares(2 * l)
                if l == 0:
                    for n in range(len(ADA_FIRST)):
                        row_copy([(0, j) for j in ADA_FIRST], n)
                modulate(l, 0)
                for hp in range(HP):
                    p = ready(act, ("bq", l, hp))
                    act.activation(E[:, 0, hp, :], p[:, 0:T], ACT.Exp, scale=-1.0).then_inc(s_eq, 1)
                for t in range(NT):
                    copy_out(tok[:, t, AV:AV + 256], ("av", l, t), 256)
                for d in range(2):
                    for hp in range(HP):
                        moved(act, ("z", l, d, hp))
                act.activation(E, Z, ACT.Exp, scale=-1.0).then_inc(s_e, 1)
                for t in range(NT):
                    copy_out(tok[:, t, BV:BV + 512], ("bvg", l, t), 512)
                act.wait_ge(s_f, l + 1)
                act.activation(F, F, ACT.Ln).then_inc(s_lf, 1)

                def decays(u):
                    act.wait_ge(s_diff, l * len(UNITS) + u + 1)
                    act.activation(dec[u % 2], dec[u % 2], ACT.Exp).then_inc(s_dec, 1)

                for t in range(NT):
                    copy_out(tok[:, t, 0:512], ("aqk", l, t), 512)
                decays(0)
                for hp in range(HP):
                    copy_out(cqT[:, hp, :], ("cq", l, hp), T)
                for hp in range(HP):
                    p = ready(act, ("ck", l, hp))
                    step(act.activation(ckT[:, hp, 0:P], p[:, 0:P], ACT.Copy))
                    release(act, act.activation(ckT[:, hp, 2 * P:4 * P], p[:, P:T], ACT.Copy), ("ck", l, hp))
                decays(1)
                for t in range(NT):
                    copy_out(tok[:, t, CV:CV + 512], ("cvdu", l, t), 512)
                for c in range(2):
                    copy_out(Ud[:, c, 0:256], ("du", l, c, 0), 256)
                    copy_out(Ud[:, c, 256:768], ("du", l, c, 1), 512)
                for c in range(2):
                    copy_out(hT[:, 6 + c, :], ("dy", l, c), T)
                copy_out(ckT[:, :, P:2 * P], ("cc", l), src=lambda p: p[:, 0:256].rearrange("p (a b) -> p a b", a=HP))
                act.wait_ge(s_rope, l + 1)
                copy_out(rtmp[:, 0:256], ("nk", l), 256)
                for u, (t, hp) in enumerate(UNITS):
                    nd = 2 if t == 0 else 1
                    copy_out(kdT[:, u % 2, 0:nd, :].rearrange("p a b -> p (a b)"), ("kd", l, u), nd * P)
                    for n in (2 * u, 2 * u + 1):
                        if n < len(BETWEEN[l]):
                            row_copy(BETWEEN[l], n)
                    if u + 2 < len(UNITS):
                        decays(u + 2)
                for t in range(NT):
                    for h2 in range(2):
                        copy_out(oB[:, t * H + h2:(t + 1) * H:2, :], ("bo", l, t, h2),
                                 src=lambda p: p[:, 0:P].rearrange("p (a b) -> p a b", a=HP))
                for hp in range(HP):
                    copy_out(aqT[:, hp, :], ("aT", l, 0, hp), T)
                for hp in range(HP):
                    copy_out(akT[:, hp, :], ("aT", l, 1, hp), 4 * P)
                for i in range(len(ATT) + 2):
                    if i < len(ATT):
                        m, t, h = ATT[i]
                        nk = T if t else P
                        act.wait_ge(s_mx, l * len(ATT) + i + 1)
                        if m == "C" and t:
                            act.activation(prob[:, i % 2, 0, 0:nk], scb[:, i % 2, 0:nk], ACT.Exp, bias=nmx[:, i % 2, 0:1],
                                           accum_out=sums[:, i % 2, 0:1]).then_inc(s_pr, 1)
                        else:
                            scale = 32 ** -0.5 if m == "A" else 64 ** -0.5
                            for mp in range(2 if m == "A" else 1):
                                p = ready(act, ("sc", l, i, mp))
                                release(act, act.activation(prob[:, i % 2, mp, 0:nk], p[:, 0:nk], ACT.Exp, scale=scale,
                                                            bias=nmx[:, i % 2, mp:mp + 1],
                                                            accum_out=sums[:, i % 2, mp:mp + 1]), ("sc", l, i, mp))
                    if 0 <= i - 1 < len(ATT):
                        nk = T if ATT[i - 1][1] else P
                        copy_out(wT[:, (i - 1) % 2, 0:nk], ("pT", l, i - 1), nk)
                    if i >= 2:
                        m, t, h = ATT[i - 2]
                        p = ready(act, ("ao", l, i - 2))
                        act.wait_ge(s_w, l * len(ATT) + i - 1)
                        dst = (oA if m == "A" else oC)[:, t * H + h, :]
                        release(act, act.activation(dst, p[:, 0:64], ACT.Copy, scale=rsum[:, (i - 2) % 4, 0:1]), ("ao", l, i - 2))
                act.activation(pz, tok[:, :, BG:BG + 256], ACT.Exp, scale=-1.0).then_inc(s_ebg, 1)
                rstd_guess(24, s_pss, l + 1, s_pln)
                for c in range(1, 6, 2):
                    copy_out(hT[:, c, :], ("mT", l, c), T)
                ready(act, ("mod", *BETWEEN[l][-1]))
                gate_copy(l, 0)
                act.wait_ge(d_out, 16 * 4 * (l + 1))
                sum_squares(2 * l + 1)
                gate_copy(l, 1)
                modulate(l, 1)
                for t in range(NT):
                    copy_out(htok[:, t, 512:], ("hb", l, t, 1))
                for t in range(NT):
                    moved(act, ("hb", l, t, 0))
                act.dma_start(hrow.rearrange("(t p) d -> p t d", p=P), htok).then_inc(d_hrow, 16)
                act.wait_ge(s_rl, l + 1)
                act.activation(score, logit, ACT.Exp, scale=-1.0).then_inc(s_re, 1)
                act.wait_ge(d_lst, 16 * (l + 1))

                def copy(dst, job, e):
                    p = ready(act, job, e)
                    release(act, act.activation(dst, p, ACT.Copy), job, e)

                def expert(i, es, first=False, last=False):
                    e = i * EXP_PER_BODY + es
                    if not last:
                        copy(hTg[:, 4:8, :].rearrange("p a b -> p (a b)"), ("xt1", l), e)
                    if not first:
                        copy(zTg.rearrange("p a b -> p (a b)"), ("zt", l), e - 1)
                    if not last:
                        p = ready(act, ("a", l), e)
                        release(act, act.activation(sS, p, ACT.Silu), ("a", l), e)
                    if not first:
                        p = ready(act, ("dn0", l), e - 1)
                        stored(act, l, i, es - 1)
                        release(act, act.activation(ybuf[:, (es - 1) % 2, 0:512], p, ACT.Copy, scale=gate_of(e - 1)), ("dn0", l), e - 1)

                for e in range(EXP_PER_BODY):
                    expert(0, e, first=(e == 0))
                with act.Fori(1, NBODY) as i:
                    for e in range(EXP_PER_BODY):
                        expert(i, e)
                expert(NBODY, 0, last=True)
                o_ = ov[l]
                act.wait_ge(s_ovt, l + 1)
                n_ov = act.value_load(ovt[0:1, 0:1], min_val=0, max_val=MAXOV)
                with act.If(n_ov > 0):
                    with act.Fori(0, n_ov) as r:
                        act.wait_ge(o_["tensor"], 4 * r + 2)
                        act.activation(sS, ps[:, 2, :], ACT.Silu).then_inc(o_["scalar"], 1)
            sum_squares(2 * L)

        @block.vector
        def _(dve):
            n_dve = [0]

            def step(ins):
                n_dve[0] += 1
                ins.then_inc(ch_dve, 1)
                dve.wait_ge(ch_dve, n_dve[0])

            def newton(cols):
                a, r = nt1[:, 0:cols], rs[:, 0:cols]
                step(dve.tensor_tensor(a, r, r, ALU.mult))
                step(dve.tensor_tensor(a, a, ms[:, 0:cols], ALU.mult))
                step(dve.tensor_scalar(a, a, -0.5, 1.5, ALU.mult, ALU.add))
                step(dve.tensor_tensor(r, r, a, ALU.mult))

            def normalize(n):
                dve.wait_ge(s_ss, n + 1)
                dve.tensor_scalar(ms[:, 0:NT], ss[:, 0:NT], 1.0 / D, EPS, ALU.mult, ALU.add).then_inc(s_ms, 1)
                dve.wait_ge(s_ms, n + 1)
                dve.wait_ge(s_ln, n + 1)
                newton(NT)
                for t in range(NT):
                    ins = dve.tensor_scalar(xn[:, t, :], x[:, t, :], rs[:, t:t + 1], None, ALU.mult)
                    if t < NT - 1:
                        step(ins)
                ins.then_inc(s_xn, 1)
                dve.wait_ge(s_xn, n + 1)

            def modulation(l, j):
                p = ready(dve, ("mod", l, j))
                b = par_ab[:, l, 4 * j:4 * j + 4].unsqueeze(2).broadcast_to([P, 4, 2])
                release(dve, dve.tensor_tensor(modv[:, l, 4 * j:4 * j + 4, :], p[:, 0:8].rearrange("p (c s) -> p c s", s=2), b, ALU.add), ("mod", l, j))

            def gate_diagonals(l, which):
                for n in range(4):
                    s, b = n // 2, n % 2
                    if n >= 2:
                        ready(dve, ("gbc", l, which, (n - 2) // 2, b))
                    g = modv[:, l, (2 + 3 * which) * KC + 4 * b:(2 + 3 * which) * KC + 4 * b + 4, s:s + 1]
                    dve.tensor_tensor(diag[:, b, :, :], ident.unsqueeze(1).broadcast_to([P, 4, P]), g.broadcast_to([P, 4, P]),
                                      ALU.mult).then_inc(s_diag, 1)
                dve.wait_ge(s_diag, 8 * l + 4 * which + 4)

            def scales(l, which):
                a = A1[:, which, :, :]
                sc1 = modv[:, l, (1 + 3 * which) * KC:(2 + 3 * which) * KC, :]
                step(dve.tensor_scalar(a, sc1, 1.0, None, ALU.add))
                g = (par_g1, par_g2)[which]
                dve.tensor_tensor(a, a, g[:, l, :].unsqueeze(2).broadcast_to([P, KC, 2]), ALU.mult).then_inc(s_mod, 1)
                dve.wait_ge(s_mod, 2 * l + which + 1)

            def modulate(l, which):
                for k in range(0, KC, 2):
                    job = ("hT", 2 * l + which, k)
                    p = ready(dve, job)
                    for s, (a, b) in enumerate(((0, P), (P, T))):
                        ins = dve.tensor_scalar(hT[:, k, a:b], p[:, a:b], A1[:, which, k, s:s + 1],
                                                modv[:, l, 3 * KC * which + k, s:s + 1], ALU.mult, ALU.add)
                        if s == 0:
                            step(ins)
                    release(dve, ins, job)

            def operands(l, u):
                t, hp = UNITS[u]
                d_, q0, k0 = dec[u % 2], qT[:, hp, t * P:(t + 1) * P], kT[:, 0, hp, t * P:(t + 1) * P]
                dve.wait_ge(s_dec, l * len(UNITS) + u + 1)
                for n, m in enumerate(LEVELS):
                    M, nb, base = 2 * m, P // (2 * m), n * 2 * P
                    o_ = strided(d_, base + m, [P - m, 2], [M, nb], [1, m])
                    step(dve.tensor_tensor(o_, o_, strided(q0, m, [-m, 2], [M, nb], [1, m]), ALU.mult))
                    o_ = strided(d_, base, [P + m, 2], [M, nb], [1, m])
                    step(dve.tensor_tensor(o_, o_, strided(k0, 0, [HP * T + m, 2], [M, nb], [1, m]), ALU.mult))
                at = NLEV * 2 * P
                if t:
                    step(dve.tensor_tensor(qdec[:, t - 1, hp, :, :], strided(d_, at, [P, 2], [1, P]),
                                           q0.unsqueeze(1).broadcast_to([P, 2, P]), ALU.mult))
                kk = strided(d_, at + 2 * P, [P, 2], [1, P])
                step(dve.tensor_tensor(kk, kk, strided(k0, 0, [HP * T, 2], [1, P]), ALU.mult))
                step(dve.tensor_copy(gdec[:, u, :], d_[:, at + 4 * P:at + 4 * P + 2]))
                dve.tensor_tensor(d_[:, at:at + P], k0, kT[:, 1, hp, t * P:(t + 1) * P], ALU.add).then_inc(s_X, 1)
                dve.wait_ge(s_X, l * len(UNITS) + u + 1)

            def masked_scores(l, u, h2):
                dst = attT[:, 2 * u + h2, :]
                for half in range(2):
                    for g in (2 * half, 2 * half + 1):
                        n = min(4, GRAM - 4 * g)
                        p = ready(dve, ("gram", l, u, h2, g))
                        release(dve, dve.tensor_tensor(mprod[:, 4 * (g % 2):4 * (g % 2) + n, :],
                                                       p[:, 0:n * P].rearrange("p (a b) -> p a b", a=n),
                                                       mk[:, 4 * g:4 * g + n, :], ALU.mult), ("gram", l, u, h2, g))
                    n = 8 - half
                    red = mprod[:, 0:n, :].rearrange("p a b -> p b a")
                    if half == 0:
                        step(dve.tensor_reduce(dst, red, AX, ALU.add))
                    else:
                        step(dve.tensor_reduce(mprod[:, 7, :], red, AX, ALU.add))
                dve.tensor_tensor(dst, dst, mprod[:, 7, :], ALU.add).then_inc(s_att, 1)
                dve.wait_ge(s_att, (l * len(UNITS) + u) * 2 + h2 + 1)

            def states(l, u):
                t, hp = UNITS[u]
                job = ("kv", l, u)
                p = ready(dve, job)
                if t == 0:
                    dve.wait_ge(s_rope, l + 1)
                else:
                    dve.wait_ge(d_state, 16 * 4 * (l + 1))
                for h2 in range(2):
                    r = slice(64 * h2, 64 * h2 + 64)
                    if t == 0:
                        ins = dve.tensor_copy(stout[r, hp, :, :], p[r, 0:2 * P].rearrange("p (d c) -> p d c", d=2)[:, :, 64 * h2:64 * h2 + 64])
                    else:
                        ins = dve.scalar_tensor_tensor(out=S1[r, hp, t - 1, :], in0=S0[r, hp, t - 1, :],
                                                       scalar=gdec[r, u, t - 1:t], in1=p[r, 64 * h2:64 * h2 + 64],
                                                       op0=ALU.mult, op1=ALU.add)
                    if h2 == 0:
                        step(ins)
                release(dve, ins, job)

            step(dve.memset(scp[:, :, :], 0.0))
            dve.wait_ge(s_expc, 1)
            step(dve.tensor_scalar(e1, e1, 1.0, None, ALU.add))
            step(dve.reciprocal(e1, e1))
            dve.wait_ge(d_par, 16)
            dve.tensor_tensor(scp[:, :, 0:2], par_c, e1, ALU.mult).then_inc(s_sc, 1)
            dve.wait_ge(d_row, 16 * 5)
            dve.wait_ge(d_const, 48)
            step(dve.tensor_tensor(lbm, par_lb[:, 0, :], par_lb[:, 1, :], ALU.max))
            step(dve.tensor_tensor(lbe, par_lb, lbm.unsqueeze(1).broadcast_to([P, L, 4]), ALU.subtract))
            step(dve.tensor_tensor(lamt[:, :, 0::2, :], lamt[:, :, 0::2, :], lamt[:, :, 1::2, :], ALU.mult))
            dve.tensor_reduce(lm2, lamt[:, :, 0::2, :], AX, ALU.add).then_inc(s_lbl, 1)
            dve.wait_ge(s_lbe, 2)
            step(dve.tensor_tensor(lbm, lbe[:, 0, :], lbe[:, 1, :], ALU.add))
            step(dve.reciprocal(lbm, lbm))
            step(dve.tensor_tensor(lbe, lbe, lbm.unsqueeze(1).broadcast_to([P, L, 4]), ALU.mult))
            step(dve.tensor_tensor(lbt[:, 0, :], lbe[:, 0, :], lbe[:, 0, :], ALU.subtract))
            step(dve.tensor_tensor(lbt[:, 1, :], lbt[:, 0, :], lbe[:, 1, :], ALU.add))
            step(dve.tensor_scalar(omlb, lbt, -1.0, 1.0, ALU.mult, ALU.add))
            for l in range(L):
                lam_init = 0.8 - 0.6 * math.exp(-0.3 * l)
                step(dve.tensor_tensor(lam[:, l:l + 1], lme[:, l, 1:2], lme[:, l, 0:1], ALU.subtract))
                step(dve.tensor_scalar(lam[:, l:l + 1], lam[:, l:l + 1], -lam_init, None, ALU.add))
                step(dve.tensor_scalar(gsub[:, 0, l, :], gsub[:, 0, l, :], 1.0 - lam_init, None, ALU.mult))

            for l in range(L):
                normalize(2 * l)
                if l == 0:
                    for j in ADA_FIRST:
                        modulation(0, j)
                scales(l, 0)
                modulate(l, 0)
                for hp in range(HP):
                    dve.wait_ge(s_eq, HP * l + hp + 1)
                    step(dve.tensor_scalar(E[:, 0, hp, :], E[:, 0, hp, :], 1.0, None, ALU.add))
                    step(dve.reciprocal(E[:, 0, hp, :], E[:, 0, hp, :]))
                    p = ready(dve, ("bq", l, hp))
                    release(dve, dve.tensor_tensor(qT[:, hp, :], E[:, 0, hp, :], p[:, 0:T], ALU.mult), ("bq", l, hp))
                for d in range(2):
                    for hp in range(HP):
                        p = ready(dve, ("z", l, d, hp))
                        release(dve, dve.tensor_scalar(Z[:, d, hp, :], p[:, 0:T], -80.0, None, ALU.max), ("z", l, d, hp))
                dve.wait_ge(s_e, l + 1)
                step(dve.tensor_scalar(Z, E, 1.0, None, ALU.add))
                step(dve.reciprocal(Z, Z))
                for d in range(2):
                    for hp in range(HP):
                        w = 2 * d + hp
                        step(dve.tensor_scalar(F[:, d, hp, :], Z[:, d, hp, :], omlb[:, l, w:w + 1], lbt[:, l, w:w + 1], ALU.mult, ALU.add))
                        step(dve.scalar_tensor_tensor(out=kT[:, d, hp, :], in0=E[:, d, hp, :], scalar=omlb[:, l, w:w + 1],
                                                      in1=Z[:, d, hp, :], op0=ALU.mult, op1=ALU.mult))
                dve.tensor_scalar(F, F, TINY, None, ALU.max).then_inc(s_f, 1)
                step(dve.memset(strided(C2[:, 0, 0, :], 0, [129, 2 * HP * NT]), 0.0))
                dve.wait_ge(s_lf, l + 1)
                for hp in range(HP):
                    for t in range(NT):
                        for d in range(2):
                            step(dve.tensor_tensor_scan(C2[:, hp, t, d * 129 + 1:d * 129 + 129], ones, F[:, d, hp, t * P:(t + 1) * P],
                                                        0.0, ALU.mult, ALU.add))
                for u in range(2):
                    exponents(dve, step, l, u)
                operands(l, 0)
                for u in range(len(UNITS)):
                    if u + 1 < len(UNITS):
                        operands(l, u + 1)
                    for h2 in range(2):
                        masked_scores(l, u, h2)
                        if h2 == 0:
                            states(l, u)
                        if 0 <= 2 * u + h2 - 1 < len(BETWEEN[l]):
                            modulation(*BETWEEN[l][2 * u + h2 - 1])
                if len(BETWEEN[l]) == 2 * len(UNITS):
                    modulation(*BETWEEN[l][-1])
                n_clat = 0
                seen = {}
                for i in range(len(ATT) + 1):
                    if i < len(ATT):
                        m, t, h = ATT[i]
                        nk = T if t else P
                        if m == "C" and t:
                            n_clat += 1
                            seen[i] = n_clat
                            job = ("sc", l, i, 0)
                            p = ready(dve, job)
                            step(dve.tensor_scalar(scb[:, i % 2, 0:P], p[:, 0:P], 64 ** -0.5, None, ALU.mult))
                            dve.wait_ge(s_bias, l + 1)
                            release(dve, dve.scalar_tensor_tensor(
                                out=scb[:, i % 2, P:T], in0=p[:, P:T], scalar=64 ** -0.5,
                                in1=bias[:, h, t - 1, :, :].rearrange("p a b -> p (a b)"), op0=ALU.mult, op1=ALU.add), job)
                            step(dve.tensor_reduce(mx[:, i % 2, 0:1], scb[:, i % 2, :], AX, ALU.max))
                            dve.tensor_scalar(nmx[:, i % 2, 0:1], mx[:, i % 2, 0:1], -1.0, None, ALU.mult).then_inc(s_mx, 1)
                        else:
                            nm = 2 if m == "A" else 1
                            scale = 32 ** -0.5 if m == "A" else 64 ** -0.5
                            for mp in range(nm):
                                p = ready(dve, ("sc", l, i, mp))
                                step(dve.tensor_reduce(mx[:, i % 2, mp:mp + 1], p[:, 0:nk], AX, ALU.max))
                            dve.tensor_scalar(nmx[:, i % 2, 0:nm], mx[:, i % 2, 0:nm], -scale, None, ALU.mult).then_inc(s_mx, 1)
                    if i >= 1:
                        m, t, h = ATT[i - 1]
                        j = i - 1
                        nk = T if t else P
                        if m == "C" and t:
                            dve.wait_ge(s_pr, l * 8 + seen[j])
                        else:
                            for mp in range(2 if m == "A" else 1):
                                moved(dve, ("sc", l, j, mp))
                        if m == "A":
                            step(dve.reciprocal(rsum[:, j % 4, :], sums[:, j % 2, :]))
                            step(dve.tensor_scalar(rneg[:, j % 2, :], sums[:, j % 2, 0:1], rsum[:, j % 4, 1:2], lam[:, l:l + 1], ALU.mult, ALU.mult))
                            if j >= 2:
                                ready(dve, ("pT", l, j - 2))
                            dve.scalar_tensor_tensor(out=wmix[:, j % 2, 0:nk], in0=prob[:, j % 2, 1, 0:nk], scalar=rneg[:, j % 2, :],
                                                     in1=prob[:, j % 2, 0, 0:nk], op0=ALU.mult, op1=ALU.add).then_inc(s_w, 1)
                        else:
                            dve.reciprocal(rsum[:, j % 4, 0:1], sums[:, j % 2, 0:1]).then_inc(s_w, 1)
                        dve.wait_ge(s_w, l * len(ATT) + j + 1)
                for t in range(NT):
                    for h2 in range(2):
                        moved(dve, ("bo", l, t, h2))
                for i in (len(ATT) - 1, len(ATT) - 2, len(ATT) - 1 - H, len(ATT) - 2 - H):
                    moved(dve, ("ao", l, i))
                for n, o_ in enumerate((oA, oB)):
                    step(dve.tensor_tensor(post[:, n, :, :], o_, o_, ALU.mult))
                step(dve.tensor_reduce(ss, post.rearrange("p a b c -> p (a b) c"), AX, ALU.add))
                dve.tensor_scalar(ms, ss, 1.0 / 64, EPS, ALU.mult, ALU.add).then_inc(s_pss, 1)
                dve.wait_ge(s_pss, l + 1)
                dve.wait_ge(s_ebg, l + 1)
                step(dve.tensor_scalar(pz, pz, 1.0, None, ALU.add))
                step(dve.reciprocal(pz, pz))
                step(dve.tensor_tensor(pz, pz, tok[:, :, BG:BG + 256], ALU.mult))
                dve.wait_ge(s_pln, l + 1)
                newton(24)
                for n, o_ in enumerate((oB, oA)):
                    r0 = 12 * (1 - n)
                    step(dve.tensor_tensor(o_, o_, rs[:, r0:r0 + 12].unsqueeze(2).broadcast_to([P, 12, 64]), ALU.mult))
                    ins = dve.tensor_tensor(o_, o_, gsub[:, 1 - n, l, :].unsqueeze(1).broadcast_to([P, 12, 64]), ALU.mult)
                    if n == 0:
                        step(ins)
                        step(dve.tensor_tensor(o_, o_, pz.rearrange("p t (h c) -> p (t h) c", c=64), ALU.mult))
                ins.then_inc(s_post, 1)
                for c in range(0, 6, 2):
                    p = ready(dve, ("mT", l, c))
                    release(dve, dve.tensor_copy(hT[:, c, :], p[:, 0:T]), ("mT", l, c))
                gate_diagonals(l, 0)
                for s in range(2):
                    for b in range(2):
                        moved(dve, ("gbc", l, 0, s, b))
                for b in range(2):
                    for t in range(NT):
                        job = ("wo", l, b, t)
                        p = ready(dve, job)
                        release(dve, dve.tensor_tensor(mflat[:, 0:512], p, gate[:, min(t, 1), b * 512:(b + 1) * 512], ALU.mult), job)
                        xs = x[:, t, b * 512:(b + 1) * 512]
                        ins = dve.tensor_tensor(xs, xs, mflat[:, 0:512], ALU.add)
                        if (b, t) != (1, NT - 1):
                            step(ins)
                ins.then_inc(s_x, 1)
                dve.wait_ge(s_x, 2 * l + 1)
                gate_diagonals(l, 1)
                scales(l, 1)
                dve.wait_ge(d_out, 16 * 4 * (l + 1))
                normalize(2 * l + 1)
                modulate(l, 1)
                for t in range(NT):
                    p = ready(dve, ("hb", l, t, 0))
                    release(dve, dve.tensor_copy(htok[:, t, 0:512], p), ("hb", l, t, 0))
                p = ready(dve, ("rt", l))
                release(dve, dve.tensor_copy(logit, p[:, 0:NT * NE].rearrange("p (t e) -> p t e", t=NT)), ("rt", l))
                dve.engine_nop().then_inc(s_rl, 1)
                dve.wait_ge(s_re, l + 1)
                step(dve.tensor_scalar(score, score, 1.0, None, ALU.add))
                step(dve.reciprocal(score, score))
                step(dve.tensor_tensor(selv, score, rbias[:, :].unsqueeze(1).broadcast_to([P, NT, NE]), ALU.add))
                sg = selv.rearrange("p t (g e) -> p (t g) e", e=4)
                rankb = rank.unsqueeze(1).broadcast_to([P, NT * 4, 4])

                def first_max(one_hot, values, best, n):
                    rb = rank.unsqueeze(1).broadcast_to([P, n, 4])
                    step(dve.tensor_reduce(best, values, AX, ALU.max))
                    step(dve.tensor_tensor(eqv[:, 0:n, :], values, best.unsqueeze(2).broadcast_to([P, n, 4]), ALU.is_equal))
                    step(dve.tensor_tensor(eqv[:, 0:n, :], eqv[:, 0:n, :], rb, ALU.mult))
                    step(dve.tensor_reduce(gsel[:, 0:n], eqv[:, 0:n, :], AX, ALU.max))
                    step(dve.tensor_tensor(one_hot, eqv[:, 0:n, :], gsel[:, 0:n].unsqueeze(2).broadcast_to([P, n, 4]), ALU.is_equal))

                first_max(oh1, sg, m1, NT * 4)
                step(dve.scalar_tensor_tensor(out=rest, in0=oh1, scalar=-1e30, in1=sg, op0=ALU.mult, op1=ALU.add))
                first_max(oh2, rest, m2, NT * 4)
                step(dve.tensor_tensor(gsc, m1, m2, ALU.add))
                g4 = slotc[:, 0:NT, :]
                first_max(g4, gsc.rearrange("p (t g) -> p t g", g=4), gm, NT)
                for oh in (oh1, oh2):
                    v = oh.rearrange("p (t g) e -> p t g e", g=4)
                    step(dve.tensor_tensor(v, v, g4.unsqueeze(3).broadcast_to([P, NT, 4, 4]), ALU.mult))
                picks = [oh.rearrange("p (t g) e -> p t (g e)", g=4) for oh in (oh1, oh2)]
                dve.tensor_tensor(selm, picks[0], picks[1], ALU.add).then_inc(s_sel, 1)
                dve.wait_ge(s_sel, l + 1)
                step(dve.tensor_tensor(gates, score, selm, ALU.mult))
                step(dve.tensor_reduce(den, gates, AX, ALU.add))
                step(dve.reciprocal(den, den))
                step(dve.tensor_tensor(gates, gates, den.unsqueeze(2).broadcast_to([P, NT, NE]), ALU.mult))
                p = ready(dve, ("pos", l))
                step(dve.tensor_tensor(posn, p[:, 0:NT * NE].rearrange("p (t e) -> p t e", t=NT),
                                       erow.unsqueeze(1).broadcast_to([P, NT, NE]), ALU.add))
                release(dve, dve.tensor_copy(cnt, p[:, NT * NE:(NT + 1) * NE]), ("pos", l))
                payf = pay[:, :, :, :].bitcast(F32)
                tmp3 = slotc.rearrange("p (t g) e -> p t (g e)", g=4)
                for k in range(2):
                    step(dve.tensor_tensor(tmp3, picks[k], posn, ALU.mult))
                    step(dve.tensor_reduce(slotf[:, :, k:k + 1], tmp3, AX, ALU.add))
                    step(dve.tensor_tensor(tmp3, picks[k], gates, ALU.mult))
                    step(dve.tensor_reduce(payf[:, :, k, 2:3], tmp3, AX, ALU.add))
                dve.tensor_copy(slotu[:, :, :], slotf).then_inc(s_pay, 1)
                step(dve.tensor_scalar(novv, cnt, float(CAP), None, ALU.is_gt))
                step(dve.tensor_scalar(ex2, cnt, float(2 * CAP), None, ALU.is_gt))
                step(dve.tensor_tensor(novv, novv, ex2, ALU.add))
                step(dve.tensor_tensor_scan(pin, ones[:, 0:NE], novv, 0.0, ALU.mult, ALU.add))
                step(dve.tensor_tensor(pexc, pin, novv, ALU.subtract))
                rb = ridx.unsqueeze(2).broadcast_to([P, MAXOV, NE])

                def over_experts(v):
                    return v.unsqueeze(1).broadcast_to([P, MAXOV, NE])

                step(dve.tensor_tensor(mat, over_experts(pexc), rb, ALU.is_le))
                step(dve.tensor_tensor(mat2, over_experts(pin), rb, ALU.is_gt))
                step(dve.tensor_tensor(mat, mat, mat2, ALU.mult))
                step(dve.tensor_tensor(mat2, mat, over_experts(eidx), ALU.mult))
                step(dve.tensor_reduce(oeid, mat2, AX, ALU.add))
                step(dve.tensor_tensor(mat2, rb, over_experts(pexc), ALU.subtract))
                step(dve.tensor_scalar(mat2, mat2, float(CAP), float(CAP), ALU.mult, ALU.add))
                step(dve.tensor_tensor(mat2, mat2, over_experts(erow), ALU.add))
                step(dve.tensor_tensor(mat2, mat2, mat, ALU.mult))
                step(dve.tensor_reduce(orow, mat2, AX, ALU.add))
                step(dve.tensor_copy(ovt[0:1, 0:1], pin[0:1, NE - 1:NE]))
                step(dve.tensor_copy(ovt[0:1, 1:1 + MAXOV], oeid[0:1, :]))
                dve.tensor_copy(ovt[0:1, 1 + MAXOV:1 + 2 * MAXOV], orow[0:1, :]).then_inc(s_ovt, 1)
                dve.wait_ge(s_ovt, l + 1)
                dve.wait_ge(s_pay, l + 1)
                dve.wait_ge(d_lst, 16 * (l + 1))

                def expert(i, es, first=False, last=False):
                    e = i * EXP_PER_BODY + es
                    if not last:
                        p = ready(dve, ("xt0", l), e)
                        release(dve, dve.tensor_copy(hTg[:, 0:4, :].rearrange("p a b -> p (a b)"), p), ("xt0", l), e)
                    if not first:
                        p = ready(dve, ("dn1", l), e - 1)
                        stored(dve, l, i, es - 1)
                        release(dve, dve.tensor_scalar(ybuf[:, (es - 1) % 2, 512:1024], p, gate_of(e - 1), None, ALU.mult), ("dn1", l), e - 1)
                    if not last:
                        p = ready(dve, ("u", l), e)
                        moved(dve, ("a", l), e)
                        release(dve, dve.tensor_tensor(zb, sS, p, ALU.mult), ("u", l), e)

                for e in range(EXP_PER_BODY):
                    expert(0, e, first=(e == 0))
                with dve.Fori(1, NBODY) as i:
                    for e in range(EXP_PER_BODY):
                        expert(i, e)
                expert(NBODY, 0, last=True)
                o_ = ov[l]
                n_ov = dve.value_load(ovt[0:1, 0:1], min_val=0, max_val=MAXOV)
                with dve.If(n_ov > 0):
                    with dve.Fori(0, n_ov) as r:
                        def sub(ins, n):
                            ins.then_inc(o_["vector"], 1)
                            dve.wait_ge(o_["vector"], 4 * r + n)

                        dve.wait_ge(o_["tensor"], 4 * r + 1)
                        sub(dve.tensor_copy(hTg, ps[:, 0:2, :].rearrange("p a (b c) -> p (a b) c", c=P)), 1)
                        dve.wait_ge(o_["tensor"], 4 * r + 2)
                        dve.wait_ge(o_["scalar"], r + 1)
                        sub(dve.tensor_tensor(zb, sS, ps[:, 3, :], ALU.mult), 2)
                        dve.wait_ge(o_["tensor"], 4 * r + 3)
                        sub(dve.tensor_copy(zTg.rearrange("p a b -> p (a b)"), ps[:, 4, :]), 3)
                        dve.wait_ge(o_["tensor"], 4 * r + 4)
                        sub(dve.tensor_scalar(ybuf[:, 0, :], ps[:, 5:7, :].rearrange("p a b -> p (a b)"), lsto[:, 2:3].bitcast(F32), None, ALU.mult), 4)
                for s in range(2):
                    for b in range(2):
                        moved(dve, ("gbc", l, 1, s, b))
                dve.wait_ge(d_yr, 16 * NT * (l + 1))
                step(dve.tensor_tensor(yr[:, :, 0, :], yr[:, :, 0, :], yr[:, :, 1, :], ALU.add))
                step(dve.tensor_tensor(yr[:, 0, 0, :], yr[:, 0, 0, :], gate[:, 0, :], ALU.mult))
                step(dve.tensor_tensor(yr[:, 1:3, 0, :], yr[:, 1:3, 0, :], gate[:, 1, :].unsqueeze(1).broadcast_to([P, 2, D]), ALU.mult))
                dve.tensor_tensor(x[:, :, :], x[:, :, :], yr[:, :, 0, :], ALU.add).then_inc(s_x, 1)
                dve.wait_ge(s_x, 2 * l + 2)
            normalize(2 * L)
            dve.wait_ge(d_fin, 16)
            dve.tensor_tensor(xn, xn, gate[:, 0, :].unsqueeze(1).broadcast_to([P, NT, D]), ALU.mult).then_inc(s_y, 1)

        @block.tensor
        def _(pe):
            def slot(l, kind, j):
                n = BLOCK_NO[(kind, l, j)]
                pe.wait_ge(landed[n % SLOTS], 16 * (n // SLOTS + 1))
                return ring[:, n % SLOTS, :].rearrange("p (k n) -> p k n", k=KC)

            def fill(ins, job, i=0):
                ins.then_inc(full[bank(job, i)[0]], 1)

            def matmuls(out, pairs):
                for n, (a, b) in enumerate(pairs):
                    ins = pe.matmul(out, a, b, start=(n == 0), stop=(n == len(pairs) - 1))
                return ins

            def mod_rows(l, j):
                w, job = slot(l, "ada", j), ("row", l, j)
                p = begin(pe, job)
                for k in range(KC):
                    c = 32 * (k % 4)
                    ins = pe.matmul(p[c:c + 32, :], scp[:, k, :], w[:, k, :], start=(k < 4), stop=(k >= 4), tile_position=(0, c))
                fill(ins, job)

            def mod_turn(l, j, b):
                job = ("mod", l, j)
                p = begin(pe, job)
                moved(pe, ("row", l, j))
                for c in range(4):
                    ins = pe.matmul(p[:, 2 * c:2 * c + 2], rows[:, b, c * P:(c + 1) * P], fold, start=True, stop=True)
                fill(ins, job)

            def gate_spread(l, which):
                for n in range(4):
                    job = ("gbc", l, which, n // 2, n % 2)
                    p = begin(pe, job)
                    pe.wait_ge(s_diag, 8 * l + 4 * which + n + 1)
                    fill(pe.matmul(p, ones, diag[:, n % 2, :, :].rearrange("p a b -> p (a b)"), start=True, stop=True), job)

            def transposes(job, srcs):
                p = begin(pe, job)
                for n, s in enumerate(srcs):
                    ins = pe.transpose(p[:, n * P:(n + 1) * P], s, ident)
                fill(ins, job)

            def hidden(n):
                pe.wait_ge(s_xn, n + 1)
                for k in range(KC):
                    transposes(("hT", n, k), [xn[:, t, k * P:(k + 1) * P] for t in range(NT)])
                for k in range(KC):
                    moved(pe, ("hT", n, k))

            def by_token(l, w, job, t, c0, c1):
                p = begin(pe, job)
                fill(matmuls(p[:, 0:c1 - c0], [(hT[:, k, t * P:(t + 1) * P], w[:, k, c0:c1]) for k in range(KC)]), job)

            def by_feature(l, w, job, c):
                p = begin(pe, job)
                fill(matmuls(p[:, 0:T], [(w[:, k, c * P:(c + 1) * P], hT[:, k, :]) for k in range(KC)]), job)

            pe.wait_ge(s_sc, 1)
            for l in range(L):
                if l == 0:
                    for n, j in enumerate(ADA_FIRST):
                        mod_rows(0, j)
                        if n == 0:
                            pe.wait_ge(d_const, 48)
                        else:
                            mod_turn(0, ADA_FIRST[n - 1], (n - 1) % 2)
                    mod_turn(0, ADA_FIRST[-1], (len(ADA_FIRST) - 1) % 2)
                hidden(2 * l)
                w = slot(l, "win", 1)
                for hp in range(HP):
                    by_feature(l, w, ("bq", l, hp), 2 + hp)
                for t in range(NT):
                    by_token(l, w, ("av", l, t), t, 0, 256)
                w = slot(l, "win", 2)
                for d in range(2):
                    for hp in range(HP):
                        by_feature(l, w, ("z", l, d, hp), 2 * d + hp)
                w = slot(l, "win", 3)
                for t in range(NT):
                    by_token(l, w, ("bvg", l, t), t, 0, 512)
                w = slot(l, "win", 0)
                for t in range(NT):
                    by_token(l, w, ("aqk", l, t), t, 0, 512)
                w = slot(l, "win", 4)
                for hp in range(HP):
                    by_feature(l, w, ("cq", l, hp), hp)
                for hp in range(HP):
                    by_feature(l, w, ("ck", l, hp), 2 + hp)
                w = slot(l, "win", 5)
                for t in range(NT):
                    by_token(l, w, ("cvdu", l, t), t, 0, 512)
                for t in range(NT):
                    moved(pe, ("cvdu", l, t))
                for c in range(2):
                    ch = slice(DU + c * P, DU + (c + 1) * P)
                    p = begin(pe, ("du", l, c, 0))
                    fill(pe.matmul(p[:, 0:256], tok[:, 0, ch], dftc, start=True, stop=True), ("du", l, c, 0))
                    p = begin(pe, ("du", l, c, 1))
                    fill(matmuls(p, [(tok[:, 1 + t, ch], dftl[:, t, :]) for t in range(2)]), ("du", l, c, 1))
                for c in range(2):
                    job = ("dy", l, c)
                    p = begin(pe, job)
                    moved(pe, ("du", l, c, 0))
                    moved(pe, ("du", l, c, 1))
                    matmuls(p[:, 0:P], [(chc, Ud[:, c, 0:P]), (chs, Ud[:, c, P:2 * P])])
                    fill(matmuls(p[:, P:T], [(chc, Ud[:, c, 256:512]), (chs, Ud[:, c, 512:768])]), job)
                pe.wait_ge(d_cache, 64 * (l + 1))
                transposes(("cc", l), [cachek[:, 2, 2 * hp:2 * hp + 2, :].rearrange("p a b -> p (a b)") for hp in range(HP)])
                for hp in range(HP):
                    moved(pe, ("ck", l, hp))
                transposes(("nk", l), [ckT[:, hp, 0:P] for hp in range(HP)])
                at = NLEV * 2 * P
                for t in range(NT):
                    moved(pe, ("bvg", l, t))
                for u, (t, hp) in enumerate(UNITS):
                    d_ = dec[u % 2]
                    pe.wait_ge(s_X, l * len(UNITS) + u + 1)
                    dirs = (0, 1) if t == 0 else (t - 1,)
                    transposes(("kd", l, u), [d_[:, at + (2 + d) * P:at + (3 + d) * P] for d in dirs])
                    for h2 in range(2):
                        r = slice(64 * h2, 64 * h2 + 64)
                        for g in range(4):
                            job = ("gram", l, u, h2, g)
                            p = begin(pe, job)
                            for n in range(4 * g, min(4 * g + 4, GRAM)):
                                if n < 2 * NLEV:
                                    a = b = d_[r, n * P:(n + 1) * P]
                                else:
                                    a, b = d_[r, at:at + P], qT[r, hp, t * P:(t + 1) * P]
                                ins = pe.matmul(p[:, (n % 4) * P:(n % 4 + 1) * P], a, b, start=True, stop=True)
                            fill(ins, job)
                        if h2 == 0:
                            job = ("kv", l, u)
                            p = begin(pe, job)
                            moved(pe, ("kd", l, u))
                            for n in range(len(dirs)):
                                ins = pe.matmul(p[:, n * P:(n + 1) * P], kdT[:, u % 2, n, :], tok[:, t, BV + hp * P:BV + (hp + 1) * P],
                                                start=True, stop=True)
                            fill(ins, job)
                        n = 2 * u + h2
                        if n < len(BETWEEN[l]):
                            mod_rows(*BETWEEN[l][n])
                        if 0 <= n - 1 < len(BETWEEN[l]):
                            mod_turn(*BETWEEN[l][n - 1], (n - 1) % 2)
                if len(BETWEEN[l]) == 2 * len(UNITS):
                    mod_turn(*BETWEEN[l][-1], (len(BETWEEN[l]) - 1) % 2)
                for u in range(len(UNITS)):
                    moved(pe, ("kv", l, u))
                pe.wait_ge(s_att, 2 * len(UNITS) * (l + 1))
                for t in range(NT):
                    for h2 in range(2):
                        job = ("bo", l, t, h2)
                        p = begin(pe, job)
                        r = slice(64 * h2, 64 * h2 + 64)
                        for hp in range(HP):
                            h = 2 * hp + h2
                            pairs = [(attT[:, 2 * (t * HP + hp) + h2, :], tok[:, t, BV + 64 * h:BV + 64 * h + 64])]
                            if t:
                                pairs += [(qdec[r, t - 1, hp, d, :], (S0 if (t == 1) == (d == 0) else S1)[r, hp, d, :]) for d in range(2)]
                            ins = matmuls(p[:, 64 * hp:64 * hp + 64], pairs)
                        fill(ins, job)
                pe.wait_ge(s_rope, l + 1)
                for hp in range(HP):
                    transposes(("aT", l, 0, hp), [tok[:, t, AQ + hp * P:AQ + (hp + 1) * P] for t in range(NT)])
                for hp in range(HP):
                    kc = cachek[:, 0, 2 * hp:2 * hp + 2, :].rearrange("p a b -> p (a b)")
                    kt = [tok[:, t, AK + hp * P:AK + (hp + 1) * P] for t in range(NT)]
                    transposes(("aT", l, 1, hp), [kt[0], kc, kt[1], kt[2]])
                for w in range(2):
                    for hp in range(HP):
                        moved(pe, ("aT", l, w, hp))
                moved(pe, ("cc", l))
                for hp in range(HP):
                    moved(pe, ("cq", l, hp))
                n_clat = 0
                for i in range(len(ATT) + 2):
                    if i < len(ATT):
                        m, t, h = ATT[i]
                        hp, h2 = h // 2, h % 2
                        keys = slice(P, 4 * P) if t else slice(0, P)
                        nk = T if t else P
                        for mp in range(2 if m == "A" else 1):
                            job = ("sc", l, i, mp)
                            p = begin(pe, job)
                            if m == "A":
                                r = slice(64 * h2 + 32 * mp, 64 * h2 + 32 * mp + 32)
                                q, k = aqT, akT
                            else:
                                r = slice(64 * h2, 64 * h2 + 64)
                                q, k = cqT, ckT
                            kw = {"tile_position": (r.start, 0)} if m == "A" else {}
                            fill(pe.matmul(p[:, 0:nk], q[r, hp, t * P:(t + 1) * P], k[r, hp, keys], start=True, stop=True, **kw), job)
                    if 0 <= i - 1 < len(ATT):
                        m, t, h = ATT[i - 1]
                        pe.wait_ge(s_w, l * len(ATT) + i)
                        src = wmix[:, (i - 1) % 2, :] if m == "A" else prob[:, (i - 1) % 2, 0, :]
                        transposes(("pT", l, i - 1), [src[:, n * P:(n + 1) * P] for n in range(3 if t else 1)])
                    if i >= 2:
                        m, t, h = ATT[i - 2]
                        c0 = AV if m == "A" else CV
                        job = ("ao", l, i - 2)
                        p = begin(pe, job)
                        moved(pe, ("pT", l, i - 2))
                        w_ = wT[:, (i - 2) % 2, :]
                        vt = [tok[:, tt, c0 + 64 * h:c0 + 64 * h + 64] for tt in range(NT)]
                        v = [cachek[:, 1 if m == "A" else 3, h, :], vt[1], vt[2]] if t else [vt[0]]
                        fill(matmuls(p[:, 0:64], [(w_[:, n * P:(n + 1) * P], v[n]) for n in range(len(v))]), job)
                pe.wait_ge(s_post, l + 1)
                for i in range(len(ATT)):
                    if i >= len(ATT) - BANKS:
                        moved(pe, ("ao", l, i))
                for c in range(6):
                    src = (oA, oB, oC)[c // 2].rearrange("p (t h) c -> p t (h c)", t=NT)
                    transposes(("mT", l, c), [src[:, t, (c % 2) * P:(c % 2 + 1) * P] for t in range(NT)])
                for c in range(6):
                    moved(pe, ("mT", l, c))
                for c in range(2):
                    moved(pe, ("dy", l, c))
                gate_spread(l, 0)
                for b in range(2):
                    w = slot(l, "wout", b)
                    for t in range(NT):
                        by_token(l, w, ("wo", l, b, t), t, 0, 512)
                gate_spread(l, 1)
                hidden(2 * l + 1)
                for t in range(NT):
                    for b in range(2):
                        transposes(("hb", l, t, b), [hT[:, k, t * P:(t + 1) * P] for k in range(4 * b, 4 * b + 4)])
                job = ("rt", l)
                p = begin(pe, job)
                pe.wait_ge(d_row, 16 * 5)
                for t in range(NT):
                    ins = matmuls(p[:, t * NE:(t + 1) * NE], [(hT[:, k, t * P:(t + 1) * P], wrt[:, k, :]) for k in range(KC)])
                fill(ins, job)
                job = ("pos", l)
                p = begin(pe, job)
                pe.wait_ge(s_sel, l + 1)
                for t in range(NT):
                    matmuls(p[:, t * NE:(t + 1) * NE], [(ones, selm[:, b, :]) for b in range(t)] + [(tri, selm[:, t, :])])
                fill(matmuls(p[:, NT * NE:(NT + 1) * NE], [(ones, selm[:, b, :]) for b in range(NT)]), job)
                n0 = FIRST_BLOCK[l] + len(PRE[l])

                def expert(i, es, first=False, last=False):
                    e = i * EXP_PER_BODY + es

                    def block_of(c, q):
                        n = n0 + 3 * c + q
                        pe.wait_ge(landed[n % SLOTS], i * (16 * 3 * EXP_PER_BODY // SLOTS) + 16 * (n // SLOTS + 1))
                        return ring[:, n % SLOTS, :].rearrange("p (k n) -> p k n", k=(KC, KC, FC)[q])

                    def turn(kind, e_, srcs):
                        p = begin(pe, (kind, l), e_)
                        for n, s in enumerate(srcs):
                            ins = pe.transpose(p[:, n * P:(n + 1) * P], s, ident)
                        fill(ins, (kind, l), e_)

                    if not last:
                        half = i * (16 * EXP_PER_BODY // 2) + 16 * (NE // 2 * l + es // 2 + 1)
                        pe.wait_ge(d_g[es % 2], half)
                        for b in range(2):
                            turn(f"xt{b}", e, [xg[:, es % 2, k * P:(k + 1) * P] for k in range(4 * b, 4 * b + 4)])
                    if not first:
                        moved(pe, ("u", l), e - 1)
                        turn("zt", e - 1, [zb[:, f * P:(f + 1) * P] for f in range(FC)])
                    if not last:
                        w = block_of(es, 0)
                        p = begin(pe, ("a", l), e)
                        for b in range(2):
                            moved(pe, (f"xt{b}", l), e)
                        fill(matmuls(p, [(hTg[:, k, :], w[:, k, :]) for k in range(KC)]), ("a", l), e)
                    if not first:
                        w = block_of(es - 1, 2)
                        moved(pe, ("zt", l), e - 1)
                        for b in range(2):
                            p = begin(pe, (f"dn{b}", l), e - 1)
                            fill(matmuls(p, [(zTg[:, f, :], w[:, f, b * 512:(b + 1) * 512]) for f in range(FC)]), (f"dn{b}", l), e - 1)
                    if not last:
                        w = block_of(es, 1)
                        p = begin(pe, ("u", l), e)
                        fill(matmuls(p, [(hTg[:, k, :], w[:, k, :]) for k in range(KC)]), ("u", l), e)

                for e in range(EXP_PER_BODY):
                    expert(0, e, first=(e == 0))
                with pe.Fori(1, NBODY) as i:
                    for e in range(EXP_PER_BODY):
                        expert(i, e)
                expert(NBODY, 0, last=True)
                o_ = ov[l]
                pe.wait_ge(s_ovt, l + 1)
                n_ov = pe.value_load(ovt[0:1, 0:1], min_val=0, max_val=MAXOV)
                with pe.If(n_ov > 0):
                    for b, kind in enumerate(EJOBS):
                        moved(pe, (kind, l), NE - 1)
                    with pe.Fori(0, n_ov) as r:
                        pe.wait_ge(o_["gathered"], 16 * r + 16)
                        for k in range(KC):
                            ins = pe.transpose(ps[:, k // 4, (k % 4) * P:(k % 4 + 1) * P], xg[:, 0, k * P:(k + 1) * P], ident)
                        ins.then_inc(o_["tensor"], 1)
                        pe.wait_ge(o_["vector"], 4 * r + 1)
                        pe.wait_ge(o_["weights_landed"], 48 * r + 48)
                        wg, wu = (ring[:, q, :].rearrange("p (k n) -> p k n", k=KC) for q in range(2))
                        wd = ring[:, 2, :].rearrange("p (k n) -> p k n", k=FC)
                        matmuls(ps[:, 2, :], [(hTg[:, k, :], wg[:, k, :]) for k in range(KC)])
                        matmuls(ps[:, 3, :], [(hTg[:, k, :], wu[:, k, :]) for k in range(KC)]).then_inc(o_["tensor"], 1)
                        pe.wait_ge(o_["vector"], 4 * r + 2)
                        for f in range(FC):
                            ins = pe.transpose(ps[:, 4, f * P:(f + 1) * P], zb[:, f * P:(f + 1) * P], ident)
                        ins.then_inc(o_["tensor"], 1)
                        pe.wait_ge(o_["vector"], 4 * r + 3)
                        for b in range(2):
                            ins = matmuls(ps[:, 5 + b, :], [(zTg[:, f, :], wd[:, f, b * 512:(b + 1) * 512]) for f in range(FC)])
                        ins.then_inc(o_["tensor"], 1)
                        pe.wait_ge(o_["vector"], 4 * r + 4)


def constants():
    def dft(n):
        ang = 2 * np.pi * (np.outer(np.arange(n), np.arange(n)) % n) / n
        return np.cos(ang), np.sin(ang)

    parts = [np.eye(P)]
    c, s = dft(P)
    parts.append(np.concatenate([c, s], 1) / math.sqrt(P))
    c, s = dft(2 * P)
    parts.append((np.concatenate([c, s], 1) / math.sqrt(2 * P)).reshape(2, P, 512).transpose(1, 0, 2))
    c, s = dft(64)
    parts += [np.kron(np.eye(2), c) / 8.0, -np.kron(np.eye(2), s) / 8.0]
    freq = (np.float32(10000.0) ** (-np.arange(8, dtype=np.float32) / np.float32(8))).astype(np.float32)
    pos = np.arange(2 * P)
    ang = np.concatenate([(pos // GRID_W).astype(np.float32)[:, None] * freq, (pos % GRID_W).astype(np.float32)[:, None] * freq], -1)
    cos, sin = np.cos(ang.astype(np.float64)), np.sin(ang.astype(np.float64))
    parts.append(np.repeat(cos, 2, -1).reshape(2, P, 32).transpose(1, 0, 2))
    parts.append(sin.reshape(2, P, 16).transpose(1, 0, 2))
    qc = np.arange(P) % GRID_W
    start = np.clip(qc - 8, 0, GRID_W - 16)
    kc = np.arange(GRID_W)
    parts.append(np.where((kc[None] >= start[:, None]) & (kc[None] < start[:, None] + 16), 0.0, -1e30))
    parts.append(np.ones((P, P)))
    parts.append((np.arange(P)[:, None] % 32 == np.arange(2)[None]).astype(np.float64))
    parts.append(np.tile(np.array([4.0, 3.0, 2.0, 1.0]), (P, 1)))
    parts.append(np.triu(np.ones((P, P)), 1))
    parts += [np.tile(v.astype(np.float64), (P, 1)) for v in (np.arange(NE), np.arange(NE) * T, np.arange(MAXOV))]
    return np.concatenate([p.reshape(P, -1) for p in parts], 1).astype(np.float32)


def slot_words():
    empty = np.tile(np.array([0, NOWHERE, 0, 0], np.uint32), (P, NE * T // P))
    tok, k = np.arange(T), np.arange(2)
    rec = np.zeros((T, 2, 4), np.uint32)
    rec[:, :, 0], rec[:, :, 1] = tok[:, None], 2 * tok[:, None] + k
    return np.concatenate([empty, rec.reshape(NT, P, 8).transpose(1, 0, 2).reshape(P, -1)], 1)


def level_masks():
    s, t = np.arange(P)[:, None], np.arange(P)[None]
    out = []
    for m in LEVELS:
        same = s // (2 * m) == t // (2 * m)
        out.append(same & (s // m % 2 == 0) & (t // m % 2 == 1))
        out.append(same & (s // m % 2 == 1) & (t // m % 2 == 0))
    out.append(s == t)
    return np.stack(out, 1).reshape(P, -1)


def kernel(**inputs):
    import ml_dtypes
    import concourse.bacc as bacc
    from concourse.bass_utils import run_bass_kernel_spmd

    a = {k: np.ascontiguousarray(v) for k, v in inputs.items()}

    def cols(v):
        v = v.reshape(v.shape[0], -1, P)
        return v.transpose(2, 0, 1).reshape(P, -1)

    cc = np.stack([a["c_ctx"].reshape(KC, P), a["c"][0].reshape(KC, P)], -1)
    params = np.concatenate([cols(a["norm1_g"]), cols(a["norm2_g"]), cols(a["ada_b"]),
                             cols(a["hgrn_lb_logits"].reshape(L, -1)), cc.transpose(1, 0, 2).reshape(P, -1)], 1)
    pad = np.zeros((L * H * RPB_H, RPER), np.float32)
    pad[:, GRID_W - RPB_W // 2 - 1:GRID_W - RPB_W // 2 - 1 + RPB_W] = a["na_rpb"].reshape(-1, RPB_W)
    direct = ["x_prompt", "x_sample", "cache_diff_k", "cache_diff_v", "cache_na_k", "cache_na_v", "state_hgrn", "ada_w",
              "ada_b", "w_in", "w_out", "diff_lambda", "diff_subln_g", "hgrn_norm_g", "router_w", "router_b",
              "moe_w_gate", "moe_w_up", "moe_w_down", "final_norm_g"]
    arrays = {n: a[n] for n in direct}
    arrays["params"] = np.ascontiguousarray(params)
    arrays["rpb_pad"] = pad
    arrays["consts"] = constants()
    arrays["slots0"] = slot_words()
    arrays["masks"] = level_masks().astype(ml_dtypes.bfloat16)

    nc = bacc.Bacc("TRN2", target_bir_lowering=False, num_devices=1)
    args = {n: nc.dram_tensor(n, v.shape, mybir.dt.from_np(v.dtype), kind="ExternalInput").ap() for n, v in arrays.items()}
    shapes = {"y_prompt": (1, P, D), "y_sample": (1, 2 * P, D), "new_diff_k": (1, L, H, P, 64), "new_diff_v": (1, L, H, P, 64),
              "new_na_k": (1, L, H, P, 64), "new_na_v": (1, L, H, P, 64), "new_state": (1, L, 2, H, 64, 64)}
    outs = [nc.dram_tensor(n, s, F32, kind="ExternalOutput").ap() for n, s in shapes.items()]
    hybrid_step(nc, outs=outs, **args)
    r = run_bass_kernel_spmd(nc, [arrays], core_ids=[0])
    return tuple(r.results[0][n] for n in shapes)
```

```python
import math
from contextlib import ExitStack

import numpy as np

import concourse.bass as bass
from concourse import mybir

F32 = mybir.dt.float32
U32 = mybir.dt.uint32
ALU = mybir.AluOpType
ACT = mybir.ActivationFunctionType
AX = mybir.AxisListType.X

P = 128
D = 1024
KC = D // P
L = 2
NT = 3
T = NT * P
H = 4
HP = 2
GRID_W = 64
EPS = 1e-6
NE = 16
FE = 512
FC = FE // P
BANKS = 8
SLOTS = 4
BLK = 4096
LEVELS = [64, 32, 16, 8, 4, 2, 1]
NLEV = len(LEVELS)
GRAM = 2 * NLEV + 1
DCOLS = 2 * NLEV * P + 4 * P + 2
TINY = 2.0 ** -60
RPB_H, RPB_W = 15, 31
RPER = 2 * GRID_W - 1
ADA_FIRST = [0, 1, 2, 3]
ADA_REST = list(range(4, 12))
WIN_ORDER = [2, 1, 3, 0, 4, 5]
EXP_PER_BODY = 4
CAP = P
MAXOV = 5
NOWHERE = 1 << 20
EJOBS = ["xt0", "xt1", "zt", "a", "dn0", "dn1", "u"]
NBODY = NE // EXP_PER_BODY
BETWEEN = [[(l, j) for j in ADA_REST] for l in range(L)]
AHEAD = [[(l + 1, j) for j in ADA_FIRST if l + 1 < L] for l in range(L)]
PRE = [[("ada", 0, j) for j in ADA_FIRST if l == 0] + [("win", l, j) for j in WIN_ORDER[:-1]]
       + [("ada", m, j) for m, j in BETWEEN[l][:2]] + [("win", l, WIN_ORDER[-1])] + [("ada", m, j) for m, j in BETWEEN[l][2:]]
       + [("wout", l, j) for j in range(2)] + [("ada", m, j) for m, j in AHEAD[l]] for l in range(L)]
FIRST_BLOCK = [sum(len(PRE[m]) + 3 * NE for m in range(l)) for l in range(L)]
BLOCK_NO = {blk: FIRST_BLOCK[l] + n for l in range(L) for n, blk in enumerate(PRE[l])}
MOD_ORDER = [(0, j) for j in ADA_FIRST] + [blk for l in range(L) for blk in BETWEEN[l] + AHEAD[l]]
MOD_BANK = 7
assert all(j % 4 == n % 4 for n, (_, j) in enumerate(MOD_ORDER))
assert all(len(p) % SLOTS == 0 for p in PRE) and 3 * NE % SLOTS == 0 and 3 * EXP_PER_BODY % SLOTS == 0
UNITS = [(t, hp) for t in range(NT) for hp in range(HP)]
ATT = ([("A", 0, h) for h in range(H)] + [("C", 0, h) for h in range(H)]
       + [(m, t, h) for m in "AC" for t in (1, 2) for h in range(H)])
BSLOTS = 2 * len(UNITS)
NSLOT_PROJ = 6
LAST_A = max(i for i, (m, _, _) in enumerate(ATT) if m == "A")
NORM_B, NORM_A = 3, LAST_A + 5
AQ, AK, AV, BV, BG, CV, DU = 0, 256, 512, 768, 1024, 1280, 1536
PTOK = 1792


def filler_jobs(l, at):
    n = filler(l, at)
    if n is None:
        return []
    return [("mod", group(*BETWEEN[l][n - 1]))] if n and n % 4 == 0 else []


def filler(l, at):
    kind, i = at
    n = i - NSLOT_PROJ if kind == "B" else BSLOTS - NSLOT_PROJ + (i - 1) // 3
    if n < 0 or n > len(BETWEEN[l]) or (kind == "AC" and i % 3 != 1):
        return None
    return n


def group(l, j):
    return MOD_ORDER.index((l, j)) // 4


def b_jobs(l, n):
    u, h2 = n // 2, n % 2
    jobs = [("kd", l, u)] if h2 == 0 else []
    jobs += [("gram", l, u, h2, g) for g in range(4)] + ([("kv", l, u)] if h2 == 0 else [])
    return jobs + filler_jobs(l, ("B", n))


def layer_jobs(l):
    jobs = [("mod", 0)] if l == 0 else []
    jobs += [("hT", 2 * l, k) for k in range(KC)]
    jobs += [("z", l, d, hp) for d in range(2) for hp in range(HP)]
    jobs += [("bq", l, 0), ("bq", l, 1)] + [("av", l, t) for t in range(NT)]
    jobs += [("bvg", l, t) for t in range(NT)] + [("aqk", l, 0)] + b_jobs(l, 0) + b_jobs(l, 1)
    jobs += [("aqk", l, 1), ("aqk", l, 2)] + b_jobs(l, 2) + b_jobs(l, 3) + [("cq", l, hp) for hp in range(HP)]
    jobs += b_jobs(l, 4) + b_jobs(l, 5) + [("ck", l, hp) for hp in range(HP)] + b_jobs(l, 6) + b_jobs(l, 7)
    jobs += [("cvdu", l, 0), ("cvdu", l, 1)] + b_jobs(l, 8) + b_jobs(l, 9) + [("cvdu", l, 2)]
    jobs += [("du", l, c, w) for c in range(2) for w in range(2)] + [("dy", l, c) for c in range(2)]
    jobs += [("cc", l), ("nk", l)]
    jobs += b_jobs(l, 10) + b_jobs(l, 11)
    jobs += [("bo", l, t, h2) for t in range(NT) for h2 in range(2)]
    jobs += [("aT", l, w, hp) for w in range(2) for hp in range(HP)]
    for i in range(len(ATT) + 3):
        if i < len(ATT):
            jobs += [("sc", l, i, m) for m in range(2 if ATT[i][0] == "A" else 1)]
        if 0 <= i - 2 < len(ATT):
            jobs += [("pT", l, i - 2)]
        if i >= 3:
            jobs += [("ao", l, i - 3)]
        jobs += filler_jobs(l, ("AC", i))
    jobs += [("mT", l, c) for c in range(6)] + [("gbc", l, 0, s, b) for s in range(2) for b in range(2)]
    jobs += [("wo", l, b, t) for t in range(NT) for b in range(2)]
    gbc = [("gbc", l, 1, s, b) for s in range(2) for b in range(2)]
    hb = [("hb", l, t, b) for t in range(NT) for b in range(2)]
    jobs += gbc + [("hT", 2 * l + 1, k) for k in range(KC)] + hb + [("rt", l)]
    jobs += [("pos", l)] + ([("mod", group(*AHEAD[l][-1]))] if AHEAD[l] else [])
    return jobs


def place_jobs():
    place, n, uses = {}, 0, [0] * BANKS
    for l in range(L):
        for job in layer_jobs(l):
            b = n % MOD_BANK
            uses[b] += 1
            place[job] = (b, uses[b])
            n += 1
        for b, kind in enumerate(EJOBS):
            place[(kind, l)] = (b, uses[b] + 1)
            uses[b] += NE
    return place


def hybrid_step(nc, x_prompt, x_sample, cache_diff_k, cache_diff_v, cache_na_k, cache_na_v, state_hgrn, ada_w, ada_b,
                w_in, w_out, diff_lambda, diff_subln_g, hgrn_norm_g, router_w, router_b, moe_w_gate, moe_w_up,
                moe_w_down, final_norm_g, params, rpb_pad, consts, masks, slots0, outs):
    y_prompt, y_sample, new_diff_k, new_diff_v, new_na_k, new_na_v, new_state = outs
    place = place_jobs()

    with ExitStack() as ctx:
        def sb(name, shape, dt=F32):
            return ctx.enter_context(nc.sbuf_tensor(name, shape, dt))

        def sem(name):
            return ctx.enter_context(nc.semaphore(name))

        ring = sb("ring", [P, SLOTS, BLK])
        x = sb("x", [P, NT, D])
        hT = sb("hT", [P, KC, T])
        gate = sb("gate", [P, 2, D])
        big = sb("big", [P, 7168])
        dbuf = sb("dbuf", [P, 2 * DCOLS])
        bbuf = sb("bbuf", [P, 3852])
        mprod = sb("mprod", [P, 8, P])
        attT = sb("attT", [P, len(UNITS) * 2, P])
        qdec = sb("qdec", [P, 2, HP, 2, P])
        kdT = sb("kdT", [P, 2, 2, P])
        bias = sb("bias", [P, H, 2, 4, GRID_W])
        cachek = sb("cachek", [P, 4, H, 64])
        S0 = sb("S0", [P, HP, 2, 64])
        S1 = sb("S1", [P, HP, 2, 64])
        mk = sb("mk", [P, GRAM, P], mybir.dt.bfloat16)
        const = sb("const", [P, consts.shape[1]])
        par = sb("par", [P, params.shape[1]])
        wrt = sb("wrt", [P, KC, NE])
        rbias = sb("rbias", [P, NE])
        gsub = sb("gsub", [P, 2, L, 64])
        modv = sb("modv", [P, L, 6 * KC, 2])
        scp = sb("scp", [P, KC, 38])
        lst = sb("lst", [P, NE, 4], U32)
        lsto = sb("lsto", [P, 4], U32)
        pay = sb("pay", [P, NT, 2, 4], U32)
        slotu = sb("slotu", [P, NT, 2], U32)
        ovt = sb("ovt", [1, 1 + 2 * MAXOV], mybir.dt.int32)
        rtmp = sb("rtmp", [P, 512])
        small = sb("small", [P, 290])
        ps = ctx.enter_context(nc.psum_tensor("ps", [P, BANKS, 512], F32))

        def carve(buf, at, *shape):
            names = "abcde"[:len(shape)]
            v = buf[:, at:at + int(np.prod(shape))]
            if len(shape) == 1:
                return v
            return v.rearrange(f"p ({' '.join(names)}) -> p {' '.join(names)}", **dict(zip(names, shape)))

        def strided(v, offset, *dims):
            return bass.AP(v.tensor, v.offset + offset, [list(v.ap[0])] + [list(d) for d in dims])

        tok = carve(big, 0, NT, PTOK)
        cqT = carve(big, NT * PTOK, HP, T)
        ckT = carve(big, NT * PTOK + HP * T, HP, 4 * P)
        xn = carve(big, 0, NT, D)
        htok = carve(big, 0, NT, D)
        ybuf = carve(big, NT * D, 2, D)
        sS = carve(big, NT * D + 2 * D, FE)
        zb = carve(big, NT * D + 2 * D + FE, FE)
        yr = carve(big, 0, NT, 2, D)
        junk = carve(big, 2 * NT * D, D)
        qT = carve(bbuf, 0, HP, T)
        kT = carve(bbuf, HP * T, 2, HP, T)
        C2 = carve(bbuf, 3 * HP * T, HP, NT, 258)
        aqT = carve(bbuf, 0, HP, T)
        akT = carve(bbuf, HP * T, HP, 4 * P)
        oA = carve(bbuf, HP * T + HP * 4 * P, NT * H, 64)
        oC = carve(bbuf, HP * T + HP * 4 * P + NT * H * 64, NT * H, 64)
        Z = carve(dbuf, 0, 2, HP, T)
        E = carve(dbuf, 2 * HP * T, 2, HP, T)
        F = carve(dbuf, 4 * HP * T, 2, HP, T)
        dec = [dbuf[:, u * DCOLS:(u + 1) * DCOLS] for u in range(2)]
        prob = carve(dbuf, 0, 2, 2, T)
        wmix = carve(dbuf, 4 * T, 2, T)
        scb = carve(dbuf, 6 * T, 2, T)
        wT = carve(dbuf, 8 * T, 2, T)
        oB = carve(dbuf, 10 * T, NT * H, 64)
        squares = carve(mprod[:, :, :].rearrange("p a b -> p (a b)"), 0, NT * H, 64)
        xg = carve(dbuf, 0, 2, D)
        hTg = carve(dbuf, 2 * D, KC, P)
        zTg = carve(dbuf, 2 * D + KC * P, FC, P)
        mflat = mprod[:, :, :].rearrange("p a b -> p (a b)")
        diag = carve(mflat, 0, 2, 4, P)
        rows2 = carve(dbuf, 2 * D + KC * P + FC * P, 512)
        rows = gate[:, 0, 0:512]
        lamt = carve(mflat, 0, L, 4, 32)
        Ud = carve(hT[:, :, :].rearrange("p a b -> p (a b)"), 0, 2, 768)
        nkout = carve(rtmp, 0, H, 64)
        stout = carve(gate[:, 1, :], 0, HP, 2, 64)

        o = [0]

        def cst(*shape):
            v = carve(const, o[0], *shape)
            o[0] += int(np.prod(shape))
            return v

        ident = cst(P)
        dftc = cst(2 * P)
        dftl = cst(2, 512)
        chc, chs = cst(P), cst(P)
        ropec, ropes = cst(2, 32), cst(2, 16)
        namask = cst(GRID_W)
        ones = cst(P)
        fold = cst(8)
        rank = cst(4)
        tri = cst(P)
        eidx, erow, ridx = cst(NE), cst(NE), cst(MAXOV)
        assert o[0] == consts.shape[1]
        par_g1, par_g2 = carve(par, 0, L, KC), carve(par, L * KC, L, KC)
        par_ab = carve(par, 2 * L * KC, L, 48)
        par_lb = carve(par, 2 * L * KC + 48 * L, L, 4)
        par_c = carve(par, 2 * L * KC + 52 * L, KC, 2)
        npar = 2 * L * KC + 52 * L + 2 * KC
        assert npar == params.shape[1]

        o[0] = 0

        def tmp(*shape):
            v = carve(small, o[0], *shape)
            o[0] += int(np.prod(shape))
            return v

        ss, ms, lnv, rs, nt1, nt2 = (tmp(24) for _ in range(6))
        lbt, omlb = tmp(L, 4), tmp(L, 4)
        lam = tmp(L)
        A1 = tmp(2, KC, 2)
        sums = tmp(2, 2)
        mx, nmx = tmp(2, 2), tmp(2, 2)
        rsum = tmp(4, 2)
        rneg = tmp(2, 1)
        gdec = tmp(6, 2)
        e1 = tmp(KC, 2)
        lbe = tmp(L, 4)
        lbm = tmp(4)
        lm2 = tmp(L, 2)
        lme = tmp(L, 2)
        rtr_at = [0]

        def rtr(*shape):
            v = carve(attT[:, :, :].rearrange("p a b -> p (a b)"), rtr_at[0], *shape)
            rtr_at[0] += int(np.prod(shape))
            return v

        logit, score, selv = rtr(NT, NE), rtr(NT, NE), rtr(NT, NE)
        eqv, oh1, oh2, rest, slotc = (rtr(NT * 4, 4) for _ in range(5))
        slotf = rtr(NT, 2)
        posn, selm = rtr(NT, NE), rtr(NT, NE)
        cnt, novv, pin, pexc, ex2 = (rtr(NE) for _ in range(5))
        mat, mat2 = rtr(MAXOV, NE), rtr(MAXOV, NE)
        oeid, orow = rtr(MAXOV), rtr(MAXOV)
        m1, m2, gsc, gsel = (rtr(NT * 4) for _ in range(4))
        gm = rtr(NT)
        den = rtr(NT)
        gates = rtr(NT, NE)

        full = [sem(f"bank{b}_filled") for b in range(BANKS)]
        free = [sem(f"bank{b}_read_out") for b in range(BANKS)]
        landed = [sem(f"slot{s}_landed") for s in range(SLOTS)]
        d_x, d_const, d_par, d_row, d_out = (sem(n) for n in ("x_landed", "consts_landed", "params_landed", "rows_landed", "outputs_stored"))
        d_st, d_y = sem("scan_states_stored"), sem("y_stored")
        d_tabs = sem("masks_and_records_landed")
        d_skew = sem("skew_rows_written")
        d_tab, d_hrow, d_slot, d_lst = (sem(n) for n in ("table_cleared", "hidden_rows_stored", "slots_scattered", "slot_lists_landed"))
        d_yr = [sem(f"expert_rows_landed{t}") for t in range(NT)]
        d_g = [sem(f"gathered{i}") for i in range(2)]
        d_sc = [sem(f"expert_rows_stored{i}") for i in range(2)]
        s_sel, s_pay, s_ovt = (sem(n) for n in ("choices_ready", "slots_ready", "overflow_table_ready"))
        sync_passed, pool_passed = sem("sync_passed"), sem("pool_passed")
        ov = [{k: sem(f"ov{l}_{k}") for k in ("weights_landed", "tensor", "vector", "scalar", "list_landed", "gathered", "stored")} for l in range(L)]
        table = nc.dram_tensor("slot_table", (NE * T, 4), U32, kind="Internal").ap()
        hrow = nc.dram_tensor("hidden_rows", (T, D), F32, kind="Internal").ap()
        yrow = nc.dram_tensor("expert_rows", (2 * T, D), F32, kind="Internal").ap()
        skew = nc.dram_tensor("skew_rows", (L * H * RPB_H, GRID_W, RPER), F32, kind="Internal").ap()
        d_cache, d_state, d_bias, d_fin = (sem(n) for n in ("cache_landed", "state_landed", "bias_landed", "final_gain_landed"))
        ch_dve, ch_act, ch_pool = (sem(n) for n in ("vector_step", "scalar_step", "pool_step"))
        s_expc, s_sc, s_lbl, s_lbe = (sem(n) for n in ("exp_c_ready", "silu_c_ready", "init_exponents_ready", "init_exps_ready"))
        s_ss, s_ms, s_ln, s_xn = (sem(n) for n in ("sumsq_ready", "meansq_ready", "rstd_guess_ready", "xnorm_ready"))
        s_mod, s_e, s_f, s_lf = (sem(n) for n in ("modulation_ready", "exp_z_ready", "forget_ready", "log_forget_ready"))
        s_q, s_diff, s_dec, s_X, s_att = (sem(n) for n in ("q_ready", "exponents_ready", "decays_ready", "operands_ready", "b_scores_ready"))
        s_rope, s_bias, s_mx, s_pr, s_w = (sem(n) for n in ("rope_done", "bias_masked", "neg_max_ready", "c_latent_probs_ready", "weights_ready"))
        s_pss, s_pln, s_post = (sem(n) for n in ("sub_meansq_ready", "sub_rstd_guess_ready", "subnorm_ready"))
        s_rows = sem("modulation_blocks_read")
        s_diag, s_sq, s_rstd = sem("gate_diagonals_ready"), sem("head_squares_ready"), sem("head_rstd_ready")
        s_x, s_rl, s_re, s_y = (sem(n) for n in ("residual_done", "logits_ready", "router_exp_ready", "result_ready"))

        def bank(job, i=0):
            b, nth = place[job]
            return b, nth + i

        def begin(pe, job, i=0):
            b, nth = bank(job, i)
            if place[job][1] > 1:
                pe.wait_ge(free[b], nth - 1)
            return ps[:, b, :]

        def ready(eng, job, i=0):
            b, nth = bank(job, i)
            eng.wait_ge(full[b], nth)
            return ps[:, b, :]

        def moved(eng, job, i=0):
            b, nth = bank(job, i)
            eng.wait_ge(free[b], nth)

        def release(eng, ins, job, i=0):
            b, nth = bank(job, i)
            ins.then_inc(free[b], 1)
            eng.wait_ge(free[b], nth)

        last_job = {}
        for l in range(L):
            for j, job in zip(WIN_ORDER, [("z", l, 1, 1), ("av", l, 2), ("bvg", l, 2), ("aqk", l, 2), ("ck", l, 1), ("cvdu", l, 2)]):
                last_job[("win", l, j)] = job
            for j in range(2):
                last_job[("wout", l, j)] = ("wo", l, j, NT - 1)

        def block_read(sp, blk):
            if blk[0] == "ada":
                sp.wait_ge(s_rows, MOD_ORDER.index(blk[1:]) + 1)
            else:
                ready(sp, last_job[blk])

        EXPERT_LAST = ["a", "u", "dn1"]

        def exponents(eng, step, l, u):
            t, hp = UNITS[u]
            c2, out = C2[:, hp, t, :], dec[u % 2]
            for n, m in enumerate(LEVELS):
                M, nb = 2 * m, P // (2 * m)
                ref = strided(c2, m, [129, 2], [M, nb], [0, m])
                right, left = (strided(c2, 1 + o_, [P, 2], [M, nb], [1, m]) for o_ in (m, 0))
                step(eng.tensor_tensor(strided(out, n * 2 * P + m, [P, 2], [M, nb], [1, m]), right, ref, ALU.subtract))
                step(eng.tensor_tensor(strided(out, n * 2 * P, [P, 2], [M, nb], [1, m]), ref, left, ALU.subtract))
            at = NLEV * 2 * P
            step(eng.tensor_copy(out[:, at:at + P], c2[:, 1:129]))
            step(eng.tensor_copy(out[:, at + 3 * P:at + 4 * P], c2[:, 129:257]))
            step(eng.tensor_scalar(out[:, at + P:at + 2 * P], c2[:, 129:257], -1.0, c2[:, 257:258], ALU.mult, ALU.add))
            step(eng.tensor_scalar(out[:, at + 2 * P:at + 3 * P], c2[:, 1:129], -1.0, c2[:, 128:129], ALU.mult, ALU.add))
            eng.tensor_copy(out[:, at + 4 * P:at + 4 * P + 2], strided(c2, 128, [129, 2])).then_inc(s_diff, 1)
            eng.wait_ge(s_diff, l * len(UNITS) + u + 1)

        def gate_of(e):
            at = slice(e, e + 1) if isinstance(e, int) else bass.ds(e, 1)
            return lst[:, at, 2].bitcast(F32)

        def stored(eng, l, i, c):
            n = 16 * (NE // 2 * l + c // 2)
            if isinstance(i, int):
                if n + 16 * (EXP_PER_BODY // 2) * i > 0:
                    eng.wait_ge(d_sc[c % 2], n + 16 * (EXP_PER_BODY // 2) * i)
            else:
                eng.wait_ge(d_sc[c % 2], i * (16 * (EXP_PER_BODY // 2)) + n)

        block = ctx.enter_context(nc.Block())

        @block.sync
        def _(sp):
            sp.dma_start(par[:, :], params).then_inc(d_par, 16)
            for l in range(L):
                for i_n, (kind, m, j) in enumerate(PRE[l]):
                    n = FIRST_BLOCK[l] + i_n
                    if i_n >= SLOTS:
                        block_read(sp, PRE[l][i_n - SLOTS])
                    elif n >= SLOTS:
                        q = 3 * NE - SLOTS + i_n
                        ready(sp, (EXPERT_LAST[q % 3], l - 1), q // 3)
                    if l and i_n == 1:
                        for t in range(NT):
                            sp.wait_ge(d_yr[t], 16 * l)
                    if kind == "ada":
                        src = ada_w[m, :, j * 512:(j + 1) * 512]
                    elif kind == "win":
                        src = w_in[l, :, j * 512:(j + 1) * 512]
                    else:
                        src = w_out[l, :, j * 512:(j + 1) * 512]
                    sp.dma_start(ring[:, n % SLOTS, :].rearrange("p (k n) -> p k n", k=KC),
                                 src.rearrange("(k p) n -> p k n", p=P)).then_inc(landed[n % SLOTS], 16)
                gview = moe_w_gate[l].rearrange("e (k p) n -> e p k n", p=P)
                uview = moe_w_up[l].rearrange("e (k p) n -> e p k n", p=P)
                dview = moe_w_down[l].rearrange("e (k p) n -> e p k n", p=P)

                def expert_block(e, i, q, first):
                    slot = (len(PRE[l]) + q) % SLOTS
                    if first and q < SLOTS:
                        block_read(sp, PRE[l][len(PRE[l]) - SLOTS + q])
                    else:
                        back = q - SLOTS
                        ready(sp, (EXPERT_LAST[back % 3], l), i * EXP_PER_BODY + back // 3)
                        if not first:
                            sp.wait_ge(d_par, 16)
                    src = (gview, uview, dview)[q % 3][e]
                    dst = ring[:, slot, :].rearrange("p (k n) -> p k n", k=(KC, KC, FC)[q % 3])
                    sp.dma_start(dst, src).then_inc(landed[slot], 16)

                for q in range(3 * EXP_PER_BODY):
                    expert_block(q // 3, 0, q, True)
                with sp.Fori(1, NBODY) as i:
                    for q in range(3 * EXP_PER_BODY):
                        expert_block(i * EXP_PER_BODY + q // 3, i, q, False)
                o_ = ov[l]
                ready(sp, ("dn1", l), NE - 1)
                sp.wait_ge(s_ovt, l + 1)
                n_ov = sp.value_load(ovt[0:1, 0:1], min_val=0, max_val=MAXOV)
                with sp.If(n_ov > 0):
                    with sp.Fori(0, n_ov) as r:
                        e = sp.value_load(ovt[0:1, bass.ds(r + 1, 1)], min_val=0, max_val=NE - 1)
                        for q, view in enumerate((gview, uview, dview)):
                            dst = ring[:, q, :].rearrange("p (k n) -> p k n", k=(KC, KC, FC)[q])
                            sp.dma_start(dst, view[e]).then_inc(o_["weights_landed"], 16)
                        sp.wait_ge(o_["tensor"], 4 * r + 4)
                        sp.sem_inc(sync_passed, 1)
            sp.wait_ge(s_y, 1)
            sp.dma_start(y_prompt[0], xn[:, 0, :]).then_inc(d_y, 16)
            sp.dma_start(y_sample[0].rearrange("(t p) d -> p t d", p=P), xn[:, 1:3, :]).then_inc(d_y, 16)
            sp.wait_ge(d_y, 32)
            sp.wait_ge(d_out, 16 * 4 * L)

        @block.gpsimd
        def _(pool):
            n_pool = [0]

            def step(ins):
                n_pool[0] += 1
                ins.then_inc(ch_pool, 1)
                pool.wait_ge(ch_pool, n_pool[0])

            pool.dma_start(const[:, :], consts).then_inc(d_const, 16)
            pool.dma_start(mflat[:, 0:L * 128], diff_lambda.rearrange('l a d -> (l a d)').partition_broadcast(P)).then_inc(d_row, 16)
            pool.dma_start(gsub[:, 0, :, :], diff_subln_g.partition_broadcast(P)).then_inc(d_row, 16)
            pool.dma_start(gsub[:, 1, :, :], hgrn_norm_g.partition_broadcast(P)).then_inc(d_row, 16)
            pool.dma_start(mk[:, :, :], masks.rearrange("p (g n) -> p g n", g=GRAM)).then_inc(d_tabs, 16)
            pool.dma_start(pay[:, :, :, :], slots0[:, 4 * NE * NT:].rearrange("p (t k w) -> p t k w", t=NT, k=2)).then_inc(d_tabs, 16)
            pool.dma_start(wrt[:, :, :], router_w.rearrange("(k p) n -> p k n", p=P)).then_inc(d_row, 16)
            pool.dma_start(rbias[:, :], router_b.partition_broadcast(P)).then_inc(d_row, 16)
            for l in range(L):
                if l:
                    moved(pool, ("ao", l - 1, len(ATT) - 1))
                for n, src in enumerate((cache_diff_k, cache_diff_v, cache_na_k, cache_na_v)):
                    pool.dma_start(cachek[:, n, :, :], src[0, l].rearrange("h p d -> p h d")).then_inc(d_cache, 16)
                for hp in range(HP):
                    for d in range(2):
                        pool.dma_start(S0[:, hp, d, :], state_hgrn[0, l, d, 2 * hp:2 * hp + 2].rearrange("h k v -> (h k) v")).then_inc(d_state, 16)
                if l == 0:
                    ready(pool, ("av", 0, 2))
                    pool.dma_start(skew, rpb_pad.unsqueeze(1).broadcast_to([L * H * RPB_H, GRID_W, RPER])).then_inc(d_skew, 16)
                def later_exponents(u):
                    ready(pool, ("gram", l, u - 2, 1, 3))
                    exponents(pool, step, l, u)

                later_exponents(2)
                later_exponents(3)
                for t in range(NT):
                    moved(pool, ("aqk", l, t))
                if l:
                    pool.wait_ge(d_st, 16 * HP * 2 * l)
                    pool.wait_ge(d_out, 16 * 4 * l)
                qk = tok[:, 1:3, 0:512]
                for t in range(2):
                    v = qk[:, t, :].rearrange("p (g r) -> p g r", r=32)
                    pr = qk[:, t, :].rearrange("p (g r two) -> p g r two", r=16, two=2)
                    rr = rtmp[:, :].rearrange("p (g r two) -> p g r two", r=16, two=2)
                    sn = ropes[:, t, :].unsqueeze(1).broadcast_to([P, 16, 16])
                    step(pool.tensor_tensor(rr[:, :, :, 0], pr[:, :, :, 1], sn, ALU.mult))
                    step(pool.tensor_tensor(rr[:, :, :, 1], pr[:, :, :, 0], sn, ALU.mult))
                    step(pool.tensor_tensor(v, v, ropec[:, t, :].unsqueeze(1).broadcast_to([P, 16, 32]), ALU.mult))
                    step(pool.tensor_tensor(pr[:, :, :, 0], pr[:, :, :, 0], rr[:, :, :, 0], ALU.subtract))
                    step(pool.tensor_tensor(pr[:, :, :, 1], pr[:, :, :, 1], rr[:, :, :, 1], ALU.add))
                pool.engine_nop().then_inc(s_rope, 1)
                later_exponents(4)
                later_exponents(5)
                if l == 0:
                    pool.wait_ge(d_skew, 16)
                for h in range(H):
                    for qt in range(2):
                        for r2 in range(2):
                            at = ((l * H + h) * RPB_H + 7 - 2 * qt - r2) * GRID_W * RPER + GRID_W - 1
                            src = bass.AP(skew.tensor, skew.offset + at, [[RPER - 1, GRID_W], [GRID_W * RPER, 4], [1, GRID_W]])
                            pool.dma_start(bias[64 * r2:64 * r2 + 64, h, qt, :, :], src).then_inc(d_bias, 16)
                pool.wait_ge(d_const, 16)
                pool.wait_ge(d_bias, 256 * (l + 1))
                bv3 = bias[:, :, :, :, :].rearrange("p h q r c -> p (h q r) c")
                pool.tensor_tensor(bv3, bv3, namask.unsqueeze(1).broadcast_to([P, 32, GRID_W]), ALU.add).then_inc(s_bias, 1)
                moved(pool, ("cvdu", l, 0))
                for dst, c0 in ((new_diff_k, AK), (new_diff_v, AV), (new_na_v, CV)):
                    pool.dma_start(dst[0, l].rearrange("h p d -> p h d"),
                                   tok[:, 0, c0:c0 + 256].rearrange("p (h d) -> p h d", h=H)).then_inc(d_out, 16)
                moved(pool, ("nk", l))
                pool.dma_start(new_na_k[0, l].rearrange("h p d -> p h d"), nkout).then_inc(d_out, 16)
                moved(pool, ("kv", l, 0))
                moved(pool, ("kv", l, 1))
                for n in range(HP * 2):
                    hp, d = n // 2, n % 2
                    pool.dma_start(new_state[0, l, d, 2 * hp:2 * hp + 2].rearrange("h k v -> (h k) v"),
                                   stout[:, hp, d, :]).then_inc(d_st, 16)
                for n, o_ in enumerate((oB, oA)):
                    if n == 0:
                        for t in range(NT):
                            for h2 in range(2):
                                moved(pool, ("bo", l, t, h2))
                    else:
                        for i in range(LAST_A - 1, LAST_A + 1):
                            moved(pool, ("ao", l, i))
                    pool.tensor_tensor(squares, o_, o_, ALU.mult).then_inc(s_sq, 1)
                    pool.wait_ge(s_rstd, 2 * l + n + 1)
                    r0 = 12 * (1 - n)
                    step(pool.tensor_tensor(o_, o_, rs[:, r0:r0 + 12].unsqueeze(2).broadcast_to([P, 12, 64]), ALU.mult))
                    ins = pool.tensor_tensor(o_, o_, gsub[:, 1 - n, l, :].unsqueeze(1).broadcast_to([P, 12, 64]), ALU.mult)
                    if n == 0:
                        step(ins)
                        ob = o_.rearrange("p (t h) c -> p t (h c)", t=NT)
                        ins = pool.tensor_tensor(ob, ob, tok[:, :, BG:BG + 256], ALU.mult)
                    ins.then_inc(s_post, 1)
                pool.dma_start(table.rearrange("(p r) w -> p (r w)", p=P), slots0[:, 0:4 * NE * NT]).then_inc(d_tab, 16)
                pool.wait_ge(d_tab, 16 * (l + 1))
                pool.wait_ge(s_pay, l + 1)
                for t in range(NT):
                    for k in range(2):
                        pool.indirect_dma_start(table, bass.IndirectOffsetOnAxis(slotu[:, t, k:k + 1], 0), pay[:, t, k, :],
                                                None).then_inc(d_slot, 16)
                pool.wait_ge(d_slot, 16 * 2 * NT * (l + 1))
                pool.dma_start(lst[:, :, :], table.rearrange("(e s) w -> s e w", e=NE)[0:CAP]).then_inc(d_lst, 16)
                pool.wait_ge(d_lst, 16 * (l + 1))
                pool.wait_ge(d_hrow, 16 * (l + 1))

                def gather(e):
                    pool.indirect_dma_start(xg[:, e % 2, :], None, hrow, bass.IndirectOffsetOnAxis(lst[:, e, 0:1], 0)).then_inc(d_g[e % 2], 16)

                gather(0)
                gather(1)
                for e in range(NE + 1):
                    if e + 2 < NE:
                        ready(pool, ("xt1", l), e)
                        gather(e + 2)
                    if e:
                        moved(pool, ("dn0", l), e - 1)
                        moved(pool, ("dn1", l), e - 1)
                        pool.indirect_dma_start(yrow, bass.IndirectOffsetOnAxis(lst[:, e - 1, 1:2], 0), ybuf[:, (e - 1) % 2, :], None,
                                                bounds_check=2 * T - 1, oob_is_err=False).then_inc(d_sc[(e - 1) % 2], 16)
                o_ = ov[l]
                pool.wait_ge(s_ovt, l + 1)
                n_ov = pool.value_load(ovt[0:1, 0:1], min_val=0, max_val=MAXOV)
                with pool.If(n_ov > 0):
                    for b in range(2):
                        pool.wait_ge(d_sc[b], 16 * (NE // 2) * (l + 1))
                    with pool.Fori(0, n_ov) as r:
                        row = pool.value_load(ovt[0:1, bass.ds(r + (1 + MAXOV), 1)], min_val=0, max_val=(NE - 1) * T + 2 * CAP)
                        pool.dma_start(lsto[:, :], table[bass.ds(row, CAP)]).then_inc(o_["list_landed"], 16)
                        pool.wait_ge(o_["list_landed"], 16 * r + 16)
                        pool.sem_inc(pool_passed, 1)
                        pool.indirect_dma_start(xg[:, 0, :], None, hrow, bass.IndirectOffsetOnAxis(lsto[:, 0:1], 0)).then_inc(o_["gathered"], 16)
                        pool.wait_ge(o_["vector"], 4 * r + 4)
                        pool.sem_inc(pool_passed, 1)
                        pool.indirect_dma_start(yrow, bass.IndirectOffsetOnAxis(lsto[:, 1:2], 0), ybuf[:, 0, :], None,
                                                bounds_check=2 * T - 1, oob_is_err=False).then_inc(o_["stored"], 16)
                        pool.wait_ge(o_["stored"], 16 * r + 16)
                        pool.sem_inc(pool_passed, 1)
                for b in range(2):
                    pool.wait_ge(d_sc[b], 16 * (NE // 2) * (l + 1))
                for t in range(NT):
                    pool.dma_start(yr[:, t, :, :], yrow[2 * t * P:2 * (t + 1) * P].rearrange("(p k) d -> p k d", k=2)).then_inc(d_yr[t], 16)
            pool.wait_ge(s_x, NT * 2 * L)
            pool.dma_start(gate[:, 0, :], final_norm_g.partition_broadcast(P)).then_inc(d_fin, 16)
            pool.wait_ge(d_st, 16 * HP * 2 * L)

        @block.scalar
        def _(act):
            n_act = [0]

            def step(ins):
                n_act[0] += 1
                ins.then_inc(ch_act, 1)
                act.wait_ge(ch_act, n_act[0])

            def rstd_guess(a, b, s_in, n_in, s_done):
                act.wait_ge(s_in, n_in)
                step(act.activation(lnv[:, a:b], ms[:, a:b], ACT.Ln))
                act.activation(rs[:, a:b], lnv[:, a:b], ACT.Exp, scale=-0.5).then_inc(s_done, 1)

            def sum_squares(n):
                for t in range(NT):
                    if n:
                        act.wait_ge(s_x, NT * (n - 1) + t + 1)
                    elif t == 0:
                        act.wait_ge(d_x, 32)
                    ins = act.activation(junk, x[:, t, :], ACT.Square, accum_out=ss[:, t:t + 1])
                    if t < NT - 1:
                        step(ins)
                    else:
                        ins.then_inc(s_ss, 1)
                rstd_guess(0, NT, s_ms, n + 1, s_ln)

            def gate_copy(l, which):
                for s in range(2):
                    for b in range(2):
                        p = ready(act, ("gbc", l, which, s, b))
                        release(act, act.activation(gate[:, s, b * 512:(b + 1) * 512], p, ACT.Copy), ("gbc", l, which, s, b))

            def rows_out(q, rows=rows):
                if q:
                    ready(act, ("mod", q - 1))
                act.wait_ge(s_rows, 4 * (q + 1))
                act.activation(rows, ps[:, MOD_BANK, :], ACT.Copy).then_inc(free[MOD_BANK], 1)

            def modulate(l, which):
                act.wait_ge(s_mod, 2 * l + which + 1)
                for k in range(1, KC, 2):
                    job = ("hT", 2 * l + which, k)
                    p = ready(act, job)
                    for s, (a, b) in enumerate(((0, P), (P, T))):
                        ins = act.activation(hT[:, k, a:b], p[:, a:b], ACT.Identity, scale=A1[:, which, k, s:s + 1],
                                             bias=modv[:, l, 3 * KC * which + k, s:s + 1])
                        if s == 0:
                            step(ins)
                    release(act, ins, job)

            def copy_out(dst, job, cols=None, src=None):
                p = ready(act, job)
                release(act, act.activation(dst, p[:, 0:cols] if src is None else src(p), ACT.Copy), job)

            act.dma_start(x[:, 0, :], x_prompt[0]).then_inc(d_x, 16)
            act.dma_start(x[:, 1:3, :], x_sample[0].rearrange("(t p) d -> p t d", p=P)).then_inc(d_x, 16)
            act.wait_ge(d_par, 16)
            act.activation(e1, par_c, ACT.Exp, scale=-1.0).then_inc(s_expc, 1)
            for l in range(L):
                sum_squares(2 * l)
                if l == 0:
                    rows_out(0)
                modulate(l, 0)
                if l == 0:
                    act.wait_ge(s_lbl, 1)
                    act.activation(lbe, lbe, ACT.Exp).then_inc(s_lbe, 1)
                    act.activation(lme, lm2, ACT.Exp).then_inc(s_lbe, 1)
                for d in range(2):
                    for hp in range(HP):
                        moved(act, ("z", l, d, hp))
                act.activation(E, Z, ACT.Exp, scale=-1.0).then_inc(s_e, 1)
                for hp in range(HP):
                    p = ready(act, ("bq", l, hp))
                    release(act, act.activation(qT[:, hp, :], p[:, 0:T], ACT.Silu), ("bq", l, hp))
                for t in range(NT):
                    copy_out(tok[:, t, AV:AV + 256], ("av", l, t), 256)
                act.wait_ge(s_f, l + 1)
                act.activation(F, F, ACT.Ln).then_inc(s_lf, 1)

                def decays(u):
                    act.wait_ge(s_diff, l * len(UNITS) + u + 1)
                    act.activation(dec[u % 2], dec[u % 2], ACT.Exp).then_inc(s_dec, 1)

                def fill_in(at):
                    n = filler(l, at)
                    if n is not None and n % 4 == 3:
                        rows_out(group(*BETWEEN[l][n]))

                def keys_out(u):
                    copy_out(kdT[:, u % 2, 0:2 if UNITS[u][0] == 0 else 1, :].rearrange("p a b -> p (a b)"), ("kd", l, u),
                             (2 if UNITS[u][0] == 0 else 1) * P)

                def by_tokens(job, c0, t):
                    copy_out(tok[:, t, c0:c0 + 512], (job, l, t), 512)

                def values_out(t):
                    p = ready(act, ("bvg", l, t))
                    act.activation(tok[:, t, BV:BV + 256], p[:, 0:256], ACT.Copy)
                    release(act, act.activation(tok[:, t, BG:BG + 256], p[:, 256:512], ACT.Silu), ("bvg", l, t))

                values_out(0)
                values_out(1)
                decays(0)
                values_out(2)
                decays(1)
                by_tokens("aqk", 0, 0)
                keys_out(0)
                by_tokens("aqk", 0, 1)
                by_tokens("aqk", 0, 2)
                decays(2)
                keys_out(1)
                for hp in range(HP):
                    copy_out(cqT[:, hp, :], ("cq", l, hp), T)
                decays(3)
                keys_out(2)
                for hp in range(HP):
                    p = ready(act, ("ck", l, hp))
                    step(act.activation(ckT[:, hp, 0:P], p[:, 0:P], ACT.Copy))
                    release(act, act.activation(ckT[:, hp, 2 * P:4 * P], p[:, P:T], ACT.Copy), ("ck", l, hp))
                decays(4)
                keys_out(3)
                by_tokens("cvdu", CV, 0)
                by_tokens("cvdu", CV, 1)
                decays(5)
                keys_out(4)
                fill_in(("B", 8))
                fill_in(("B", 9))
                by_tokens("cvdu", CV, 2)
                for c in range(2):
                    copy_out(Ud[:, c, 0:256], ("du", l, c, 0), 256)
                    copy_out(Ud[:, c, 256:768], ("du", l, c, 1), 512)
                for c in range(2):
                    copy_out(hT[:, 6 + c, :], ("dy", l, c), T)
                copy_out(ckT[:, :, P:2 * P], ("cc", l), src=lambda p: p[:, 0:256].rearrange("p (a b) -> p a b", a=HP))
                act.wait_ge(s_rope, l + 1)
                copy_out(rtmp[:, 0:256], ("nk", l), 256)
                keys_out(5)
                fill_in(("B", 10))
                fill_in(("B", 11))
                for t in range(NT):
                    for h2 in range(2):
                        copy_out(oB[:, t * H + h2:(t + 1) * H:2, :], ("bo", l, t, h2),
                                 src=lambda p: p[:, 0:P].rearrange("p (a b) -> p a b", a=HP))
                for hp in range(HP):
                    copy_out(aqT[:, hp, :], ("aT", l, 0, hp), T)
                for hp in range(HP):
                    copy_out(akT[:, hp, :], ("aT", l, 1, hp), 4 * P)
                for i in range(len(ATT) + 3):
                    if i < len(ATT):
                        m, t, h = ATT[i]
                        nk = T if t else P
                        act.wait_ge(s_mx, l * len(ATT) + i + 1)
                        if i >= 2:
                            ready(act, ("pT", l, i - 2))
                        if m == "C" and t:
                            act.activation(prob[:, i % 2, 0, 0:nk], scb[:, i % 2, 0:nk], ACT.Exp, bias=nmx[:, i % 2, 0:1],
                                           accum_out=sums[:, i % 2, 0:1]).then_inc(s_pr, 1)
                        else:
                            scale = 32 ** -0.5 if m == "A" else 64 ** -0.5
                            for mp in range(2 if m == "A" else 1):
                                p = ready(act, ("sc", l, i, mp))
                                release(act, act.activation(prob[:, i % 2, mp, 0:nk], p[:, 0:nk], ACT.Exp, scale=scale,
                                                            bias=nmx[:, i % 2, mp:mp + 1],
                                                            accum_out=sums[:, i % 2, mp:mp + 1]), ("sc", l, i, mp))
                    if 0 <= i - 2 < len(ATT):
                        nk = T if ATT[i - 2][1] else P
                        copy_out(wT[:, i % 2, 0:nk], ("pT", l, i - 2), nk)
                    if i >= 3:
                        m, t, h = ATT[i - 3]
                        p = ready(act, ("ao", l, i - 3))
                        act.wait_ge(s_w, l * len(ATT) + i - 2)
                        dst = (oA if m == "A" else oC)[:, t * H + h, :]
                        release(act, act.activation(dst, p[:, 0:64], ACT.Copy, scale=rsum[:, (i - 3) % 4, 0:1]), ("ao", l, i - 3))
                    fill_in(("AC", i))
                    if i == NORM_B + 1:
                        rstd_guess(12, 24, s_pss, 2 * l + 1, s_pln)
                    if i == NORM_A + 1:
                        rstd_guess(0, 12, s_pss, 2 * l + 2, s_pln)
                for c in range(1, 6, 2):
                    copy_out(hT[:, c, :], ("mT", l, c), T)
                ready(act, ("mod", group(*BETWEEN[l][-1])))
                act.wait_ge(d_st, 16 * HP * 2 * (l + 1))
                gate_copy(l, 0)
                act.wait_ge(d_out, 16 * 4 * (l + 1))
                sum_squares(2 * l + 1)
                gate_copy(l, 1)
                modulate(l, 1)
                for t in range(NT):
                    copy_out(htok[:, t, 512:], ("hb", l, t, 1))
                for t in range(NT):
                    moved(act, ("hb", l, t, 0))
                act.dma_start(hrow.rearrange("(t p) d -> p t d", p=P), htok).then_inc(d_hrow, 16)
                act.wait_ge(s_rl, l + 1)
                act.activation(score, logit, ACT.Exp, scale=-1.0).then_inc(s_re, 1)
                if AHEAD[l]:
                    rows_out(group(*AHEAD[l][-1]), rows2)
                act.wait_ge(d_lst, 16 * (l + 1))

                def copy(dst, job, e):
                    p = ready(act, job, e)
                    release(act, act.activation(dst, p, ACT.Copy), job, e)

                def expert(i, es, first=False, last=False):
                    e = i * EXP_PER_BODY + es
                    if not last:
                        copy(hTg[:, 4:8, :].rearrange("p a b -> p (a b)"), ("xt1", l), e)
                    if not first:
                        copy(zTg.rearrange("p a b -> p (a b)"), ("zt", l), e - 1)
                    if not last:
                        p = ready(act, ("a", l), e)
                        release(act, act.activation(sS, p, ACT.Silu), ("a", l), e)
                    if not first:
                        p = ready(act, ("dn0", l), e - 1)
                        stored(act, l, i, es - 1)
                        release(act, act.activation(ybuf[:, (es - 1) % 2, 0:512], p, ACT.Copy, scale=gate_of(e - 1)), ("dn0", l), e - 1)

                for e in range(EXP_PER_BODY):
                    expert(0, e, first=(e == 0))
                with act.Fori(1, NBODY) as i:
                    for e in range(EXP_PER_BODY):
                        expert(i, e)
                expert(NBODY, 0, last=True)
                o_ = ov[l]
                act.wait_ge(s_ovt, l + 1)
                n_ov = act.value_load(ovt[0:1, 0:1], min_val=0, max_val=MAXOV)
                with act.If(n_ov > 0):
                    with act.Fori(0, n_ov) as r:
                        act.wait_ge(o_["tensor"], 4 * r + 2)
                        act.activation(sS, ps[:, 2, :], ACT.Silu).then_inc(o_["scalar"], 1)
            sum_squares(2 * L)

        @block.vector
        def _(dve):
            n_dve = [0]

            def step(ins):
                n_dve[0] += 1
                ins.then_inc(ch_dve, 1)
                dve.wait_ge(ch_dve, n_dve[0])

            def newton(c0, c1):
                a, r = nt1[:, c0:c1], rs[:, c0:c1]
                step(dve.tensor_tensor(a, r, r, ALU.mult))
                step(dve.tensor_tensor(a, a, ms[:, c0:c1], ALU.mult))
                step(dve.tensor_scalar(a, a, -0.5, 1.5, ALU.mult, ALU.add))
                step(dve.tensor_tensor(r, r, a, ALU.mult))

            def normalize(n):
                dve.wait_ge(s_ss, n + 1)
                dve.tensor_scalar(ms[:, 0:NT], ss[:, 0:NT], 1.0 / D, EPS, ALU.mult, ALU.add).then_inc(s_ms, 1)
                dve.wait_ge(s_ms, n + 1)
                dve.wait_ge(s_ln, n + 1)
                newton(0, NT)
                for t in range(NT):
                    ins = dve.tensor_scalar(xn[:, t, :], x[:, t, :], rs[:, t:t + 1], None, ALU.mult)
                    if t < NT - 1:
                        step(ins)
                ins.then_inc(s_xn, 1)
                dve.wait_ge(s_xn, n + 1)

            def modulation(q):
                l, g = MOD_ORDER[4 * q][0], MOD_ORDER[4 * q][1] // 4
                p = ready(dve, ("mod", q))
                out = modv[:, l, 16 * g:16 * g + 16, :].rearrange("p (b c) s -> p b c s", b=4)
                b = par_ab[:, l, 16 * g:16 * g + 16].rearrange("p (b c) -> p b c", b=4).unsqueeze(3).broadcast_to([P, 4, 4, 2])
                release(dve, dve.tensor_tensor(out, p[:, 0:32].rearrange("p (c b s) -> p b c s", b=4, s=2), b, ALU.add), ("mod", q))

            def gate_diagonals(l, which):
                for n in range(4):
                    s, b = n // 2, n % 2
                    if n >= 2:
                        ready(dve, ("gbc", l, which, (n - 2) // 2, b))
                    g = modv[:, l, (2 + 3 * which) * KC + 4 * b:(2 + 3 * which) * KC + 4 * b + 4, s:s + 1]
                    dve.tensor_tensor(diag[:, b, :, :], ident.unsqueeze(1).broadcast_to([P, 4, P]), g.broadcast_to([P, 4, P]),
                                      ALU.mult).then_inc(s_diag, 1)
                dve.wait_ge(s_diag, 8 * l + 4 * which + 4)

            def scales(l, which):
                a = A1[:, which, :, :]
                sc1 = modv[:, l, (1 + 3 * which) * KC:(2 + 3 * which) * KC, :]
                step(dve.tensor_scalar(a, sc1, 1.0, None, ALU.add))
                g = (par_g1, par_g2)[which]
                dve.tensor_tensor(a, a, g[:, l, :].unsqueeze(2).broadcast_to([P, KC, 2]), ALU.mult).then_inc(s_mod, 1)
                dve.wait_ge(s_mod, 2 * l + which + 1)

            def modulate(l, which):
                for k in range(0, KC, 2):
                    job = ("hT", 2 * l + which, k)
                    p = ready(dve, job)
                    for s, (a, b) in enumerate(((0, P), (P, T))):
                        ins = dve.tensor_scalar(hT[:, k, a:b], p[:, a:b], A1[:, which, k, s:s + 1],
                                                modv[:, l, 3 * KC * which + k, s:s + 1], ALU.mult, ALU.add)
                        if s == 0:
                            step(ins)
                    release(dve, ins, job)

            def operands(l, u):
                t, hp = UNITS[u]
                d_, q0, k0 = dec[u % 2], qT[:, hp, t * P:(t + 1) * P], kT[:, 0, hp, t * P:(t + 1) * P]
                dve.wait_ge(s_dec, l * len(UNITS) + u + 1)
                for n, m in enumerate(LEVELS):
                    M, nb, base = 2 * m, P // (2 * m), n * 2 * P
                    o_ = strided(d_, base + m, [P - m, 2], [M, nb], [1, m])
                    step(dve.tensor_tensor(o_, o_, strided(q0, m, [-m, 2], [M, nb], [1, m]), ALU.mult))
                    o_ = strided(d_, base, [P + m, 2], [M, nb], [1, m])
                    step(dve.tensor_tensor(o_, o_, strided(k0, 0, [HP * T + m, 2], [M, nb], [1, m]), ALU.mult))
                at = NLEV * 2 * P
                if t:
                    step(dve.tensor_tensor(qdec[:, t - 1, hp, :, :], strided(d_, at, [P, 2], [1, P]),
                                           q0.unsqueeze(1).broadcast_to([P, 2, P]), ALU.mult))
                kk = strided(d_, at + 2 * P, [P, 2], [1, P])
                step(dve.tensor_tensor(kk, kk, strided(k0, 0, [HP * T, 2], [1, P]), ALU.mult))
                step(dve.tensor_copy(gdec[:, u, :], d_[:, at + 4 * P:at + 4 * P + 2]))
                dve.tensor_tensor(d_[:, at:at + P], k0, kT[:, 1, hp, t * P:(t + 1) * P], ALU.add).then_inc(s_X, 1)
                dve.wait_ge(s_X, l * len(UNITS) + u + 1)

            def masked_scores(l, u, h2):
                dst = attT[:, 2 * u + h2, :]
                for half in range(2):
                    for g in (2 * half, 2 * half + 1):
                        n = min(4, GRAM - 4 * g)
                        p = ready(dve, ("gram", l, u, h2, g))
                        release(dve, dve.tensor_tensor(mprod[:, 4 * (g % 2):4 * (g % 2) + n, :],
                                                       p[:, 0:n * P].rearrange("p (a b) -> p a b", a=n),
                                                       mk[:, 4 * g:4 * g + n, :], ALU.mult), ("gram", l, u, h2, g))
                    n = 8 - half
                    red = mprod[:, 0:n, :].rearrange("p a b -> p b a")
                    if half == 0:
                        step(dve.tensor_reduce(dst, red, AX, ALU.add))
                    else:
                        step(dve.tensor_reduce(mprod[:, 7, :], red, AX, ALU.add))
                dve.tensor_tensor(dst, dst, mprod[:, 7, :], ALU.add).then_inc(s_att, 1)
                dve.wait_ge(s_att, (l * len(UNITS) + u) * 2 + h2 + 1)

            def states(l, u):
                t, hp = UNITS[u]
                job = ("kv", l, u)
                p = ready(dve, job)
                if t:
                    dve.wait_ge(d_state, 16 * 4 * (l + 1))
                for h2 in range(2):
                    r = slice(64 * h2, 64 * h2 + 64)
                    if t == 0:
                        ins = dve.tensor_copy(stout[r, hp, :, :], p[r, 0:2 * P].rearrange("p (d c) -> p d c", d=2)[:, :, 64 * h2:64 * h2 + 64])
                    else:
                        ins = dve.scalar_tensor_tensor(out=S1[r, hp, t - 1, :], in0=S0[r, hp, t - 1, :],
                                                       scalar=gdec[r, u, t - 1:t], in1=p[r, 64 * h2:64 * h2 + 64],
                                                       op0=ALU.mult, op1=ALU.add)
                    if h2 == 0:
                        step(ins)
                release(dve, ins, job)

            step(dve.memset(scp[:, :, :], 0.0))
            dve.wait_ge(s_expc, 1)
            step(dve.tensor_scalar(e1, e1, 1.0, None, ALU.add))
            step(dve.reciprocal(e1, e1))
            dve.wait_ge(d_par, 16)
            dve.tensor_tensor(scp[:, :, 6:8], par_c, e1, ALU.mult).then_inc(s_sc, 1)
            dve.wait_ge(d_const, 16)
            for l in range(L):
                normalize(2 * l)
                if l == 0:
                    modulation(0)
                scales(l, 0)
                modulate(l, 0)
                if l == 0:
                    dve.wait_ge(d_row, 16 * 5)
                    step(dve.tensor_tensor(lbm, par_lb[:, 0, :], par_lb[:, 1, :], ALU.max))
                    step(dve.tensor_tensor(lbe, par_lb, lbm.unsqueeze(1).broadcast_to([P, L, 4]), ALU.subtract))
                    step(dve.tensor_tensor(lamt[:, :, 0::2, :], lamt[:, :, 0::2, :], lamt[:, :, 1::2, :], ALU.mult))
                    dve.tensor_reduce(lm2, lamt[:, :, 0::2, :], AX, ALU.add).then_inc(s_lbl, 1)
                    dve.wait_ge(s_lbe, 2)
                    step(dve.tensor_tensor(lbm, lbe[:, 0, :], lbe[:, 1, :], ALU.add))
                    step(dve.reciprocal(lbm, lbm))
                    step(dve.tensor_tensor(lbe, lbe, lbm.unsqueeze(1).broadcast_to([P, L, 4]), ALU.mult))
                    step(dve.tensor_tensor(lbt[:, 0, :], lbe[:, 0, :], lbe[:, 0, :], ALU.subtract))
                    step(dve.tensor_tensor(lbt[:, 1, :], lbt[:, 0, :], lbe[:, 1, :], ALU.add))
                    step(dve.tensor_scalar(omlb, lbt, -1.0, 1.0, ALU.mult, ALU.add))
                    for m in range(L):
                        lam_init = 0.8 - 0.6 * math.exp(-0.3 * m)
                        step(dve.tensor_tensor(lam[:, m:m + 1], lme[:, m, 1:2], lme[:, m, 0:1], ALU.subtract))
                        step(dve.tensor_scalar(lam[:, m:m + 1], lam[:, m:m + 1], -lam_init, None, ALU.add))
                        step(dve.tensor_scalar(gsub[:, 0, m, :], gsub[:, 0, m, :], 1.0 - lam_init, None, ALU.mult))
                for d in range(2):
                    for hp in range(HP):
                        p = ready(dve, ("z", l, d, hp))
                        release(dve, dve.tensor_scalar(Z[:, d, hp, :], p[:, 0:T], -80.0, None, ALU.max), ("z", l, d, hp))
                dve.wait_ge(s_e, l + 1)
                step(dve.tensor_scalar(Z, E, 1.0, None, ALU.add))
                step(dve.reciprocal(Z, Z))
                for d in range(2):
                    for hp in range(HP):
                        w = 2 * d + hp
                        step(dve.tensor_scalar(F[:, d, hp, :], Z[:, d, hp, :], omlb[:, l, w:w + 1], lbt[:, l, w:w + 1], ALU.mult, ALU.add))
                        step(dve.scalar_tensor_tensor(out=kT[:, d, hp, :], in0=E[:, d, hp, :], scalar=omlb[:, l, w:w + 1],
                                                      in1=Z[:, d, hp, :], op0=ALU.mult, op1=ALU.mult))
                dve.tensor_scalar(F, F, TINY, None, ALU.max).then_inc(s_f, 1)
                step(dve.memset(strided(C2[:, 0, 0, :], 0, [129, 2 * HP * NT]), 0.0))
                dve.wait_ge(s_lf, l + 1)
                for hp in range(HP):
                    for t in range(NT):
                        for d in range(2):
                            step(dve.tensor_tensor_scan(C2[:, hp, t, d * 129 + 1:d * 129 + 129], ones, F[:, d, hp, t * P:(t + 1) * P],
                                                        0.0, ALU.mult, ALU.add))

                def fill_in(at):
                    n = filler(l, at)
                    if n and n % 4 == 0:
                        modulation(group(*BETWEEN[l][n - 1]))

                dve.wait_ge(d_tabs, 32)
                for u in range(2):
                    exponents(dve, step, l, u)
                operands(l, 0)
                for u in range(len(UNITS)):
                    for h2 in range(2):
                        masked_scores(l, u, h2)
                        if h2 == 0:
                            states(l, u)
                        if h2 == 0 and u + 1 < len(UNITS):
                            operands(l, u + 1)
                        fill_in(("B", 2 * u + h2))
                n_clat = 0
                seen = {}
                for i in range(len(ATT) + 3):
                    if i < len(ATT):
                        m, t, h = ATT[i]
                        nk = T if t else P
                        if m == "C" and t:
                            n_clat += 1
                            seen[i] = n_clat
                            job = ("sc", l, i, 0)
                            p = ready(dve, job)
                            step(dve.tensor_scalar(scb[:, i % 2, 0:P], p[:, 0:P], 64 ** -0.5, None, ALU.mult))
                            dve.wait_ge(s_bias, l + 1)
                            release(dve, dve.scalar_tensor_tensor(
                                out=scb[:, i % 2, P:T], in0=p[:, P:T], scalar=64 ** -0.5,
                                in1=bias[:, h, t - 1, :, :].rearrange("p a b -> p (a b)"), op0=ALU.mult, op1=ALU.add), job)
                            step(dve.tensor_reduce(mx[:, i % 2, 0:1], scb[:, i % 2, :], AX, ALU.max))
                            dve.tensor_scalar(nmx[:, i % 2, 0:1], mx[:, i % 2, 0:1], -1.0, None, ALU.mult).then_inc(s_mx, 1)
                        else:
                            nm = 2 if m == "A" else 1
                            scale = 32 ** -0.5 if m == "A" else 64 ** -0.5
                            for mp in range(nm):
                                p = ready(dve, ("sc", l, i, mp))
                                step(dve.tensor_reduce(mx[:, i % 2, mp:mp + 1], p[:, 0:nk], AX, ALU.max))
                            dve.tensor_scalar(nmx[:, i % 2, 0:nm], mx[:, i % 2, 0:nm], -scale, None, ALU.mult).then_inc(s_mx, 1)
                    if 1 <= i <= len(ATT):
                        m, t, h = ATT[i - 1]
                        j = i - 1
                        nk = T if t else P
                        if m == "C" and t:
                            dve.wait_ge(s_pr, l * 8 + seen[j])
                        else:
                            for mp in range(2 if m == "A" else 1):
                                moved(dve, ("sc", l, j, mp))
                        if m == "A":
                            step(dve.reciprocal(rsum[:, j % 4, :], sums[:, j % 2, :]))
                            step(dve.tensor_scalar(rneg[:, j % 2, :], sums[:, j % 2, 0:1], rsum[:, j % 4, 1:2], lam[:, l:l + 1], ALU.mult, ALU.mult))
                            if j >= 2:
                                ready(dve, ("pT", l, j - 2))
                            dve.scalar_tensor_tensor(out=wmix[:, j % 2, 0:nk], in0=prob[:, j % 2, 1, 0:nk], scalar=rneg[:, j % 2, :],
                                                     in1=prob[:, j % 2, 0, 0:nk], op0=ALU.mult, op1=ALU.add).then_inc(s_w, 1)
                        else:
                            dve.reciprocal(rsum[:, j % 4, 0:1], sums[:, j % 2, 0:1]).then_inc(s_w, 1)
                        dve.wait_ge(s_w, l * len(ATT) + j + 1)
                    fill_in(("AC", i))
                    for n, (at_, c0) in enumerate(((NORM_B, 12), (NORM_A, 0))):
                        if i == at_:
                            dve.wait_ge(s_sq, 2 * l + n + 1)
                            step(dve.tensor_reduce(ss[:, c0:c0 + 12], squares, AX, ALU.add))
                            dve.tensor_scalar(ms[:, c0:c0 + 12], ss[:, c0:c0 + 12], 1.0 / 64, EPS, ALU.mult, ALU.add).then_inc(s_pss, 1)
                        if i == at_ + 2:
                            dve.wait_ge(s_pss, 2 * l + n + 1)
                            dve.wait_ge(s_pln, 2 * l + n + 1)
                            newton(c0, c0 + 12)
                            dve.engine_nop().then_inc(s_rstd, 1)
                for c in range(0, 6, 2):
                    p = ready(dve, ("mT", l, c))
                    release(dve, dve.tensor_copy(hT[:, c, :], p[:, 0:T]), ("mT", l, c))
                gate_diagonals(l, 0)
                for s in range(2):
                    for b in range(2):
                        moved(dve, ("gbc", l, 0, s, b))
                for t in range(NT):
                    for b in range(2):
                        job = ("wo", l, b, t)
                        p = ready(dve, job)
                        release(dve, dve.tensor_tensor(mflat[:, 0:512], p, gate[:, min(t, 1), b * 512:(b + 1) * 512], ALU.mult), job)
                        xs = x[:, t, b * 512:(b + 1) * 512]
                        ins = dve.tensor_tensor(xs, xs, mflat[:, 0:512], ALU.add)
                        if b == 0:
                            step(ins)
                    ins.then_inc(s_x, 1)
                    dve.wait_ge(s_x, NT * 2 * l + t + 1)
                gate_diagonals(l, 1)
                scales(l, 1)
                dve.wait_ge(d_out, 16 * 4 * (l + 1))
                normalize(2 * l + 1)
                modulate(l, 1)
                for t in range(NT):
                    p = ready(dve, ("hb", l, t, 0))
                    release(dve, dve.tensor_copy(htok[:, t, 0:512], p), ("hb", l, t, 0))
                p = ready(dve, ("rt", l))
                release(dve, dve.tensor_copy(logit, p[:, 0:NT * NE].rearrange("p (t e) -> p t e", t=NT)), ("rt", l))
                dve.engine_nop().then_inc(s_rl, 1)
                dve.wait_ge(s_re, l + 1)
                step(dve.tensor_scalar(score, score, 1.0, None, ALU.add))
                step(dve.reciprocal(score, score))
                step(dve.tensor_tensor(selv, score, rbias[:, :].unsqueeze(1).broadcast_to([P, NT, NE]), ALU.add))
                sg = selv.rearrange("p t (g e) -> p (t g) e", e=4)
                rankb = rank.unsqueeze(1).broadcast_to([P, NT * 4, 4])

                def first_max(one_hot, values, best, n):
                    rb = rank.unsqueeze(1).broadcast_to([P, n, 4])
                    step(dve.tensor_reduce(best, values, AX, ALU.max))
                    step(dve.tensor_tensor(eqv[:, 0:n, :], values, best.unsqueeze(2).broadcast_to([P, n, 4]), ALU.is_equal))
                    step(dve.tensor_tensor(eqv[:, 0:n, :], eqv[:, 0:n, :], rb, ALU.mult))
                    step(dve.tensor_reduce(gsel[:, 0:n], eqv[:, 0:n, :], AX, ALU.max))
                    step(dve.tensor_tensor(one_hot, eqv[:, 0:n, :], gsel[:, 0:n].unsqueeze(2).broadcast_to([P, n, 4]), ALU.is_equal))

                first_max(oh1, sg, m1, NT * 4)
                step(dve.scalar_tensor_tensor(out=rest, in0=oh1, scalar=-1e30, in1=sg, op0=ALU.mult, op1=ALU.add))
                first_max(oh2, rest, m2, NT * 4)
                step(dve.tensor_tensor(gsc, m1, m2, ALU.add))
                g4 = slotc[:, 0:NT, :]
                first_max(g4, gsc.rearrange("p (t g) -> p t g", g=4), gm, NT)
                for oh in (oh1, oh2):
                    v = oh.rearrange("p (t g) e -> p t g e", g=4)
                    step(dve.tensor_tensor(v, v, g4.unsqueeze(3).broadcast_to([P, NT, 4, 4]), ALU.mult))
                picks = [oh.rearrange("p (t g) e -> p t (g e)", g=4) for oh in (oh1, oh2)]
                dve.tensor_tensor(selm, picks[0], picks[1], ALU.add).then_inc(s_sel, 1)
                dve.wait_ge(s_sel, l + 1)
                step(dve.tensor_tensor(gates, score, selm, ALU.mult))
                step(dve.tensor_reduce(den, gates, AX, ALU.add))
                step(dve.reciprocal(den, den))
                step(dve.tensor_tensor(gates, gates, den.unsqueeze(2).broadcast_to([P, NT, NE]), ALU.mult))
                p = ready(dve, ("pos", l))
                step(dve.tensor_tensor(posn, p[:, 0:NT * NE].rearrange("p (t e) -> p t e", t=NT),
                                       erow.unsqueeze(1).broadcast_to([P, NT, NE]), ALU.add))
                release(dve, dve.tensor_copy(cnt, p[:, NT * NE:(NT + 1) * NE]), ("pos", l))
                payf = pay[:, :, :, :].bitcast(F32)
                tmp3 = slotc.rearrange("p (t g) e -> p t (g e)", g=4)
                for k in range(2):
                    step(dve.tensor_tensor(tmp3, picks[k], posn, ALU.mult))
                    step(dve.tensor_reduce(slotf[:, :, k:k + 1], tmp3, AX, ALU.add))
                    step(dve.tensor_tensor(tmp3, picks[k], gates, ALU.mult))
                    step(dve.tensor_reduce(payf[:, :, k, 2:3], tmp3, AX, ALU.add))
                dve.tensor_copy(slotu[:, :, :], slotf).then_inc(s_pay, 1)
                if AHEAD[l]:
                    modulation(group(*AHEAD[l][-1]))
                step(dve.tensor_scalar(novv, cnt, float(CAP), None, ALU.is_gt))
                step(dve.tensor_scalar(ex2, cnt, float(2 * CAP), None, ALU.is_gt))
                step(dve.tensor_tensor(novv, novv, ex2, ALU.add))
                step(dve.tensor_tensor_scan(pin, ones[:, 0:NE], novv, 0.0, ALU.mult, ALU.add))
                step(dve.tensor_tensor(pexc, pin, novv, ALU.subtract))
                rb = ridx.unsqueeze(2).broadcast_to([P, MAXOV, NE])

                def over_experts(v):
                    return v.unsqueeze(1).broadcast_to([P, MAXOV, NE])

                step(dve.tensor_tensor(mat, over_experts(pexc), rb, ALU.is_le))
                step(dve.tensor_tensor(mat2, over_experts(pin), rb, ALU.is_gt))
                step(dve.tensor_tensor(mat, mat, mat2, ALU.mult))
                step(dve.tensor_tensor(mat2, mat, over_experts(eidx), ALU.mult))
                step(dve.tensor_reduce(oeid, mat2, AX, ALU.add))
                step(dve.tensor_tensor(mat2, rb, over_experts(pexc), ALU.subtract))
                step(dve.tensor_scalar(mat2, mat2, float(CAP), float(CAP), ALU.mult, ALU.add))
                step(dve.tensor_tensor(mat2, mat2, over_experts(erow), ALU.add))
                step(dve.tensor_tensor(mat2, mat2, mat, ALU.mult))
                step(dve.tensor_reduce(orow, mat2, AX, ALU.add))
                step(dve.tensor_copy(ovt[0:1, 0:1], pin[0:1, NE - 1:NE]))
                step(dve.tensor_copy(ovt[0:1, 1:1 + MAXOV], oeid[0:1, :]))
                dve.tensor_copy(ovt[0:1, 1 + MAXOV:1 + 2 * MAXOV], orow[0:1, :]).then_inc(s_ovt, 1)
                dve.wait_ge(s_ovt, l + 1)
                dve.wait_ge(s_pay, l + 1)
                dve.wait_ge(d_lst, 16 * (l + 1))

                def expert(i, es, first=False, last=False):
                    e = i * EXP_PER_BODY + es
                    if not last:
                        p = ready(dve, ("xt0", l), e)
                        release(dve, dve.tensor_copy(hTg[:, 0:4, :].rearrange("p a b -> p (a b)"), p), ("xt0", l), e)
                    if not first:
                        p = ready(dve, ("dn1", l), e - 1)
                        stored(dve, l, i, es - 1)
                        release(dve, dve.tensor_scalar(ybuf[:, (es - 1) % 2, 512:1024], p, gate_of(e - 1), None, ALU.mult), ("dn1", l), e - 1)
                    if not last:
                        p = ready(dve, ("u", l), e)
                        moved(dve, ("a", l), e)
                        release(dve, dve.tensor_tensor(zb, sS, p, ALU.mult), ("u", l), e)

                for e in range(EXP_PER_BODY):
                    expert(0, e, first=(e == 0))
                with dve.Fori(1, NBODY) as i:
                    for e in range(EXP_PER_BODY):
                        expert(i, e)
                expert(NBODY, 0, last=True)
                o_ = ov[l]
                n_ov = dve.value_load(ovt[0:1, 0:1], min_val=0, max_val=MAXOV)
                with dve.If(n_ov > 0):
                    with dve.Fori(0, n_ov) as r:
                        def sub(ins, n):
                            ins.then_inc(o_["vector"], 1)
                            dve.wait_ge(o_["vector"], 4 * r + n)

                        dve.wait_ge(o_["tensor"], 4 * r + 1)
                        sub(dve.tensor_copy(hTg, ps[:, 0:2, :].rearrange("p a (b c) -> p (a b) c", c=P)), 1)
                        dve.wait_ge(o_["tensor"], 4 * r + 2)
                        dve.wait_ge(o_["scalar"], r + 1)
                        sub(dve.tensor_tensor(zb, sS, ps[:, 3, :], ALU.mult), 2)
                        dve.wait_ge(o_["tensor"], 4 * r + 3)
                        sub(dve.tensor_copy(zTg.rearrange("p a b -> p (a b)"), ps[:, 4, :]), 3)
                        dve.wait_ge(o_["tensor"], 4 * r + 4)
                        sub(dve.tensor_scalar(ybuf[:, 0, :], ps[:, 5:7, :].rearrange("p a b -> p (a b)"), lsto[:, 2:3].bitcast(F32), None, ALU.mult), 4)
                for s in range(2):
                    for b in range(2):
                        moved(dve, ("gbc", l, 1, s, b))
                for t in range(NT):
                    dve.wait_ge(d_yr[t], 16 * (l + 1))
                    y = yr[:, t, 0, :]
                    step(dve.tensor_tensor(y, y, yr[:, t, 1, :], ALU.add))
                    step(dve.tensor_tensor(y, y, gate[:, min(t, 1), :], ALU.mult))
                    dve.tensor_tensor(x[:, t, :], x[:, t, :], y, ALU.add).then_inc(s_x, 1)
                    dve.wait_ge(s_x, NT * (2 * l + 1) + t + 1)
            normalize(2 * L)
            dve.wait_ge(d_fin, 16)
            dve.tensor_tensor(xn, xn, gate[:, 0, :].unsqueeze(1).broadcast_to([P, NT, D]), ALU.mult).then_inc(s_y, 1)

        @block.tensor
        def _(pe):
            def slot(l, kind, j):
                n = BLOCK_NO[(kind, l, j)]
                pe.wait_ge(landed[n % SLOTS], 16 * (n // SLOTS + 1))
                return ring[:, n % SLOTS, :].rearrange("p (k n) -> p k n", k=KC)

            def fill(ins, job, i=0):
                ins.then_inc(full[bank(job, i)[0]], 1)

            def matmuls(out, pairs):
                for n, (a, b) in enumerate(pairs):
                    ins = pe.matmul(out, a, b, start=(n == 0), stop=(n == len(pairs) - 1))
                return ins

            def mod_rows(l, j):
                w, q, b = slot(l, "ada", j), group(l, j), j % 4
                if b == 0 and q:
                    pe.wait_ge(free[MOD_BANK], q)
                for k in range(KC):
                    c = 32 * (k % 4)
                    ins = pe.matmul(ps[c:c + 32, MOD_BANK, :], scp[:, k, 6 - 2 * b:38 - 2 * b], w[:, k, :],
                                    start=(b == 0 and k < 4), stop=(b == 3 and k >= 4), tile_position=(0, c))
                ins.then_inc(s_rows, 1)

            def mod_turn(q, rows=rows):
                job = ("mod", q)
                p = begin(pe, job)
                pe.wait_ge(free[MOD_BANK], q + 1)
                for c in range(4):
                    ins = pe.matmul(p[:, 8 * c:8 * c + 8], rows[:, c * P:(c + 1) * P], fold, start=True, stop=True)
                fill(ins, job)

            def gate_spread(l, which):
                for n in range(4):
                    job = ("gbc", l, which, n // 2, n % 2)
                    p = begin(pe, job)
                    pe.wait_ge(s_diag, 8 * l + 4 * which + n + 1)
                    fill(pe.matmul(p, ones, diag[:, n % 2, :, :].rearrange("p a b -> p (a b)"), start=True, stop=True), job)

            def transposes(job, srcs):
                p = begin(pe, job)
                for n, s in enumerate(srcs):
                    ins = pe.transpose(p[:, n * P:(n + 1) * P], s, ident)
                fill(ins, job)

            def hidden(n):
                pe.wait_ge(s_xn, n + 1)
                for k in range(KC):
                    transposes(("hT", n, k), [xn[:, t, k * P:(k + 1) * P] for t in range(NT)])
                for k in range(KC):
                    moved(pe, ("hT", n, k))

            def by_token(l, w, job, t, c0, c1):
                p = begin(pe, job)
                fill(matmuls(p[:, 0:c1 - c0], [(hT[:, k, t * P:(t + 1) * P], w[:, k, c0:c1]) for k in range(KC)]), job)

            def by_feature(l, w, job, c):
                p = begin(pe, job)
                fill(matmuls(p[:, 0:T], [(w[:, k, c * P:(c + 1) * P], hT[:, k, :]) for k in range(KC)]), job)

            pe.wait_ge(s_sc, 1)
            for l in range(L):
                if l == 0:
                    for j in ADA_FIRST:
                        mod_rows(0, j)
                    pe.wait_ge(d_const, 16)
                    mod_turn(0)
                hidden(2 * l)

                def fill_in(at):
                    n = filler(l, at)
                    if n is not None and n < len(BETWEEN[l]):
                        mod_rows(*BETWEEN[l][n])
                    if n and n % 4 == 0:
                        mod_turn(group(*BETWEEN[l][n - 1]))

                def b_products(n):
                    u, h2 = n // 2, n % 2
                    t, hp = UNITS[u]
                    d_, at = dec[u % 2], NLEV * 2 * P
                    dirs = (0, 1) if t == 0 else (t - 1,)
                    if n == 0:
                        for tt in range(NT):
                            moved(pe, ("bvg", l, tt))
                    if h2 == 0:
                        pe.wait_ge(s_X, l * len(UNITS) + u + 1)
                        transposes(("kd", l, u), [d_[:, at + (2 + d) * P:at + (3 + d) * P] for d in dirs])
                    r = slice(64 * h2, 64 * h2 + 64)
                    for g in range(4):
                        job = ("gram", l, u, h2, g)
                        p = begin(pe, job)
                        for k in range(4 * g, min(4 * g + 4, GRAM)):
                            if k < 2 * NLEV:
                                a = b = d_[r, k * P:(k + 1) * P]
                            else:
                                a, b = d_[r, at:at + P], qT[r, hp, t * P:(t + 1) * P]
                            ins = pe.matmul(p[:, (k % 4) * P:(k % 4 + 1) * P], a, b, start=True, stop=True)
                        fill(ins, job)
                    if h2 == 0:
                        job = ("kv", l, u)
                        p = begin(pe, job)
                        moved(pe, ("kd", l, u))
                        for k in range(len(dirs)):
                            ins = pe.matmul(p[:, k * P:(k + 1) * P], kdT[:, u % 2, k, :], tok[:, t, BV + hp * P:BV + (hp + 1) * P],
                                            start=True, stop=True)
                        fill(ins, job)
                    fill_in(("B", n))

                w = slot(l, "win", 2)
                for d in range(2):
                    for hp in range(HP):
                        by_feature(l, w, ("z", l, d, hp), 2 * d + hp)
                w = slot(l, "win", 1)
                for hp in range(HP):
                    by_feature(l, w, ("bq", l, hp), 2 + hp)
                for t in range(NT):
                    by_token(l, w, ("av", l, t), t, 0, 256)
                w = slot(l, "win", 3)
                for t in range(NT):
                    by_token(l, w, ("bvg", l, t), t, 0, 512)
                w = slot(l, "win", 0)
                by_token(l, w, ("aqk", l, 0), 0, 0, 512)
                b_products(0)
                b_products(1)
                for t in (1, 2):
                    by_token(l, w, ("aqk", l, t), t, 0, 512)
                b_products(2)
                b_products(3)
                w = slot(l, "win", 4)
                for hp in range(HP):
                    by_feature(l, w, ("cq", l, hp), hp)
                b_products(4)
                b_products(5)
                for hp in range(HP):
                    by_feature(l, w, ("ck", l, hp), 2 + hp)
                b_products(6)
                b_products(7)
                w = slot(l, "win", 5)
                for t in (0, 1):
                    by_token(l, w, ("cvdu", l, t), t, 0, 512)
                b_products(8)
                b_products(9)
                by_token(l, w, ("cvdu", l, 2), 2, 0, 512)
                for t in range(NT):
                    moved(pe, ("cvdu", l, t))
                for c in range(2):
                    ch = slice(DU + c * P, DU + (c + 1) * P)
                    p = begin(pe, ("du", l, c, 0))
                    fill(pe.matmul(p[:, 0:256], tok[:, 0, ch], dftc, start=True, stop=True), ("du", l, c, 0))
                    p = begin(pe, ("du", l, c, 1))
                    fill(matmuls(p, [(tok[:, 1 + t, ch], dftl[:, t, :]) for t in range(2)]), ("du", l, c, 1))
                for c in range(2):
                    job = ("dy", l, c)
                    p = begin(pe, job)
                    moved(pe, ("du", l, c, 0))
                    moved(pe, ("du", l, c, 1))
                    matmuls(p[:, 0:P], [(chc, Ud[:, c, 0:P]), (chs, Ud[:, c, P:2 * P])])
                    fill(matmuls(p[:, P:T], [(chc, Ud[:, c, 256:512]), (chs, Ud[:, c, 512:768])]), job)
                pe.wait_ge(d_cache, 64 * (l + 1))
                transposes(("cc", l), [cachek[:, 2, 2 * hp:2 * hp + 2, :].rearrange("p a b -> p (a b)") for hp in range(HP)])
                for hp in range(HP):
                    moved(pe, ("ck", l, hp))
                transposes(("nk", l), [ckT[:, hp, 0:P] for hp in range(HP)])
                b_products(10)
                b_products(11)
                for u in range(len(UNITS)):
                    moved(pe, ("kv", l, u))
                pe.wait_ge(s_att, 2 * len(UNITS) * (l + 1))
                for t in range(NT):
                    for h2 in range(2):
                        job = ("bo", l, t, h2)
                        p = begin(pe, job)
                        r = slice(64 * h2, 64 * h2 + 64)
                        for hp in range(HP):
                            h = 2 * hp + h2
                            pairs = [(attT[:, 2 * (t * HP + hp) + h2, :], tok[:, t, BV + 64 * h:BV + 64 * h + 64])]
                            if t:
                                pairs += [(qdec[r, t - 1, hp, d, :], (S0 if (t == 1) == (d == 0) else S1)[r, hp, d, :]) for d in range(2)]
                            ins = matmuls(p[:, 64 * hp:64 * hp + 64], pairs)
                        fill(ins, job)
                pe.wait_ge(s_rope, l + 1)
                for hp in range(HP):
                    transposes(("aT", l, 0, hp), [tok[:, t, AQ + hp * P:AQ + (hp + 1) * P] for t in range(NT)])
                for hp in range(HP):
                    kc = cachek[:, 0, 2 * hp:2 * hp + 2, :].rearrange("p a b -> p (a b)")
                    kt = [tok[:, t, AK + hp * P:AK + (hp + 1) * P] for t in range(NT)]
                    transposes(("aT", l, 1, hp), [kt[0], kc, kt[1], kt[2]])
                for w in range(2):
                    for hp in range(HP):
                        moved(pe, ("aT", l, w, hp))
                moved(pe, ("cc", l))
                for hp in range(HP):
                    moved(pe, ("cq", l, hp))
                for i in range(len(ATT) + 3):
                    if i < len(ATT):
                        m, t, h = ATT[i]
                        hp, h2 = h // 2, h % 2
                        keys = slice(P, 4 * P) if t else slice(0, P)
                        nk = T if t else P
                        for mp in range(2 if m == "A" else 1):
                            job = ("sc", l, i, mp)
                            p = begin(pe, job)
                            if m == "A":
                                r = slice(64 * h2 + 32 * mp, 64 * h2 + 32 * mp + 32)
                                q, k = aqT, akT
                            else:
                                r = slice(64 * h2, 64 * h2 + 64)
                                q, k = cqT, ckT
                            kw = {"tile_position": (r.start, 0)} if m == "A" else {}
                            fill(pe.matmul(p[:, 0:nk], q[r, hp, t * P:(t + 1) * P], k[r, hp, keys], start=True, stop=True, **kw), job)
                    if 0 <= i - 2 < len(ATT):
                        m, t, h = ATT[i - 2]
                        pe.wait_ge(s_w, l * len(ATT) + i - 1)
                        src = wmix[:, i % 2, :] if m == "A" else prob[:, i % 2, 0, :]
                        transposes(("pT", l, i - 2), [src[:, n * P:(n + 1) * P] for n in range(3 if t else 1)])
                    if i >= 3:
                        m, t, h = ATT[i - 3]
                        c0 = AV if m == "A" else CV
                        job = ("ao", l, i - 3)
                        p = begin(pe, job)
                        moved(pe, ("pT", l, i - 3))
                        w_ = wT[:, (i - 3) % 2, :]
                        vt = [tok[:, tt, c0 + 64 * h:c0 + 64 * h + 64] for tt in range(NT)]
                        v = [cachek[:, 1 if m == "A" else 3, h, :], vt[1], vt[2]] if t else [vt[0]]
                        fill(matmuls(p[:, 0:64], [(w_[:, n * P:(n + 1) * P], v[n]) for n in range(len(v))]), job)
                    fill_in(("AC", i))
                pe.wait_ge(s_post, 2 * l + 2)
                for i in range(len(ATT)):
                    if i >= len(ATT) - BANKS:
                        moved(pe, ("ao", l, i))
                for c in range(6):
                    src = (oA, oB, oC)[c // 2].rearrange("p (t h) c -> p t (h c)", t=NT)
                    transposes(("mT", l, c), [src[:, t, (c % 2) * P:(c % 2 + 1) * P] for t in range(NT)])
                for c in range(6):
                    moved(pe, ("mT", l, c))
                for c in range(2):
                    moved(pe, ("dy", l, c))
                gate_spread(l, 0)
                for t in range(NT):
                    for b in range(2):
                        by_token(l, slot(l, "wout", b), ("wo", l, b, t), t, 0, 512)

                for blk in AHEAD[l][0:1]:
                    mod_rows(*blk)
                gate_spread(l, 1)
                for blk in AHEAD[l][1:2]:
                    mod_rows(*blk)
                hidden(2 * l + 1)
                for blk in AHEAD[l][2:3]:
                    mod_rows(*blk)
                for t in range(NT):
                    for b in range(2):
                        transposes(("hb", l, t, b), [hT[:, k, t * P:(t + 1) * P] for k in range(4 * b, 4 * b + 4)])
                job = ("rt", l)
                p = begin(pe, job)
                pe.wait_ge(d_row, 16 * 5)
                for t in range(NT):
                    ins = matmuls(p[:, t * NE:(t + 1) * NE], [(hT[:, k, t * P:(t + 1) * P], wrt[:, k, :]) for k in range(KC)])
                fill(ins, job)
                for blk in AHEAD[l][3:]:
                    mod_rows(*blk)
                job = ("pos", l)
                p = begin(pe, job)
                pe.wait_ge(s_sel, l + 1)
                for t in range(NT):
                    matmuls(p[:, t * NE:(t + 1) * NE], [(ones, selm[:, b, :]) for b in range(t)] + [(tri, selm[:, t, :])])
                fill(matmuls(p[:, NT * NE:(NT + 1) * NE], [(ones, selm[:, b, :]) for b in range(NT)]), job)
                if AHEAD[l]:
                    mod_turn(group(*AHEAD[l][-1]), rows2)
                n0 = FIRST_BLOCK[l] + len(PRE[l])

                def expert(i, es, first=False, last=False):
                    e = i * EXP_PER_BODY + es

                    def block_of(c, q):
                        n = n0 + 3 * c + q
                        pe.wait_ge(landed[n % SLOTS], i * (16 * 3 * EXP_PER_BODY // SLOTS) + 16 * (n // SLOTS + 1))
                        return ring[:, n % SLOTS, :].rearrange("p (k n) -> p k n", k=(KC, KC, FC)[q])

                    def turn(kind, e_, srcs):
                        p = begin(pe, (kind, l), e_)
                        for n, s in enumerate(srcs):
                            ins = pe.transpose(p[:, n * P:(n + 1) * P], s, ident)
                        fill(ins, (kind, l), e_)

                    if not last:
                        half = i * (16 * EXP_PER_BODY // 2) + 16 * (NE // 2 * l + es // 2 + 1)
                        pe.wait_ge(d_g[es % 2], half)
                        for b in range(2):
                            turn(f"xt{b}", e, [xg[:, es % 2, k * P:(k + 1) * P] for k in range(4 * b, 4 * b + 4)])
                    if not first:
                        moved(pe, ("u", l), e - 1)
                        turn("zt", e - 1, [zb[:, f * P:(f + 1) * P] for f in range(FC)])
                    if not last:
                        w = block_of(es, 0)
                        p = begin(pe, ("a", l), e)
                        for b in range(2):
                            moved(pe, (f"xt{b}", l), e)
                        fill(matmuls(p, [(hTg[:, k, :], w[:, k, :]) for k in range(KC)]), ("a", l), e)
                    if not first:
                        w = block_of(es - 1, 2)
                        moved(pe, ("zt", l), e - 1)
                        for b in range(2):
                            p = begin(pe, (f"dn{b}", l), e - 1)
                            fill(matmuls(p, [(zTg[:, f, :], w[:, f, b * 512:(b + 1) * 512]) for f in range(FC)]), (f"dn{b}", l), e - 1)
                    if not last:
                        w = block_of(es, 1)
                        p = begin(pe, ("u", l), e)
                        fill(matmuls(p, [(hTg[:, k, :], w[:, k, :]) for k in range(KC)]), ("u", l), e)

                for e in range(EXP_PER_BODY):
                    expert(0, e, first=(e == 0))
                with pe.Fori(1, NBODY) as i:
                    for e in range(EXP_PER_BODY):
                        expert(i, e)
                expert(NBODY, 0, last=True)
                o_ = ov[l]
                pe.wait_ge(s_ovt, l + 1)
                n_ov = pe.value_load(ovt[0:1, 0:1], min_val=0, max_val=MAXOV)
                with pe.If(n_ov > 0):
                    for b, kind in enumerate(EJOBS):
                        moved(pe, (kind, l), NE - 1)
                    with pe.Fori(0, n_ov) as r:
                        pe.wait_ge(o_["gathered"], 16 * r + 16)
                        for k in range(KC):
                            ins = pe.transpose(ps[:, k // 4, (k % 4) * P:(k % 4 + 1) * P], xg[:, 0, k * P:(k + 1) * P], ident)
                        ins.then_inc(o_["tensor"], 1)
                        pe.wait_ge(o_["vector"], 4 * r + 1)
                        pe.wait_ge(o_["weights_landed"], 48 * r + 48)
                        wg, wu = (ring[:, q, :].rearrange("p (k n) -> p k n", k=KC) for q in range(2))
                        wd = ring[:, 2, :].rearrange("p (k n) -> p k n", k=FC)
                        matmuls(ps[:, 2, :], [(hTg[:, k, :], wg[:, k, :]) for k in range(KC)])
                        matmuls(ps[:, 3, :], [(hTg[:, k, :], wu[:, k, :]) for k in range(KC)]).then_inc(o_["tensor"], 1)
                        pe.wait_ge(o_["vector"], 4 * r + 2)
                        for f in range(FC):
                            ins = pe.transpose(ps[:, 4, f * P:(f + 1) * P], zb[:, f * P:(f + 1) * P], ident)
                        ins.then_inc(o_["tensor"], 1)
                        pe.wait_ge(o_["vector"], 4 * r + 3)
                        for b in range(2):
                            ins = matmuls(ps[:, 5 + b, :], [(zTg[:, f, :], wd[:, f, b * 512:(b + 1) * 512]) for f in range(FC)])
                        ins.then_inc(o_["tensor"], 1)
                        pe.wait_ge(o_["vector"], 4 * r + 4)


def constants():
    def dft(n):
        ang = 2 * np.pi * (np.outer(np.arange(n), np.arange(n)) % n) / n
        return np.cos(ang), np.sin(ang)

    parts = [np.eye(P)]
    c, s = dft(P)
    parts.append(np.concatenate([c, s], 1) / math.sqrt(P))
    c, s = dft(2 * P)
    parts.append((np.concatenate([c, s], 1) / math.sqrt(2 * P)).reshape(2, P, 512).transpose(1, 0, 2))
    c, s = dft(64)
    parts += [np.kron(np.eye(2), c) / 8.0, -np.kron(np.eye(2), s) / 8.0]
    freq = (np.float32(10000.0) ** (-np.arange(8, dtype=np.float32) / np.float32(8))).astype(np.float32)
    pos = np.arange(2 * P)
    ang = np.concatenate([(pos // GRID_W).astype(np.float32)[:, None] * freq, (pos % GRID_W).astype(np.float32)[:, None] * freq], -1)
    cos, sin = np.cos(ang.astype(np.float64)), np.sin(ang.astype(np.float64))
    parts.append(np.repeat(cos, 2, -1).reshape(2, P, 32).transpose(1, 0, 2))
    parts.append(sin.reshape(2, P, 16).transpose(1, 0, 2))
    qc = np.arange(P) % GRID_W
    start = np.clip(qc - 8, 0, GRID_W - 16)
    kc = np.arange(GRID_W)
    parts.append(np.where((kc[None] >= start[:, None]) & (kc[None] < start[:, None] + 16), 0.0, -1e30))
    parts.append(np.ones((P, P)))
    parts.append((np.arange(P)[:, None] % 32 == np.arange(8)[None]).astype(np.float64))
    parts.append(np.tile(np.array([4.0, 3.0, 2.0, 1.0]), (P, 1)))
    parts.append(np.triu(np.ones((P, P)), 1))
    parts += [np.tile(v.astype(np.float64), (P, 1)) for v in (np.arange(NE), np.arange(NE) * T, np.arange(MAXOV))]
    return np.concatenate([p.reshape(P, -1) for p in parts], 1).astype(np.float32)


def slot_words():
    empty = np.tile(np.array([0, NOWHERE, 0, 0], np.uint32), (P, NE * T // P))
    tok, k = np.arange(T), np.arange(2)
    rec = np.zeros((T, 2, 4), np.uint32)
    rec[:, :, 0], rec[:, :, 1] = tok[:, None], 2 * tok[:, None] + k
    return np.concatenate([empty, rec.reshape(NT, P, 8).transpose(1, 0, 2).reshape(P, -1)], 1)


def level_masks():
    s, t = np.arange(P)[:, None], np.arange(P)[None]
    out = []
    for m in LEVELS:
        same = s // (2 * m) == t // (2 * m)
        out.append(same & (s // m % 2 == 0) & (t // m % 2 == 1))
        out.append(same & (s // m % 2 == 1) & (t // m % 2 == 0))
    out.append(s == t)
    return np.stack(out, 1).reshape(P, -1)


def kernel(**inputs):
    import ml_dtypes
    import concourse.bacc as bacc
    from concourse.bass_utils import run_bass_kernel_spmd

    a = {k: np.ascontiguousarray(v) for k, v in inputs.items()}

    def cols(v):
        v = v.reshape(v.shape[0], -1, P)
        return v.transpose(2, 0, 1).reshape(P, -1)

    cc = np.stack([a["c_ctx"].reshape(KC, P), a["c"][0].reshape(KC, P)], -1)
    params = np.concatenate([cols(a["norm1_g"]), cols(a["norm2_g"]), cols(a["ada_b"]),
                             cols(a["hgrn_lb_logits"].reshape(L, -1)), cc.transpose(1, 0, 2).reshape(P, -1)], 1)
    pad = np.zeros((L * H * RPB_H, RPER), np.float32)
    pad[:, GRID_W - RPB_W // 2 - 1:GRID_W - RPB_W // 2 - 1 + RPB_W] = a["na_rpb"].reshape(-1, RPB_W)
    direct = ["x_prompt", "x_sample", "cache_diff_k", "cache_diff_v", "cache_na_k", "cache_na_v", "state_hgrn", "ada_w",
              "ada_b", "w_in", "w_out", "diff_lambda", "diff_subln_g", "hgrn_norm_g", "router_w", "router_b",
              "moe_w_gate", "moe_w_up", "moe_w_down", "final_norm_g"]
    arrays = {n: a[n] for n in direct}
    arrays["params"] = np.ascontiguousarray(params)
    arrays["rpb_pad"] = pad
    arrays["consts"] = constants()
    arrays["slots0"] = slot_words()
    arrays["masks"] = level_masks().astype(ml_dtypes.bfloat16)

    nc = bacc.Bacc("TRN2", target_bir_lowering=False, num_devices=1)
    args = {n: nc.dram_tensor(n, v.shape, mybir.dt.from_np(v.dtype), kind="ExternalInput").ap() for n, v in arrays.items()}
    shapes = {"y_prompt": (1, P, D), "y_sample": (1, 2 * P, D), "new_diff_k": (1, L, H, P, 64), "new_diff_v": (1, L, H, P, 64),
              "new_na_k": (1, L, H, P, 64), "new_na_v": (1, L, H, P, 64), "new_state": (1, L, 2, H, 64, 64)}
    outs = [nc.dram_tensor(n, s, F32, kind="ExternalOutput").ap() for n, s in shapes.items()]
    hybrid_step(nc, outs=outs, **args)
    r = run_bass_kernel_spmd(nc, [arrays], core_ids=[0])
    return tuple(r.results[0][n] for n in shapes)
```
